# Optimizing a Trainium2 kernel written in Bass

```python
import math
import jax, jax.numpy as jnp
from jax import lax
import numpy as np

D_MODEL = 1024
BATCH = 1
SEQ = 512
DEPTH = 2

GRID_W = 64
CTX_LEN = 256
Q_BLOCK = 128
ROPE_BASE = 10000.0
LN_EPS = 1e-6
RMS_EPS = 1e-6
SUBLN_EPS = 1e-5
DA_HEADS = D_MODEL // 256
DA_DIM = 64
DA_VDIM = 2 * DA_DIM
MLA_HEADS = D_MODEL // 256
MLA_Q_RANK = D_MODEL // 4
MLA_KV_RANK = D_MODEL // 8
MLA_NOPE = 64
MLA_ROPE = 32
MLA_VDIM = 64
NA_HEADS = D_MODEL // 256
NA_DIM = 64
NA_KH = 8
NA_KW = 16
D_FF = 4 * D_MODEL
MIX_WIDTH = DA_HEADS * DA_VDIM + MLA_HEADS * MLA_VDIM + NA_HEADS * NA_DIM
IN_SIZES = (DA_HEADS * 2 * DA_DIM, DA_HEADS * 2 * DA_DIM, DA_HEADS * DA_VDIM,
            MLA_Q_RANK, MLA_KV_RANK, MLA_ROPE,
            NA_HEADS * NA_DIM, NA_HEADS * NA_DIM, NA_HEADS * NA_DIM)
IN_WIDTH = sum(IN_SIZES)
DN_ALPHA = (2.0 * DEPTH) ** 0.25
DN_BETA = (8.0 * DEPTH) ** -0.25

kernel_name = 'hybrid_parallel_head_dit_block'

def layer_norm(x, g, b):
    xf = x.astype(jnp.float32)
    mu = jnp.mean(xf, axis=-1, keepdims=True)
    var = jnp.mean(jnp.square(xf - mu), axis=-1, keepdims=True)
    y = (xf - mu) * lax.rsqrt(var + LN_EPS) * g.astype(jnp.float32) + b.astype(jnp.float32)
    return y.astype(x.dtype)

def rms_norm(x, g, eps):
    xf = x.astype(jnp.float32)
    y = xf * lax.rsqrt(jnp.mean(jnp.square(xf), axis=-1, keepdims=True) + eps)
    return (y * g.astype(jnp.float32)).astype(x.dtype)

def softmax_f32(s):
    return jax.nn.softmax(s.astype(jnp.float32), axis=-1)

def modulate(x, shift, scale):
    return x * (1 + scale) + shift

def rope_1d(x, pos):
    n = x.shape[-1]
    half = n // 2
    inv_freq = ROPE_BASE ** (-2.0 * jnp.arange(half, dtype=jnp.float32) / n)
    ang = pos.astype(jnp.float32)[:, None] * inv_freq[None, :]
    shape = (ang.shape[0],) + (1,) * (x.ndim - 3) + (half,)
    cos = jnp.cos(ang).reshape(shape).astype(x.dtype)
    sin = jnp.sin(ang).reshape(shape).astype(x.dtype)
    x1, x2 = x[..., :half], x[..., half:]
    return jnp.concatenate([x1 * cos - x2 * sin, x2 * cos + x1 * sin], axis=-1)

def axial_rope(x, row, col):
    n = x.shape[-1] // 2
    return jnp.concatenate([rope_1d(x[..., :n], row), rope_1d(x[..., n:], col)], axis=-1)

def split_cols(p):
    offs = [int(o) for o in np.cumsum(IN_SIZES)[:-1]]
    return jnp.split(p, offs, axis=-1)

def sweep_query_blocks(fn, *qs):
    b, length = qs[0].shape[:2]
    nb = length // Q_BLOCK
    blocks = tuple(jnp.moveaxis(q.reshape((b, nb, Q_BLOCK) + q.shape[2:]), 1, 0) for q in qs)
    out = lax.map(lambda qb: fn(*qb), blocks)
    return jnp.moveaxis(out, 0, 1).reshape((b, length) + out.shape[3:])

def da_heads(q, k, v):
    b, n = q.shape[:2]
    q = q.reshape(b, n, DA_HEADS, 2, DA_DIM)
    k = k.reshape(b, n, DA_HEADS, 2, DA_DIM)
    return (q[..., 0, :], q[..., 1, :], k[..., 0, :], k[..., 1, :],
            v.reshape(b, n, DA_HEADS, DA_VDIM))

def diff_attention(q1, q2, k1, k2, v, lam, subln_g, lam_init):
    scale = DA_DIM ** -0.5
    a1 = softmax_f32(jnp.einsum('bqhd,bkhd->bhqk', q1, k1) * scale)
    a2 = softmax_f32(jnp.einsum('bqhd,bkhd->bhqk', q2, k2) * scale)
    p = (a1 - lam * a2).astype(v.dtype)
    o = jnp.einsum('bhqk,bkhe->bqhe', p, v)
    return rms_norm(o, subln_g, SUBLN_EPS) * (1.0 - lam_init)

def mla_heads(cq, ckv, kr, q_norm_g, w_uq, kv_norm_g, w_ukv):
    b, n = cq.shape[:2]
    q = (rms_norm(cq, q_norm_g, RMS_EPS) @ w_uq).reshape(b, n, MLA_HEADS, MLA_NOPE + MLA_ROPE)
    kv = (rms_norm(ckv, kv_norm_g, RMS_EPS) @ w_ukv).reshape(b, n, MLA_HEADS, MLA_NOPE + MLA_VDIM)
    return q[..., :MLA_NOPE], q[..., MLA_NOPE:], kv[..., :MLA_NOPE], kr, kv[..., MLA_NOPE:]

def mla_attention(q_nope, q_pe, k_nope, k_pe, v):
    scale = (MLA_NOPE + MLA_ROPE) ** -0.5
    s = (jnp.einsum('bqhd,bkhd->bhqk', q_nope, k_nope)
         + jnp.einsum('bqhr,bkr->bhqk', q_pe, k_pe))
    p = softmax_f32(s * scale).astype(v.dtype)
    return jnp.einsum('bhqk,bkhd->bqhd', p, v)

def dense_attention(q, k, v):
    s = jnp.einsum('bqhd,bkhd->bhqk', q, k) * (q.shape[-1] ** -0.5)
    p = softmax_f32(s).astype(v.dtype)
    return jnp.einsum('bhqk,bkhd->bqhd', p, v)

def neighbourhood_attention(q, k, v, kc, vc, rpb):
    b, length, nh, d = q.shape
    rows = length // GRID_W
    kh = min(NA_KH, rows)
    qg = q.reshape(b, rows, GRID_W, nh, d)
    kg = k.reshape(b, rows, GRID_W, nh, d)
    vg = v.reshape(b, rows, GRID_W, nh, d)
    cols = np.arange(GRID_W)
    col_start = np.clip(cols - NA_KW // 2, 0, GRID_W - NA_KW)
    col_idx = col_start[:, None] + np.arange(NA_KW)[None, :]
    dx = col_idx - cols[:, None] + (NA_KW - 1)
    bias_cols = rpb[:, :, dx]
    scale = d ** -0.5
    n_win = kh * NA_KW

    def row_block(r):
        rs = jnp.clip(r - kh // 2, 0, rows - kh)
        k_win = lax.dynamic_slice_in_dim(kg, rs, kh, axis=1)[:, :, col_idx]
        v_win = lax.dynamic_slice_in_dim(vg, rs, kh, axis=1)[:, :, col_idx]
        q_r = lax.dynamic_index_in_dim(qg, r, axis=1, keepdims=False)
        dy = rs + jnp.arange(kh) - r + (NA_KH - 1)
        bias = jnp.transpose(jnp.take(bias_cols, dy, axis=1), (0, 2, 1, 3))
        s_win = (jnp.einsum('bqhd,biqjhd->bhqij', q_r, k_win) * scale).astype(jnp.float32) + bias[None].astype(jnp.float32)
        s_ctx = jnp.einsum('bqhd,bchd->bhqc', q_r, kc) * scale
        s = jnp.concatenate([s_win.reshape(b, nh, GRID_W, n_win), s_ctx.astype(jnp.float32)], axis=-1)
        p = softmax_f32(s).astype(v.dtype)
        p_win = p[..., :n_win].reshape(b, nh, GRID_W, kh, NA_KW)
        return (jnp.einsum('bhqij,biqjhd->bqhd', p_win, v_win)
                + jnp.einsum('bhqc,bchd->bqhd', p[..., n_win:], vc))

    out = lax.map(row_block, jnp.arange(rows))
    return jnp.moveaxis(out, 0, 1).reshape(b, length, nh * d)

def token_mixers(h, hc, row, col, lam_init, need_ctx, w_in, lam_q1, lam_k1, lam_q2, lam_k2,
                 subln_g, q_norm_g, w_uq, kv_norm_g, w_ukv, rpb):
    b, length, _ = h.shape
    lc = hc.shape[1]
    aq, ak, av, cq, ckv, kr, nq, nk, nv = split_cols(h @ w_in)
    aqc, akc, avc, cqc, ckvc, krc, nqc, nkc, nvc = split_cols(hc @ w_in)

    f32 = jnp.float32
    lam = (jnp.exp(jnp.sum(lam_q1.astype(f32) * lam_k1.astype(f32)))
           - jnp.exp(jnp.sum(lam_q2.astype(f32) * lam_k2.astype(f32))) + lam_init)
    q1, q2, k1, k2, va = da_heads(aq, ak, av)
    q1, q2, k1, k2 = (axial_rope(t, row, col) for t in (q1, q2, k1, k2))
    q1c, q2c, k1c, k2c, vac = da_heads(aqc, akc, avc)
    k1_all = jnp.concatenate([k1c, k1], axis=1)
    k2_all = jnp.concatenate([k2c, k2], axis=1)
    va_all = jnp.concatenate([vac, va], axis=1)
    y_a = sweep_query_blocks(
        lambda qa, qb: diff_attention(qa, qb, k1_all, k2_all, va_all, lam, subln_g, lam_init),
        q1, q2).reshape(b, length, -1)

    qn, qp, kn, kp, vm = mla_heads(cq, ckv, kr, q_norm_g, w_uq, kv_norm_g, w_ukv)
    qp = axial_rope(qp, row, col)
    kp = axial_rope(kp, row, col)
    qnc, qpc, knc, kpc, vmc = mla_heads(cqc, ckvc, krc, q_norm_g, w_uq, kv_norm_g, w_ukv)
    kn_all = jnp.concatenate([knc, kn], axis=1)
    kp_all = jnp.concatenate([kpc, kp], axis=1)
    vm_all = jnp.concatenate([vmc, vm], axis=1)
    y_b = sweep_query_blocks(
        lambda a, p_: mla_attention(a, p_, kn_all, kp_all, vm_all), qn, qp).reshape(b, length, -1)

    nq, nk, nv = (t.reshape(b, length, NA_HEADS, NA_DIM) for t in (nq, nk, nv))
    nqc, nkc, nvc = (t.reshape(b, lc, NA_HEADS, NA_DIM) for t in (nqc, nkc, nvc))
    y_c = neighbourhood_attention(nq, nk, nv, nkc, nvc, rpb)

    y = jnp.concatenate([y_a, y_b, y_c], axis=-1)
    if not need_ctx:
        return y, None
    y_ctx = jnp.concatenate([
        diff_attention(q1c, q2c, k1c, k2c, vac, lam, subln_g, lam_init).reshape(b, lc, -1),
        mla_attention(qnc, qpc, knc, kpc, vmc).reshape(b, lc, -1),
        dense_attention(nqc, nkc, nvc).reshape(b, lc, -1)], axis=-1)
    return y, y_ctx

def sq_relu_mlp(h, w1, w2):
    return jnp.square(jax.nn.relu(h @ w1)) @ w2

def setup_inputs(seed: int = 0) -> dict:
    key = jax.random.key(seed)
    ks = jax.random.split(key, 24)

    def nrm(k, shape, s):
        return jax.random.normal(k, shape, jnp.float32) * s

    nl = DEPTH
    return {
        'x': nrm(ks[0], (BATCH, SEQ, D_MODEL), 1.0),
        'c': nrm(ks[1], (BATCH, D_MODEL), 1.0),
        'ctx': nrm(ks[2], (BATCH, CTX_LEN, D_MODEL), 1.0),
        'c_ctx': nrm(ks[3], (D_MODEL,), 1.0),
        'w_mod': nrm(ks[4], (nl, D_MODEL, 6 * D_MODEL), 0.5 * D_MODEL ** -0.5),
        'b_mod': nrm(ks[5], (nl, 6 * D_MODEL), 0.01),
        'w_in': nrm(ks[6], (nl, D_MODEL, IN_WIDTH), D_MODEL ** -0.5),
        'da_lam_q1': nrm(ks[7], (nl, DA_DIM), 0.1),
        'da_lam_k1': nrm(ks[8], (nl, DA_DIM), 0.1),
        'da_lam_q2': nrm(ks[9], (nl, DA_DIM), 0.1),
        'da_lam_k2': nrm(ks[10], (nl, DA_DIM), 0.1),
        'da_subln_g': 1.0 + nrm(ks[11], (nl, DA_VDIM), 0.01),
        'mla_q_norm_g': 1.0 + nrm(ks[12], (nl, MLA_Q_RANK), 0.01),
        'mla_w_uq': nrm(ks[13], (nl, MLA_Q_RANK, MLA_HEADS * (MLA_NOPE + MLA_ROPE)), MLA_Q_RANK ** -0.5),
        'mla_kv_norm_g': 1.0 + nrm(ks[14], (nl, MLA_KV_RANK), 0.01),
        'mla_w_ukv': nrm(ks[15], (nl, MLA_KV_RANK, MLA_HEADS * (MLA_NOPE + MLA_VDIM)), MLA_KV_RANK ** -0.5),
        'na_rpb': nrm(ks[16], (nl, NA_HEADS, 2 * NA_KH - 1, 2 * NA_KW - 1), 0.05),
        'w_out': nrm(ks[17], (nl, MIX_WIDTH, D_MODEL), DN_BETA * MIX_WIDTH ** -0.5),
        'ln1_g': 1.0 + nrm(ks[18], (nl, D_MODEL), 0.01),
        'ln1_b': nrm(ks[19], (nl, D_MODEL), 0.01),
        'w_ff1': nrm(ks[20], (nl, D_MODEL, D_FF), D_MODEL ** -0.5),
        'w_ff2': nrm(ks[21], (nl, D_FF, D_MODEL), DN_BETA * D_FF ** -0.5),
        'ln2_g': 1.0 + nrm(ks[22], (nl, D_MODEL), 0.01),
        'ln2_b': nrm(ks[23], (nl, D_MODEL), 0.01),
    }

def reference(x, c, ctx, c_ctx, w_mod, b_mod, w_in, da_lam_q1, da_lam_k1, da_lam_q2, da_lam_k2,
              da_subln_g, mla_q_norm_g, mla_w_uq, mla_kv_norm_g, mla_w_ukv, na_rpb, w_out,
              ln1_g, ln1_b, w_ff1, w_ff2, ln2_g, ln2_b):
    length = x.shape[1]
    t = jnp.arange(length, dtype=jnp.int32)
    row = t // GRID_W
    col = t % GRID_W
    s_c = jax.nn.silu(c)
    s_cc = jax.nn.silu(c_ctx)
    xc = ctx
    for l in range(DEPTH):
        last = l == DEPTH - 1
        lam_init = 0.8 - 0.6 * math.exp(-0.3 * l)
        mod = jnp.split(s_c @ w_mod[l] + b_mod[l], 6, axis=-1)
        shift1, scale1, gate1, shift2, scale2, gate2 = (m[:, None, :] for m in mod)
        mod_c = jnp.split(s_cc @ w_mod[l] + b_mod[l], 6, axis=-1)
        y, yc = token_mixers(modulate(x, shift1, scale1), modulate(xc, mod_c[0], mod_c[1]),
                             row, col, lam_init, not last, w_in[l],
                             da_lam_q1[l], da_lam_k1[l], da_lam_q2[l], da_lam_k2[l], da_subln_g[l],
                             mla_q_norm_g[l], mla_w_uq[l], mla_kv_norm_g[l], mla_w_ukv[l], na_rpb[l])
        x = layer_norm(DN_ALPHA * x + gate1 * (y @ w_out[l]), ln1_g[l], ln1_b[l])
        x = layer_norm(DN_ALPHA * x + gate2 * sq_relu_mlp(modulate(x, shift2, scale2), w_ff1[l], w_ff2[l]),
                       ln2_g[l], ln2_b[l])
        if not last:
            xc = layer_norm(DN_ALPHA * xc + mod_c[2] * (yc @ w_out[l]), ln1_g[l], ln1_b[l])
            xc = layer_norm(DN_ALPHA * xc + mod_c[5] * sq_relu_mlp(modulate(xc, mod_c[3], mod_c[4]), w_ff1[l], w_ff2[l]),
                            ln2_g[l], ln2_b[l])
    return x


_drawn_inputs = setup_inputs


def setup_inputs(seed=0):
    import zlib

    import numpy as np

    out = dict(_drawn_inputs(seed))
    spreads = {}
    factors = {'ctx': 3.088,
     'b_mod': 6.405,
     'da_lam_q1': 8.0,
     'da_lam_k1': 8.0,
     'da_lam_q2': 8.0,
     'da_lam_k2': 8.0,
     'da_subln_g': 8.0,
     'mla_q_norm_g': 8.0,
     'mla_w_uq': 7.913,
     'mla_kv_norm_g': 8.0,
     'mla_w_ukv': 3.166,
     'na_rpb': 64.0,
     'ln1_g': 4.079,
     'ln1_b': 4.091,
     'ln2_g': 3.907,
     'ln2_b': 4.03}
    for name, (base, spread) in spreads.items():
        noise = np.random.default_rng([zlib.crc32(name.encode()), seed]).standard_normal(out[name].shape)
        drawn = base * np.exp(spread * noise) if base else spread * noise
        out[name] = __import__('jax').numpy.asarray(drawn.astype(out[name].dtype))
    for name, factor in factors.items():
        out[name] = (out[name] * factor).astype(out[name].dtype)
    return out
```

```python
from contextlib import ExitStack

import numpy as np

import concourse.bass as bass
from concourse import mybir

P = 128
F32 = mybir.dt.float32
F32R = mybir.dt.float32r
ALU = mybir.AluOpType
ACT = mybir.ActivationFunctionType
AX = mybir.AxisListType

D = 1024
DEPTH = 2
GRID_W = 64
SEQ = 512
CTX = 256
ROWS = SEQ // GRID_W
TOK = SEQ + CTX
LT = SEQ // P
NT = TOK // P
KT = D // P
HEADS = 4
HD = 64
DA_V = 2 * HD
ROPE = 32
MQ = HD + ROPE
Q_RANK, KV_RANK = D // 4, D // 8
NA_KH, NA_KW = 8, 16
D_FF = 4 * D
IN_WIDTH = 2720
COL_CQ = 1536
COL_CKV = COL_CQ + Q_RANK
COL_NQ = COL_CKV + KV_RANK + ROPE
ALPHA = (2.0 * DEPTH) ** 0.25
LN_EPS = 1e-6
RMS_EPS = 1e-6
SUBLN_EPS = 1e-5
LAM_INIT = [float(0.8 - 0.6 * np.exp(-0.3 * l)) for l in range(DEPTH)]
MASKED = -1.0e30

UW = 256
UC = KT * UW
IN_UNITS = [(c, min(UW, lim - c)) for lo, lim in ((0, COL_CQ), (COL_CQ, COL_CKV), (COL_CKV, COL_NQ),
                                                  (COL_NQ, IN_WIDTH)) for c in range(lo, lim, UW)]
N_IN = len(IN_UNITS)
N_OUT = D // UW
FG = 4
GF = FG * P
GROUPS = D_FF // GF
FU = 4
N_UNITS = N_IN + N_OUT + GROUPS * FU
WMOD_UNITS = 6 * D // UW
MR = 4

V_BMOD, V_G1, V_B1, V_G2, V_B2, V_QN, V_KN, V_C, V_CC, V_ROWS = 0, 48, 56, 64, 72, 80, 82, 83, 91, 99
SHIFT1, SCALE1, GATE1, SHIFT2, SCALE2, GATE2 = (8 * i for i in range(6))
SKEW = 64 * 129


def shape_constants():
    def inv(n):
        return (np.float32(10000.0) ** (np.float32(-2.0) * np.arange(n // 2, dtype=np.float32) / np.float32(n))).astype(np.float32)
    tok = np.arange(SEQ)
    row, col = (tok // GRID_W).astype(np.float32), (tok % GRID_W).astype(np.float32)

    def tables(width, parts):
        n = width // 2
        cos = np.ones((parts, SEQ), np.float32)
        sin = np.zeros((parts, SEQ), np.float32)
        rot = np.zeros((parts, parts), np.float32)
        first = 0 if width == HD else HD
        for d in range(first, parts):
            e = (d - first) % width
            pos = row if e < n else col
            ang = (pos * inv(n)[e % n % (n // 2)]).astype(np.float32)
            cos[d] = np.cos(ang)
            sin[d] = np.sin(ang)
            if e % n < n // 2:
                rot[d + n // 2, d] = -1.0
            else:
                rot[d - n // 2, d] = 1.0
        return cos, sin, rot

    c64, s64, r64 = tables(HD, P)
    c32, s32, r32 = tables(ROPE, MQ)
    q = np.arange(P) % GRID_W
    start = np.clip(q - NA_KW // 2, 0, GRID_W - NA_KW)
    k = np.arange(GRID_W)[None, :]
    inside = (k >= start[:, None]) & (k < start[:, None] + NA_KW)
    mask = np.where(inside, np.float32(0), np.float32(MASKED)).astype(np.float32)
    return {"k_cos64": c64, "k_sin64": s64, "k_rot64": r64, "k_cos32": c32, "k_sin32": s32,
            "k_rot32": r32, "k_mask": mask, "k_ident": np.eye(P, dtype=np.float32)}


def build(nc, A, out):
    ctx = ExitStack()
    with ctx:
        def sb(name, shape, dt=F32):
            return ctx.enter_context(nc.sbuf_tensor(name, shape, dt))

        def sem(name):
            return ctx.enter_context(nc.semaphore(name))

        xt_hi = sb("xt_hi", [P, KT, TOK], F32R)
        xt_lo = sb("xt_lo", [P, KT, TOK], F32R)
        w_raw = sb("w_raw", [P, 2, UC])
        w_hi = sb("w_hi", [P, 2, UC], F32R)
        w_lo = sb("w_lo", [P, 2, UC], F32R)
        hid_hi = sb("hid_hi", [P, FG, TOK], F32R)
        hid_lo = sb("hid_lo", [P, FG, TOK], F32R)
        arena = sb("arena", [P, 18432])
        cos64, sin64 = sb("cos64", [P, SEQ]), sb("sin64", [P, SEQ])
        cos32, sin32 = sb("cos32", [MQ, SEQ]), sb("sin32", [MQ, SEQ])
        rot64, rot32 = sb("rot64", [P, P]), sb("rot32", [MQ, MQ])
        ident = sb("ident", [P, P])
        mask = sb("mask", [P, GRID_W])
        vec = [sb(f"vec{l}", [P, V_ROWS]) for l in range(DEPTH)]
        modv = [sb(f"modv{l}", [P, 48, 2]) for l in range(DEPTH)]
        mod_a = [[sb(f"mod_a{l}{w}", [P, KT, 2]) for w in range(2)] for l in range(DEPTH)]
        mod_b = [[sb(f"mod_b{l}{w}", [P, KT, 2]) for w in range(2)] for l in range(DEPTH)]
        silu = sb("silu", [P, 2, KT])
        silu_tmp = sb("silu_tmp", [P, 2, KT])
        neg_lam = [sb(f"neg_lam{l}", [P, 1]) for l in range(DEPTH)]
        lam_tmp = sb("lam_tmp", [P, 4])
        subln = [sb(f"subln{l}", [P, DA_V]) for l in range(DEPTH)]
        att_st = sb("att_st", [P, 4, 12])
        ln_st = sb("ln_st", [P, 2, 17])
        rms_st = sb("rms_st", [P, 2 * NT])
        rms_eps = sb("rms_eps", [P, 2 * NT])
        rms_inv = sb("rms_inv", [P, 2 * NT])
        neg_half = sb("neg_half", [P, 2 * NT])

        def ar(c, *dims, parts=P):
            n = int(np.prod(dims))
            v = arena[0:parts, c:c + n]
            if len(dims) == 2:
                v = v.rearrange("p (a b) -> p a b", b=dims[1])
            if len(dims) == 3:
                v = v.rearrange("p (a b c) -> p a b c", b=dims[1], c=dims[2])
            return v

        wm_ring = ar(0, MR, KT, UW)
        vrow = ar(8192, DEPTH, P)
        lamv = ar(8448, 4 * DEPTH, HD)
        pad = ar(8960, DEPTH, P)
        gate_t = ar(9216, DEPTH, P)
        lam_junk = ar(9472, HD)
        da_q, da_k, da_v = ar(0, HEADS, TOK), ar(3072, HEADS, TOK), ar(6144, NT, HEADS * DA_V)
        da_raw, da_t = ar(9216, 2, SEQ), ar(10240, 2, SEQ)
        da_p, da_pt, da_y = ar(9216, 2, 2, TOK), ar(12288, 2, TOK), ar(13824, 2, 512)
        da_o, da_junk = ar(14848, 2, 128), ar(15104, 128)
        ml_q, ml_k, ml_v = ar(0, HEADS, TOK, parts=MQ), ar(3072, HEADS, TOK, parts=MQ), ar(6144, NT, 256)
        ml_rows, ml_cq = ar(7680, NT, Q_RANK + KV_RANK + ROPE), ar(10176, 2, TOK)
        ml_ckv, ml_kr = ar(11712, TOK), ar(12480, TOK)
        ml_wq, ml_wkv = ar(13248, 2, HEADS * MQ), ar(14016, 512)
        ml_raw, ml_t = ar(14528, 2, SEQ), ar(15552, 2, SEQ)
        ml_junk = ar(16576, Q_RANK)
        ml_p, ml_pt, ml_y = ar(7680, 2, 1, TOK), ar(9216, 2, TOK), ar(10752, 2, 256)
        na_q, na_k, na_v = ar(0, 2, TOK), ar(1536, 2, TOK), ar(3072, NT, 256)
        na_bias = ar(4608, HEADS, 14 * GRID_W)
        na_p, na_pt, na_y = ar(8192, 2, 1, TOK), ar(9728, 2, TOK), ar(11264, 2, 256)
        acc = ar(0, NT, D)
        x_in, x_n, x_out, h32 = ar(6144, 2, D), ar(8192, 2, D), ar(10240, 2, D), ar(12288, 2, D)
        relu, squares = ar(12288, 2, TOK), ar(10240, 2, TOK)
        gate_row, g_row, b_row = ar(14336, 2, D), ar(16384, D), ar(17408, D)

        psum = ctx.enter_context(nc.psum_tensor("psum", [P, 8 * 512], F32))

        def bank(b, n=512, parts=P, at=0):
            return psum[0:parts, b * 512 + at:b * 512 + at + n]

        y_dram = nc.dram_tensor("y_scratch", [NT, P, D], F32).ap()
        x_dram = [nc.dram_tensor(f"x_scratch{i}", [NT, P, D], F32).ap() for i in range(2)]
        gate_dram = nc.dram_tensor("gate_scratch", [DEPTH, 48, 2, P], F32).ap()
        skew_dram = nc.dram_tensor("skew_scratch", [DEPTH, HEADS * 15, SKEW], F32).ap()

        pe_phase, act_phase, dve_phase, pool_phase = (sem(n) for n in ("pe_phase", "act_phase", "dve_phase", "pool_phase"))
        raw_landed = [sem("raw_landed0"), sem("raw_landed1")]
        w_hi_ready, w_lo_ready = sem("w_hi_ready"), sem("w_lo_ready")
        const_landed, vrow_landed, lamv_landed, pad_landed = (sem(n) for n in ("const_landed", "vrow_landed", "lamv_landed", "pad_landed"))
        wm_landed = [sem(f"wm_landed{i}") for i in range(MR)]
        wm_used = sem("wm_used")
        pad_zeroed, skew_written, gate_written = sem("pad_zeroed"), sem("skew_written"), sem("gate_written")
        vec_turned, silu_exp, silu_ready, vec_ready = sem("vec_turned"), sem("silu_exp"), sem("silu_ready"), sem("vec_ready")
        modv_ready, gate_turned, gate_copied = sem("modv_ready"), sem("gate_turned"), sem("gate_copied")
        lam_dot, lam_exp = sem("lam_dot"), sem("lam_exp")
        dve_step = sem("dve_step")
        act_step = sem("act_step")
        pool_step = sem("pool_step")

        T_Q = [NT if l < DEPTH - 1 else LT for l in range(DEPTH)]

        class Signal:
            def __init__(self, sem, base):
                self.sem, self.base = sem, base

            def at(self, n):
                return self.sem, self.base + n

        semaphores, counted = {}, {}

        def signals(family, **increments):
            of = {}
            for name, n in increments.items():
                key = f"{family}_{name}"
                if key not in semaphores:
                    semaphores[key], counted[key] = sem(key), 0
                of[name] = Signal(semaphores[key], counted[key])
                counted[key] += n
            return of

        def halves(T):
            return 16 * ((T + 1) // 2), 16 * (T // 2)

        def ln_signals(T, T_turned, rows):
            a, b = halves(T)
            c, d = halves(T if rows else 0)
            r = T if rows else 0
            return signals("ln", x_loaded0=a, x_loaded1=b, summed=r, variance=r, rstd=r, stats=r, normed=r, turned=T_turned, h_act=T_turned,
                           h_dve=T_turned, hi=T_turned, lo=T_turned, x_gained=r, x_new=r, x_stored0=c, x_stored1=d,
                           rows_landed=16 * (4 if T == NT else 3) if rows else 0)

        X0 = ln_signals(NT, NT, False)
        IN, ML, AT, YT, OP, LN, FF, BIAS = [], [], [], [], [], [], [], []
        for T in T_Q:
            a, b = halves(T)
            IN.append([signals("in", tile=8, raw=8, rot=8, done=8, v=2 * NT, v_copied=2 * NT),
                       signals("in", tile=2 * HEADS, raw=HEADS, rot=HEADS + 1, done=HEADS + 1, v=T + NT, v_copied=0),
                       signals("in", tile=4, raw=0, rot=0, done=4, v=NT, v_copied=NT)])
            ML.append(signals("ml", rows_copied=T + NT, mean_squares=1, rms=1, normed=NT, turned=NT, evacuated=NT, up=HEADS, weights=32, v_ready=NT, v_copied=NT))
            n = HEADS * T
            AT.append([signals("at", scores=k * n, negmax=k * n, probs=k * n, mixed=(k - 1) * n, mean_square=(k - 1) * n, rms=(k - 1) * n, turned=n, turned_copied=n,
                               mixed_values=n, y=n, y_stored0=a, y_stored1=b) for k in (2, 1, 1)])
            BIAS.append(signals("bias", landed=16 * 2 * HEADS, ready=1))
            YT.append(signals("yt", loaded0=a, loaded1=b, turned=T, hi=T, lo=T))
            OP.append(signals("op", product=N_OUT * T, gated=N_OUT * T))
            LN.append([ln_signals(T, T, True), ln_signals(T, T if T == NT else 0, True)])
            FF.append(signals("ff", hidden=GROUPS * FG, bank1_free=2 + GROUPS * FG, hid_hi=GROUPS * FG, hid_lo=2 + GROUPS * FG, squared=GROUPS * FG,
                              product=GROUPS * 2 * T, bank2_free=4 + GROUPS * 2 * T))

        def chunks(l, all_tokens=False):
            return [(0, SEQ), (SEQ, CTX)] if all_tokens or T_Q[l] == NT else [(0, SEQ)]

        phases = {}
        for l in range(DEPTH):
            for name in (["setup", "x0"] if l == 0 else []) + ["inA", "atA", "inB", "atB", "inC", "atC", "yT", "out", "ln0", "ffn", "ln1"]:
                phases[(l, name)] = len(phases)

        def fence(eng, l, name):
            n = phases[(l, name)]
            if n:
                for s in (pe_phase, act_phase, dve_phase, pool_phase):
                    eng.wait_ge(s, n)

        def in_unit(l, u):
            return l * N_UNITS + u

        def w_view(t, u, cols=UW):
            return t[:, u % 2, 0:KT * cols].rearrange("p (k n) -> p k n", n=cols)

        def w_view_ff2(t, u):
            return t[:, u % 2, :].rearrange("p (k n) -> p k n", n=512)

        ITEMS = [[(qt, h) for qt in range(T_Q[l]) for h in range(HEADS)] for l in range(DEPTH)]

        block = ctx.enter_context(nc.Block())

        @block.sync
        def _(sp):
            def load(u, dst, src):
                if not isinstance(u, int) or u >= 2:
                    sp.wait_ge(w_lo_ready, u - 1)
                return sp.dma_start(dst, src)

            def projection(l, u):
                g = in_unit(l, u)
                if u < N_IN:
                    c, n = IN_UNITS[u]
                    src = A["w_in"][l, :, c:c + n]
                else:
                    c, n = (u - N_IN) * UW, UW
                    src = A["w_out"][l, :, c:c + n]
                load(g, w_view(w_raw, g, n), src.rearrange("(k p) n -> p k n", p=P)).then_inc(raw_landed[g % 2], 16)

            def wmod(l, m, at, first):
                k = at
                if not first:
                    sp.wait_ge(wm_used, l * WMOD_UNITS + m - MR + 1)
                src = A["w_mod"][l, :, bass.ds(m * UW, UW)] if not isinstance(m, int) else A["w_mod"][l, :, m * UW:(m + 1) * UW]
                sp.dma_start(wm_ring[:, k, :, :], src.rearrange("(k p) n -> p k n", p=P)).then_inc(wm_landed[k], 16)

            projection(0, 0)
            projection(0, 1)
            for k in range(MR):
                wmod(0, k, k, True)
            with sp.Fori(1, WMOD_UNITS // MR) as i:
                for k in range(MR):
                    wmod(0, i * MR + k, k, False)
            with sp.Fori(0, WMOD_UNITS // MR) as i:
                for k in range(MR):
                    wmod(1, i * MR + k, k, False)
            for l in range(DEPTH):
                for u in range(2 if l == 0 else 0, N_IN + N_OUT):
                    projection(l, u)
                u0 = in_unit(l, N_IN + N_OUT)
                with sp.Fori(0, GROUPS) as i:
                    for k in range(FU):
                        s = (u0 + k) % 2
                        if k < 2:
                            src = A["w_ff1"][l, :, bass.ds(i * GF + k * UW, UW)].rearrange("(k p) n -> p k n", p=P)
                            dst = w_view(w_raw, s)
                        else:
                            src = A["w_ff2"][l, bass.ds(i * GF, GF), (k - 2) * 512:(k - 1) * 512].rearrange("(k p) n -> p k n", p=P)
                            dst = w_view_ff2(w_raw, s)
                        load(i * FU + (u0 + k), dst, src).then_inc(raw_landed[s], 16)

        @block.gpsimd
        def _(pool):
            def end():
                pool.drain().then_inc(pool_phase, 1)

            consts = [(cos64, "k_cos64"), (sin64, "k_sin64"), (cos32, "k_cos32"), (sin32, "k_sin32"),
                      (rot64, "k_rot64"), (rot32, "k_rot32"), (ident, "k_ident"), (mask, "k_mask")]
            pool.memset(pad[:, :, :], 0.0).then_inc(pad_zeroed, 1)
            pool.memset(vrow[:, :, :], 0.0).then_inc(pad_zeroed, 1)
            pool.memset(neg_half[:, :], -0.5).then_inc(pad_zeroed, 1)
            for t, name in consts:
                pool.dma_start(t[:, :], A[name]).then_inc(const_landed, 16)
            pool.wait_ge(pad_zeroed, 3)
            for l in range(DEPTH):
                for r, src in ((V_BMOD, A["b_mod"][l]), (V_G1, A["ln1_g"][l]), (V_B1, A["ln1_b"][l]), (V_G2, A["ln2_g"][l]),
                               (V_B2, A["ln2_b"][l]), (V_QN, A["mla_q_norm_g"][l]), (V_KN, A["mla_kv_norm_g"][l]),
                               (V_C, A["c"][0]), (V_CC, A["c_ctx"])):
                    n = src.shape[0] // P
                    pool.dma_start(vrow[r:r + n, l, :], src.rearrange("(a p) -> a p", p=P)).then_inc(vrow_landed, 16)
                for i, name in enumerate(("da_lam_q1", "da_lam_k1", "da_lam_q2", "da_lam_k2")):
                    pool.dma_start(lamv[:, 4 * l + i, :], A[name][l].partition_broadcast(P)).then_inc(lamv_landed, 16)
                pool.dma_start(subln[l][:, :], A["da_subln_g"][l].partition_broadcast(P)).then_inc(lamv_landed, 16)
                pool.dma_start(pad[0:HEADS * 15, l, 48:79], A["na_rpb"][l].rearrange("h y x -> (h y) x")).then_inc(pad_landed, 16)
            pool.wait_ge(pad_landed, 16 * DEPTH)
            for l in range(DEPTH):
                dst = skew_dram[l].rearrange("r (q x) -> r q x", x=129)[:, :, 0:P]
                src = pad[0:HEADS * 15, l, :].unsqueeze(1).broadcast_to([HEADS * 15, GRID_W, P])
                pool.dma_start(dst, src).then_inc(skew_written, 16)
            for l in range(DEPTH):
                pool.wait_ge(gate_copied, l + 1)
                pool.dma_start(gate_dram[l].rearrange("n s p -> (n s) p"), gate_t[0:96, l, :]).then_inc(gate_written, 16)
            pool.wait_ge(skew_written, 16 * DEPTH)
            pool.wait_ge(gate_written, 16 * DEPTH)
            end()

            def x_source(l, w, t):
                if l == 0 and w == 0:
                    return A["x"][0, t * P:(t + 1) * P, :] if t < LT else A["ctx"][0, (t - LT) * P:(t - LT + 1) * P, :]
                return x_dram[1 - w][t]

            fence(pool, 0, "x0")
            for t in range(NT):
                if t >= 2:
                    pool.wait_ge(*X0["turned"].at(t - 1))
                pool.dma_start(x_in[:, t % 2, :], x_source(0, 0, t)).then_inc((X0["x_loaded0"], X0["x_loaded1"])[t % 2].sem, 16)
            end()

            def store_y(l, g, off, width, y):
                s = AT[l][g]
                for qt in range(T_Q[l]):
                    if g == 0:
                        for n in range(HEADS * qt, HEADS * (qt + 1)):
                            st = att_st[:, n % 4, :]
                            pool.wait_ge(*s["mean_square"].at(n + 1))
                            pool.tensor_tensor(st[:, 9:10], st[:, 8:9], neg_half[:, 0:1], ALU.pow).then_inc(s["rms"].sem, 1)
                    pool.wait_ge(*s["y"].at(HEADS * (qt + 1)))
                    pool.dma_start(y_dram[qt][:, off:off + width], y[:, qt % 2, :]).then_inc((s["y_stored0"], s["y_stored1"])[qt % 2].sem, 16)
                for i, q in enumerate((s["y_stored0"], s["y_stored1"])):
                    pool.wait_ge(*q.at(16 * len(range(i, T_Q[l], 2))))

            def ln(l, w):
                s = LN[l][w]
                last = l == DEPTH - 1 and w == 1
                pool.wait_ge(*LN[l][w]["rows_landed"].at(16 * (4 if T_Q[l] == NT else 3)))
                for t in range(T_Q[l]):
                    if t >= 2:
                        pool.wait_ge(*s["summed"].at(t - 1))
                    pool.dma_start(x_in[:, t % 2, :], x_source(l, w, t)).then_inc((s["x_loaded0"], s["x_loaded1"])[t % 2].sem, 16)
                    pool.wait_ge(*s["variance"].at(t + 1))
                    st = ln_st[:, t % 2, :]
                    pool.tensor_tensor(st[:, 15:16], st[:, 14:15], neg_half[:, 0:1], ALU.pow).then_inc(s["rstd"].sem, 1)
                    if t >= 1:
                        ln_rows(l, w, t - 1, last)
                ln_rows(l, w, T_Q[l] - 1, last)
                for i, q in enumerate((s["x_stored0"], s["x_stored1"])):
                    pool.wait_ge(*q.at(16 * len(range(i, T_Q[l], 2))))

            def ln_rows(l, w, t, last):
                s = LN[l][w]
                st = (s["x_stored0"], s["x_stored1"])[t % 2]
                pool.wait_ge(*s["normed"].at(t + 1))
                if t >= 2:
                    pool.wait_ge(*st.at(16 * (t // 2)))
                pool.tensor_tensor(x_out[:, t % 2, :], x_n[:, t % 2, :], g_row, ALU.mult).then_inc(s["x_gained"].sem, 1)
                pool.wait_ge(*s["x_gained"].at(t + 1))
                pool.tensor_tensor(x_out[:, t % 2, :], x_out[:, t % 2, :], b_row, ALU.add).then_inc(s["x_new"].sem, 1)
                pool.wait_ge(*s["x_new"].at(t + 1))
                dst = out[0, t * P:(t + 1) * P, :] if last else x_dram[w][t]
                pool.dma_start(dst, x_out[:, t % 2, :]).then_inc(st.sem, 16)

            def rows(l, w):
                s = LN[l][w]["rows_landed"]
                gate = GATE1 if w == 0 else GATE2
                for strm in range(2 if T_Q[l] == NT else 1):
                    pool.dma_start(gate_row[:, strm, :].rearrange("p (k n) -> p k n", n=P), gate_dram[l, gate:gate + KT, strm, :].partition_broadcast(P)).then_inc(s.sem, 16)
                pool.dma_start(g_row, A["ln1_g" if w == 0 else "ln2_g"][l].partition_broadcast(P)).then_inc(s.sem, 16)
                pool.dma_start(b_row, A["ln1_b" if w == 0 else "ln2_b"][l].partition_broadcast(P)).then_inc(s.sem, 16)

            for l in range(DEPTH):
                fence(pool, l, "inA")
                end()
                fence(pool, l, "atA")
                store_y(l, 0, 0, 512, da_y)
                end()
                fence(pool, l, "inB")
                pool.dma_start(ml_wq[:, :, :], A["mla_w_uq"][l].rearrange("(k p) n -> p k n", p=P)).then_inc(ML[l]["weights"].sem, 16)
                pool.dma_start(ml_wkv[:, :], A["mla_w_ukv"][l]).then_inc(ML[l]["weights"].sem, 16)
                pool.wait_ge(*ML[l]["mean_squares"].at(1))
                pool.tensor_tensor(rms_inv[:, :], rms_eps[:, :], neg_half[:, :], ALU.pow).then_inc(ML[l]["rms"].sem, 1)
                end()
                fence(pool, l, "atB")
                store_y(l, 1, 512, 256, ml_y)
                end()
                fence(pool, l, "inC")
                for rr in range(2):
                    for h in range(HEADS):
                        r = h * 15 + 1 - rr
                        src = skew_dram[l, r:r + 14, 63:63 + GRID_W * P].rearrange("j (q k) -> q j k", k=P)[:, :, 0:GRID_W]
                        dst = na_bias[rr * GRID_W:(rr + 1) * GRID_W, h, :].rearrange("p (j k) -> p j k", k=GRID_W)
                        pool.dma_start(dst, src).then_inc(BIAS[l]["landed"].sem, 16)
                pool.wait_ge(*BIAS[l]["landed"].at(16 * 2 * HEADS))
                b3 = na_bias[:, :, :].rearrange("p h (j k) -> p (h j) k", k=GRID_W)
                pool.tensor_tensor(b3, b3, mask[:, :].unsqueeze(1).broadcast_to([P, HEADS * 14, GRID_W]), ALU.add).then_inc(BIAS[l]["ready"].sem, 1)
                end()
                fence(pool, l, "atC")
                store_y(l, 2, 768, 256, na_y)
                end()
                fence(pool, l, "yT")
                for t in range(T_Q[l]):
                    if t >= 2:
                        pool.wait_ge(*YT[l]["turned"].at(t - 1))
                    pool.dma_start(x_in[:, t % 2, :], y_dram[t]).then_inc((YT[l]["loaded0"], YT[l]["loaded1"])[t % 2].sem, 16)
                end()
                fence(pool, l, "out")
                rows(l, 0)
                end()
                fence(pool, l, "ln0")
                ln(l, 0)
                end()
                fence(pool, l, "ffn")
                rows(l, 1)
                end()
                fence(pool, l, "ln1")
                ln(l, 1)
                end()

        @block.scalar
        def _(act):
            def end():
                act.drain().then_inc(act_phase, 1)

            def split(u):
                if isinstance(u, int) and u >= DEPTH * N_UNITS:
                    return
                split_at(u, u % 2, u // 2)

            def split_at(u, slot, turn):
                act.wait_ge(raw_landed[slot], (turn + 1) * 16)
                act.activation(w_hi[:, slot, :], w_raw[:, slot, :], ACT.Copy).then_inc(w_hi_ready, 1)

            act.wait_ge(vec_turned, DEPTH)
            act.wait_ge(vec_ready, 1)
            act.activation(silu_tmp[:, :, :], vec[0][:, V_C:V_ROWS].rearrange("p (s k) -> p s k", k=KT), ACT.Exp, scale=-1.0).then_inc(silu_exp, 1)
            for l in range(DEPTH):
                act.wait_ge(lam_dot, l + 1)
                act.activation(lam_tmp[:, 2 * l:2 * l + 2], lam_tmp[:, 2 * l:2 * l + 2], ACT.Exp).then_inc(lam_exp, 1)
            for l in range(DEPTH):
                act.wait_ge(gate_turned, l + 1)
                act.activation(gate_t[0:96, l, :], bank(4 + l, P, 96), ACT.Copy).then_inc(gate_copied, 1)
            split(0)
            split(1)
            end()

            def modulated(s, t, l, w, n_prev):
                strm = 0 if t < LT else 1
                act.wait_ge(*s["turned"].at(t + 1))
                if t >= 2:
                    act.wait_ge(*s["lo"].at(t - 1))
                for k in range(4):
                    i = act.activation(h32[:, t % 2, k * P:(k + 1) * P], bank(2 * (t % 2), P, at=k * P), ACT.Identity,
                                       bias=mod_b[l][w][:, k, strm:strm + 1], scale=mod_a[l][w][:, k, strm:strm + 1])
                i.then_inc(s["h_act"].sem, 1)
                act.wait_ge(*s["h_act"].at(t + 1))
                act.wait_ge(*s["h_dve"].at(t + 1))
                act.activation(xt_hi[:, :, t * P:(t + 1) * P], h32[:, t % 2, :].rearrange("p (k n) -> p k n", n=P), ACT.Copy).then_inc(s["hi"].sem, 1)

            fence(act, 0, "x0")
            for t in range(NT):
                modulated(X0, t, 0, 0, 0)
            end()

            def in_tile(s, i, psum_bank, parts, raw, dst, scale, ctx_too, prev_raw_free):
                act.wait_ge(*s["tile"].at(i + 1))
                if i >= 2:
                    act.wait_ge(*s["done"].at(i - 1))
                if ctx_too:
                    act.activation(dst[:, SEQ:TOK], bank(psum_bank + 1, CTX, parts), ACT.Copy, scale=scale)
                act.activation(raw[0:parts, i % 2, :], bank(psum_bank, SEQ, parts), ACT.Copy, scale=scale).then_inc(s["raw"].sem, 1)

            def attention(l, g, nmaps, p, pt, from_sbuf):
                s = AT[l][g]
                items = ITEMS[l]

                def exps(n):
                    qt, h = items[n]
                    nk = TOK if qt < LT else CTX
                    if n >= 2:
                        act.wait_ge(*s["turned"].at(n - 1))
                    for m in range(nmaps):
                        act.wait_ge(*s["negmax"].at(n * nmaps + m + 1))
                        b = 2 * m if nmaps == 2 else 2 * (n % 2)
                        src = p[:, n % 2, m, 0:nk] if from_sbuf and qt < LT else bank(b, nk)
                        act.activation(p[:, n % 2, m, 0:nk], src, ACT.Exp, bias=att_st[:, n % 4, m:m + 1],
                                       accum_out=att_st[:, n % 4, 2 + m:3 + m]).then_inc(s["probs"].sem, 1)

                exps(0)
                for n, (qt, h) in enumerate(items):
                    nk = TOK if qt < LT else CTX
                    act.wait_ge(*s["turned"].at(n + 1))
                    if n >= 2:
                        act.wait_ge(*s["mixed_values"].at(n - 1))
                    act.activation(pt[:, n % 2, 0:nk], bank(4, nk), ACT.Copy).then_inc(s["turned_copied"].sem, 1)
                    if n + 1 < len(items):
                        exps(n + 1)

            for l in range(DEPTH):
                q_ctx = T_Q[l] == NT
                fence(act, l, "inA")
                s = IN[l][0]
                for i in range(8):
                    dst = da_q[:, i, :] if i < HEADS else da_k[:, i - HEADS, :]
                    in_tile(s, i, 2 * (i % 2), P, da_raw, dst, HD ** -0.5 if i < HEADS else 1.0, i >= HEADS or q_ctx, None)
                    if i % 2:
                        split(in_unit(l, i // 2 + 2))
                for u in range(2):
                    for t in range(NT):
                        act.wait_ge(*s["v"].at(u * NT + t + 1))
                        act.activation(da_v[:, t, u * UW:(u + 1) * UW], bank(6 + t % 2, UW), ACT.Copy).then_inc(s["v_copied"].sem, 1)
                    split(in_unit(l, 4 + u + 2))
                end()
                fence(act, l, "atA")
                attention(l, 0, 2, da_p, da_pt, False)
                end()

                fence(act, l, "inB")
                s, m = IN[l][1], ML[l]
                n = 0
                for u, tiles, c, w in ((6, T_Q[l], 0, Q_RANK), (7, NT, Q_RANK, KV_RANK + ROPE)):
                    for t in range(tiles):
                        act.wait_ge(*s["v"].at(n + 1))
                        act.activation(ml_rows[:, t, c:c + w], bank(n % 4, w), ACT.Copy).then_inc(m["rows_copied"].sem, 1)
                        n += 1
                    split(in_unit(l, u + 2))
                for t in range(NT):
                    act.wait_ge(*m["turned"].at(t + 1))
                    b = 4 + t % 2
                    tk = slice(t * P, (t + 1) * P)
                    if t < T_Q[l]:
                        for k in range(2):
                            act.activation(ml_cq[:, k, tk], bank(b, P, at=k * P), ACT.Copy, scale=vec[l][:, V_QN + k:V_QN + k + 1])
                    act.activation(ml_kr[HD:MQ, tk], psum[HD:MQ, b * 512 + 3 * P:b * 512 + 4 * P], ACT.Copy)
                    act.activation(ml_ckv[:, tk], bank(b, P, at=2 * P), ACT.Copy, scale=vec[l][:, V_KN:V_KN + 1]).then_inc(m["evacuated"].sem, 1)
                for h in range(HEADS):
                    in_tile(s, h, 2 * (h % 2), MQ, ml_raw, ml_q[:, h, :], MQ ** -0.5, q_ctx, None)
                for h in range(HEADS):
                    act.wait_ge(*s["tile"].at(HEADS + h + 1))
                    b = 2 * (h % 2)
                    act.activation(ml_k[0:HD, h, :], psum[0:HD, b * 512:b * 512 + TOK], ACT.Copy).then_inc(m["up"].sem, 1)
                for t in range(NT):
                    act.wait_ge(*m["v_ready"].at(t + 1))
                    act.activation(ml_v[:, t, :], bank(6 + t % 2, 256), ACT.Copy).then_inc(m["v_copied"].sem, 1)
                act.wait_ge(*s["done"].at(HEADS + 1))
                for h in range(HEADS):
                    act.activation(ml_k[HD:MQ, h, SEQ:TOK], ml_kr[HD:MQ, SEQ:TOK], ACT.Copy)
                    act.activation(ml_k[HD:MQ, h, 0:SEQ], ml_t[HD:MQ, 0, :], ACT.Copy)
                end()
                fence(act, l, "atB")
                attention(l, 1, 1, ml_p, ml_pt, False)
                end()

                fence(act, l, "inC")
                s = IN[l][2]
                for i in range(4):
                    act.wait_ge(*s["tile"].at(i + 1))
                    dst, sc = (na_q[:, i, :], HD ** -0.5) if i < 2 else (na_k[:, i - 2, :], 1.0)
                    n = TOK if i >= 2 or q_ctx else SEQ
                    act.activation(dst[:, 0:n], bank(2 * (i % 2), n), ACT.Copy, scale=sc).then_inc(s["done"].sem, 1)
                    if i % 2:
                        split(in_unit(l, 8 + i // 2 + 2))
                for t in range(NT):
                    act.wait_ge(*s["v"].at(t + 1))
                    act.activation(na_v[:, t, :], bank(6 + t % 2, 256), ACT.Copy).then_inc(s["v_copied"].sem, 1)
                split(in_unit(l, 12))
                end()
                fence(act, l, "atC")
                attention(l, 2, 1, na_p, na_pt, True)
                end()

                fence(act, l, "yT")
                for t in range(T_Q[l]):
                    act.wait_ge(*YT[l]["turned"].at(t + 1))
                    act.activation(xt_hi[:, :, t * P:(t + 1) * P], bank(2 * (t % 2), D).rearrange("p (k n) -> p k n", n=P), ACT.Copy).then_inc(YT[l]["hi"].sem, 1)
                end()
                fence(act, l, "out")
                for u in range(N_OUT):
                    act.wait_ge(*OP[l]["product"].at((u + 1) * T_Q[l]))
                    split(in_unit(l, N_IN + u + 2))
                end()
                fence(act, l, "ln0")

                def ln(w, turn):
                    s = LN[l][w]
                    for t in range(T_Q[l]):
                        act.wait_ge(*s["stats"].at(t + 1))
                        if t >= 2:
                            act.wait_ge(*s["x_new"].at(t - 1))
                            if turn:
                                act.wait_ge(*s["turned"].at(t - 1))
                        act.activation(x_n[:, t % 2, :], acc[:, t, :], ACT.Identity, bias=ln_st[:, t % 2, 16:17],
                                       scale=ln_st[:, t % 2, 15:16]).then_inc(s["normed"].sem, 1)
                        if turn and t >= 1:
                            modulated(s, t - 1, l if w == 0 else l + 1, 1 - w, 0)
                    if turn:
                        modulated(s, T_Q[l] - 1, l if w == 0 else l + 1, 1 - w, 0)

                ln(0, True)
                end()
                fence(act, l, "ffn")
                s = FF[l]
                tokens = T_Q[l] * P
                u0 = in_unit(l, N_IN + N_OUT)
                act.drain().then_inc(s["bank1_free"].sem, 2)

                def group(i, more):
                    for a in range(2):
                        for j in (2 * a, 2 * a + 1):
                            act.wait_ge(*s["hidden"].at(i * FG + j + 1))
                            act.wait_ge(*s["hid_lo"].at(i * FG + j + 1))
                            act.activation(relu[:, j % 2, 0:tokens], bank(2 * (j % 2), tokens), ACT.Relu).then_inc(s["bank1_free"].sem, 1)
                            act.wait_ge(*s["bank1_free"].at(i * FG + j + 3))
                            act.activation(hid_hi[:, j, 0:tokens], relu[:, j % 2, 0:tokens], ACT.Square).then_inc(s["hid_hi"].sem, 1)
                        u = u0 + a + 2
                        split_at(None, u % 2, i * 2 + u // 2)
                    for b in range(2):
                        act.wait_ge(*s["product"].at(i * (2 * T_Q[l]) + (b + 1) * T_Q[l]))
                        if more:
                            u = u0 + 2 + b + 2
                            split_at(None, u % 2, i * 2 + u // 2)

                with act.Fori(0, GROUPS - 1) as i:
                    group(i, True)
                group(GROUPS - 1, l + 1 < DEPTH)
                end()
                fence(act, l, "ln1")
                ln(1, l + 1 < DEPTH)
                end()

        @block.vector
        def _(dve):
            def end():
                dve.drain().then_inc(dve_phase, 1)

            steps = [0]

            def link(ins):
                steps[0] += 1
                ins.then_inc(dve_step, 1)
                dve.wait_ge(dve_step, steps[0])

            def split(u):
                if isinstance(u, int) and u >= DEPTH * N_UNITS:
                    return
                split_at(u, u % 2)

            def split_at(u, slot):
                dve.wait_ge(w_hi_ready, u + 1)
                dve.tensor_tensor(w_lo[:, slot, :], w_raw[:, slot, :], w_hi[:, slot, :].bitcast(F32), ALU.subtract).then_inc(w_lo_ready, 1)

            dve.memset(rms_st[:, :], 1.0)
            for l in range(DEPTH):
                dve.wait_ge(vec_turned, l + 1)
                dve.tensor_copy(vec[l][:, :], bank(2 + l, V_ROWS)).then_inc(vec_ready, 1)
            dve.wait_ge(silu_exp, 1)
            dve.wait_ge(vec_ready, 2)
            link(dve.tensor_scalar(silu_tmp[:, :, :], silu_tmp[:, :, :], 1.0, None, ALU.add))
            link(dve.reciprocal(silu_tmp[:, :, :], silu_tmp[:, :, :]))
            dve.tensor_tensor(silu[:, :, :], vec[0][:, V_C:V_ROWS].rearrange("p (s k) -> p s k", k=KT), silu_tmp[:, :, :], ALU.mult).then_inc(silu_ready, 1)
            dve.wait_ge(lamv_landed, 16 * 5 * DEPTH)
            for l in range(DEPTH):
                link(dve.tensor_tensor_reduce(lam_junk, lamv[:, 4 * l, :], lamv[:, 4 * l + 1, :], 1.0, 0.0, ALU.mult, ALU.add, lam_tmp[:, 2 * l:2 * l + 1]))
                dve.tensor_tensor_reduce(lam_junk, lamv[:, 4 * l + 2, :], lamv[:, 4 * l + 3, :], 1.0, 0.0, ALU.mult, ALU.add, lam_tmp[:, 2 * l + 1:2 * l + 2]).then_inc(lam_dot, 1)
                dve.wait_ge(lam_dot, l + 1)
                dve.tensor_scalar(subln[l][:, :], subln[l][:, :], 1.0 - LAM_INIT[l], None, ALU.mult)
            for l in range(DEPTH):
                dve.wait_ge(lam_exp, l + 1)
                link(dve.tensor_tensor(neg_lam[l][:, :], lam_tmp[:, 2 * l + 1:2 * l + 2], lam_tmp[:, 2 * l:2 * l + 1], ALU.subtract))
                link(dve.tensor_scalar(neg_lam[l][:, :], neg_lam[l][:, :], LAM_INIT[l], None, ALU.subtract))
            for l in range(DEPTH):
                dve.wait_ge(wm_used, (l + 1) * WMOD_UNITS)
                link(dve.tensor_tensor(modv[l][:, :, :], bank(l, 96).rearrange("p (n s) -> p n s", s=2),
                                       vec[l][:, V_BMOD:V_BMOD + 48].unsqueeze(2).broadcast_to([P, 48, 2]), ALU.add))
                for w, (sh, sc) in enumerate(((SHIFT1, SCALE1), (SHIFT2, SCALE2))):
                    a, b = mod_a[l][w], mod_b[l][w]
                    link(dve.tensor_scalar(a[:, :, :], modv[l][:, sc:sc + KT, :], 1.0, None, ALU.add))
                    if w == 0 and l == 0:
                        link(dve.tensor_copy(b[:, :, :], modv[l][:, sh:sh + KT, :]))
                        continue
                    v, g0, b0 = (vec[l], V_G1, V_B1) if w == 1 else (vec[l - 1], V_G2, V_B2)
                    link(dve.tensor_tensor(b[:, :, :], a[:, :, :], v[:, b0:b0 + KT].unsqueeze(2).broadcast_to([P, KT, 2]), ALU.mult))
                    link(dve.tensor_tensor(b[:, :, :], b[:, :, :], modv[l][:, sh:sh + KT, :], ALU.add))
                    ins = dve.tensor_tensor(a[:, :, :], a[:, :, :], v[:, g0:g0 + KT].unsqueeze(2).broadcast_to([P, KT, 2]), ALU.mult)
                    if w == 0:
                        link(ins)
                ins.then_inc(modv_ready, 1)
            split(0)
            split(1)
            end()

            def modulated(s, t, l, w):
                strm = 0 if t < LT else 1
                dve.wait_ge(*s["turned"].at(t + 1))
                if t >= 2:
                    dve.wait_ge(*s["lo"].at(t - 1))
                for k in range(4, 8):
                    i = dve.tensor_scalar(h32[:, t % 2, k * P:(k + 1) * P], bank(2 * (t % 2) + 1, P, at=(k - 4) * P),
                                          mod_a[l][w][:, k, strm:strm + 1], mod_b[l][w][:, k, strm:strm + 1], ALU.mult, ALU.add)
                i.then_inc(s["h_dve"].sem, 1)

            def low(s, t):
                dve.wait_ge(*s["hi"].at(t + 1))
                tk = slice(t * P, (t + 1) * P)
                dve.tensor_tensor(xt_lo[:, :, tk], h32[:, t % 2, :].rearrange("p (k n) -> p k n", n=P),
                                  xt_hi[:, :, tk].bitcast(F32), ALU.subtract).then_inc(s["lo"].sem, 1)

            fence(dve, 0, "x0")
            for t in range(NT):
                modulated(X0, t, 0, 0)
                low(X0, t)
            end()

            def rotate(s, i, rot_bank, parts, lo, raw, tmp, dst, cos, sin):
                r = slice(lo, parts)
                dve.wait_ge(*s["raw"].at(i + 1))
                if i >= 1:
                    dve.wait_ge(*s["done"].at(i))
                dve.tensor_tensor(tmp[r, 0, :], raw[r, i % 2, :] if raw is not ml_kr else ml_kr[r, 0:SEQ], cos[r, :], ALU.mult)
                dve.wait_ge(*s["rot"].at(i + 1))
                link(dve.tensor_tensor(tmp[r, 1, :], psum[r, rot_bank * 512:rot_bank * 512 + SEQ], sin[r, :], ALU.mult))
                dve.tensor_tensor(dst, tmp[r, 0, :], tmp[r, 1, :], ALU.add).then_inc(s["done"].sem, 1)

            def attention(l, g, nmaps, p, y, dv, bias):
                s = AT[l][g]
                items = ITEMS[l]

                def maxima(n):
                    qt, h = items[n]
                    nk = TOK if qt < LT else CTX
                    for m in range(nmaps):
                        dve.wait_ge(*s["scores"].at(n * nmaps + m + 1))
                        b = 2 * m if nmaps == 2 else 2 * (n % 2)
                        src = bank(b, nk)
                        if bias is not None and qt < LT:
                            if n >= 2:
                                dve.wait_ge(*s["turned"].at(n - 1))
                            j = (6 - 2 * qt) * GRID_W
                            dve.tensor_tensor(p[:, n % 2, 0, 0:SEQ], bank(b, SEQ), bias[:, h, j:j + SEQ], ALU.add)
                            link(dve.tensor_copy(p[:, n % 2, 0, SEQ:TOK], bank(b + 1, CTX)))
                            src = p[:, n % 2, 0, :]
                        dve.tensor_reduce(att_st[:, n % 4, m:m + 1], src, AX.X, ALU.max, negate=True).then_inc(s["negmax"].sem, 1)

                def mix(n):
                    qt, h = items[n]
                    nk = TOK if qt < LT else CTX
                    st = att_st[:, n % 4, :]
                    dve.wait_ge(*s["probs"].at(2 * n + 2))
                    link(dve.reciprocal(st[:, 4:5], st[:, 3:4]))
                    link(dve.tensor_scalar(st[:, 5:6], st[:, 2:3], st[:, 4:5], neg_lam[l][:, 0:1], ALU.mult, ALU.mult))
                    dve.scalar_tensor_tensor(out=p[:, n % 2, 0, 0:nk], in0=p[:, n % 2, 1, 0:nk], scalar=st[:, 5:6],
                                             in1=p[:, n % 2, 0, 0:nk], op0=ALU.mult, op1=ALU.add).then_inc(s["mixed"].sem, 1)

                def finish(n):
                    qt, h = items[n]
                    st = att_st[:, n % 4, :]
                    o = bank(6 + n % 2, dv)
                    dst = y[:, qt % 2, h * dv:(h + 1) * dv]
                    dve.wait_ge(*s["probs"].at((n + 1) * nmaps))
                    link(dve.reciprocal(st[:, 6:7], st[:, 2:3]))
                    dve.wait_ge(*s["mixed_values"].at(n + 1))
                    if nmaps == 1:
                        if h == 0 and qt >= 2:
                            dve.wait_ge(*(s["y_stored0"], s["y_stored1"])[qt % 2].at(16 * (qt // 2)))
                        dve.tensor_scalar(dst, o, st[:, 6:7], None, ALU.mult).then_inc(s["y"].sem, 1)
                        return
                    oh = da_o[:, n % 2, :]
                    if n >= 2:
                        dve.wait_ge(*s["y"].at(n - 1))
                    link(dve.tensor_scalar(oh, o, st[:, 6:7], None, ALU.mult))
                    link(dve.tensor_tensor_reduce(da_junk, oh, oh, 1.0 / DA_V, 0.0, ALU.mult, ALU.add, st[:, 7:8]))
                    dve.tensor_scalar(st[:, 8:9], st[:, 7:8], SUBLN_EPS, None, ALU.add).then_inc(s["mean_square"].sem, 1)

                def sub_norm(n):
                    qt, h = items[n]
                    dve.wait_ge(*s["rms"].at(n + 1))
                    if h == 0 and qt >= 2:
                        dve.wait_ge(*(s["y_stored0"], s["y_stored1"])[qt % 2].at(16 * (qt // 2)))
                    dve.scalar_tensor_tensor(out=y[:, qt % 2, h * dv:(h + 1) * dv], in0=da_o[:, n % 2, :], scalar=att_st[:, n % 4, 9:10],
                                             in1=subln[l][:, :], op0=ALU.mult, op1=ALU.mult).then_inc(s["y"].sem, 1)

                maxima(0)
                for n in range(len(items)):
                    if nmaps == 2:
                        mix(n)
                    if n + 1 < len(items):
                        maxima(n + 1)
                    if nmaps == 2 and n >= 1:
                        sub_norm(n - 1)
                    finish(n)
                if nmaps == 2:
                    sub_norm(len(items) - 1)

            def norm_rows(l, n_q):
                m = ML[l]
                parts = [(k, c, w, t) for t in range(NT) for k, c, w in ((0, 0, Q_RANK), (1, Q_RANK, KV_RANK)) if k or t < n_q]
                for k, c, w, t in parts:
                    if k == 0 or t >= n_q:
                        dve.wait_ge(*m["rows_copied"].at(n_q + t + 1))
                    r = ml_rows[:, t, c:c + w]
                    link(dve.tensor_tensor_reduce(ml_junk[:, 0:w], r, r, 1.0 / w, 0.0, ALU.mult, ALU.add, rms_st[:, k * NT + t:k * NT + t + 1]))
                dve.tensor_scalar(rms_eps[:, :], rms_st[:, :], RMS_EPS, None, ALU.add).then_inc(m["mean_squares"].sem, 1)
                dve.wait_ge(*m["rms"].at(1))
                for k, c, w, t in parts:
                    r = ml_rows[:, t, c:c + w]
                    ins = dve.tensor_scalar(r, r, rms_inv[:, k * NT + t:k * NT + t + 1], None, ALU.mult)
                    if k:
                        ins.then_inc(m["normed"].sem, 1)

            for l in range(DEPTH):
                fence(dve, l, "inA")
                s = IN[l][0]
                for i in range(8):
                    dst = da_q[:, i, 0:SEQ] if i < HEADS else da_k[:, i - HEADS, 0:SEQ]
                    rotate(s, i, 4 + i % 2, P, 0, da_raw, da_t, dst, cos64, sin64)
                    if i % 2:
                        split(in_unit(l, i // 2 + 2))
                for u in range(2):
                    split(in_unit(l, 4 + u + 2))
                end()
                fence(dve, l, "atA")
                attention(l, 0, 2, da_p, da_y, DA_V, None)
                end()

                fence(dve, l, "inB")
                s, m = IN[l][1], ML[l]
                split(in_unit(l, 8))
                norm_rows(l, T_Q[l])
                split(in_unit(l, 9))
                for h in range(HEADS):
                    rotate(s, h, 4 + h % 2, MQ, 0, ml_raw, ml_t, ml_q[:, h, 0:SEQ], cos32, sin32)
                dve.wait_ge(*s["rot"].at(HEADS + 1))
                dve.wait_ge(*s["done"].at(HEADS))
                r = slice(HD, MQ)
                dve.tensor_tensor(ml_t[r, 0, :], ml_kr[r, 0:SEQ], cos32[r, :], ALU.mult)
                link(dve.tensor_tensor(ml_t[r, 1, :], psum[r, 4 * 512:5 * 512], sin32[r, :], ALU.mult))
                dve.tensor_tensor(ml_t[r, 0, :], ml_t[r, 0, :], ml_t[r, 1, :], ALU.add).then_inc(s["done"].sem, 1)
                end()
                fence(dve, l, "atB")
                attention(l, 1, 1, ml_p, ml_y, HD, None)
                end()

                fence(dve, l, "inC")
                for u in (10, 11, 12):
                    split(in_unit(l, u))
                end()
                fence(dve, l, "atC")
                dve.wait_ge(*BIAS[l]["ready"].at(1))
                attention(l, 2, 1, na_p, na_y, HD, na_bias)
                end()

                fence(dve, l, "yT")
                for t in range(T_Q[l]):
                    dve.wait_ge(*YT[l]["hi"].at(t + 1))
                    tk = slice(t * P, (t + 1) * P)
                    dve.tensor_tensor(xt_lo[:, :, tk], bank(2 * (t % 2), D).rearrange("p (k n) -> p k n", n=P),
                                      xt_hi[:, :, tk].bitcast(F32), ALU.subtract).then_inc(YT[l]["lo"].sem, 1)
                end()
                fence(dve, l, "out")
                dve.wait_ge(*LN[l][0]["rows_landed"].at(16 * (4 if T_Q[l] == NT else 3)))
                n = 0
                for u in range(N_OUT):
                    for t in range(T_Q[l]):
                        dve.wait_ge(*OP[l]["product"].at(n + 1))
                        dve.tensor_tensor(acc[:, t, u * UW:(u + 1) * UW], bank(4 + n % 4, UW),
                                          gate_row[:, 0 if t < LT else 1, u * UW:(u + 1) * UW], ALU.mult).then_inc(OP[l]["gated"].sem, 1)
                        n += 1
                    split(in_unit(l, N_IN + u + 2))
                end()

                def ln(w, turn):
                    s = LN[l][w]
                    nl, nw = (l, 1) if w == 0 else (l + 1, 0)

                    def stats(t):
                        st = ln_st[:, t % 2, :]
                        if w == 1:
                            link(dve.tensor_tensor(acc[:, t, :], acc[:, t, :], gate_row[:, 0 if t < LT else 1, :], ALU.mult))
                        dve.wait_ge(*(s["x_loaded0"], s["x_loaded1"])[t % 2].at(16 * (t // 2 + 1)))
                        ins = dve.scalar_tensor_tensor(out=acc[:, t, :], in0=x_in[:, t % 2, :], scalar=ALPHA, in1=acc[:, t, :],
                                                       op0=ALU.mult, op1=ALU.add)
                        ins.then_inc(s["summed"].sem, 1)
                        dve.wait_ge(*s["summed"].at(t + 1))
                        if t >= 2:
                            dve.wait_ge(*s["normed"].at(t - 1))
                        for k in range(2):
                            ins = dve.bn_stats(st[:, 6 * k:6 * k + 6], acc[:, t, k * 512:(k + 1) * 512])
                        link(ins)
                        link(dve.bn_aggr(st[:, 12:14], st[:, 0:12]))
                        dve.tensor_scalar(st[:, 14:15], st[:, 13:14], LN_EPS, None, ALU.add).then_inc(s["variance"].sem, 1)
                        dve.wait_ge(*s["rstd"].at(t + 1))
                        dve.scalar_tensor_tensor(out=st[:, 16:17], in0=st[:, 12:13], scalar=-1.0, in1=st[:, 15:16],
                                                 op0=ALU.mult, op1=ALU.mult).then_inc(s["stats"].sem, 1)

                    stats(0)
                    for t in range(T_Q[l]):
                        if t + 1 < T_Q[l]:
                            stats(t + 1)
                        if turn:
                            modulated(s, t, nl, nw)
                            low(s, t)

                fence(dve, l, "ln0")
                ln(0, True)
                end()

                fence(dve, l, "ffn")
                s = FF[l]
                tokens = T_Q[l] * P
                u0 = in_unit(l, N_IN + N_OUT)
                width = T_Q[l] * D // 4
                flat = arena[:, 0:T_Q[l] * D]
                for k in range(4):
                    dve.memset(flat[:, k * width:(k + 1) * width], 0.0).then_inc(s["bank2_free"].sem, 1)
                dve.drain().then_inc(s["hid_lo"].sem, 2)

                def group(i, more):
                    dve.wait_ge(*s["bank2_free"].at(i * (2 * T_Q[l]) + 4))
                    for a in range(2):
                        for j in (2 * a, 2 * a + 1):
                            dve.wait_ge(*s["bank1_free"].at(i * FG + j + 3))
                            r = relu[:, j % 2, 0:tokens]
                            dve.tensor_tensor(squares[:, j % 2, 0:tokens], r, r, ALU.mult).then_inc(s["squared"].sem, 1)
                            dve.wait_ge(*s["squared"].at(i * FG + j + 1))
                            dve.wait_ge(*s["hid_hi"].at(i * FG + j + 1))
                            dve.tensor_tensor(hid_lo[:, j, 0:tokens], squares[:, j % 2, 0:tokens], hid_hi[:, j, 0:tokens].bitcast(F32),
                                              ALU.subtract).then_inc(s["hid_lo"].sem, 1)
                        split_at(i * FU + (u0 + a + 2), (u0 + a) % 2)
                    for b in range(2):
                        for t in range(T_Q[l]):
                            n = b * T_Q[l] + t
                            dve.wait_ge(*s["product"].at(i * (2 * T_Q[l]) + n + 1))
                            dst = acc[:, t, b * 512:(b + 1) * 512]
                            dve.tensor_tensor(dst, dst, bank(4 + n % 4), ALU.add).then_inc(s["bank2_free"].sem, 1)
                        if more:
                            split_at(i * FU + (u0 + 2 + b + 2), (u0 + b) % 2)

                with dve.Fori(0, GROUPS - 1) as i:
                    group(i, True)
                group(GROUPS - 1, l + 1 < DEPTH)
                end()

                fence(dve, l, "ln1")
                dve.wait_ge(*LN[l][1]["rows_landed"].at(16 * (4 if T_Q[l] == NT else 3)))
                ln(1, l + 1 < DEPTH)
                end()

        @block.tensor
        def _(pe):
            def end():
                pe.drain().then_inc(pe_phase, 1)

            def products(outs, lhs, rhs, start=True, stop=True):
                ks = lhs[0]
                for i, k in enumerate(ks):
                    l_hi, l_lo = lhs[1](k)
                    for n, (a, half) in enumerate(((l_hi, 0), (l_hi, 1), (l_lo, 0))):
                        for c, o in enumerate(outs):
                            ins = pe.matmul(o, a, rhs(k, c)[half], start=start and i == 0 and n == 0,
                                            stop=stop and i == len(ks) - 1 and n == 2)
                return ins

            pe.wait_ge(const_landed, 16 * 8)
            pe.wait_ge(vrow_landed, 16 * 9 * DEPTH)
            for l in range(DEPTH):
                pe.transpose(bank(2 + l, P), vrow[:, l, :], ident[:, :]).then_inc(vec_turned, 1)
            pe.wait_ge(silu_ready, 1)
            for l in range(DEPTH):
                with pe.Fori(0, WMOD_UNITS // MR) as i:
                    for k in range(MR):
                        pe.wait_ge(wm_landed[k], (i + (l * WMOD_UNITS // MR + 1)) * 16)
                        for n in range(2):
                            for kt in range(KT):
                                ins = pe.matmul(psum[:, bass.ds((i * MR + k) * 4 + (l * 512 + 2 * n), 2)], wm_ring[:, k, kt, n * P:(n + 1) * P],
                                                silu[:, :, kt], start=kt == 0, stop=kt == KT - 1)
                        ins.then_inc(wm_used, 1)
            for l in range(DEPTH):
                pe.wait_ge(modv_ready, l + 1)
                pe.transpose(bank(4 + l, P, 96), modv[l][:, :, :].rearrange("p n s -> p (n s)"), ident[:, :]).then_inc(gate_turned, 1)
            end()

            def turn_rows(s, t, src, loaded):
                pe.wait_ge(*loaded)
                if t >= 2:
                    pe.wait_ge(*s["lo"].at(t - 1))
                for k in range(KT):
                    ins = pe.transpose(bank(2 * (t % 2), P, at=k * P), src[:, t % 2, k * P:(k + 1) * P], ident[:, :])
                ins.then_inc(s["turned"].sem, 1)

            fence(pe, 0, "x0")
            for t in range(NT):
                turn_rows(X0, t, x_in, (X0["x_loaded0"], X0["x_loaded1"])[t % 2].at(16 * (t // 2 + 1)))
            end()

            def xt(k, c0, n):
                return xt_hi[:, k, c0:c0 + n], xt_lo[:, k, c0:c0 + n]

            def weights_ready(u):
                pe.wait_ge(w_lo_ready, u + 1)

            def feature_tile(slot, col, l, all_tokens, banks):
                wh, wl = w_view(w_hi, slot), w_view(w_lo, slot)
                ch = chunks(l, all_tokens)
                return products([bank(banks + c, n) for c, (_, n) in enumerate(ch)],
                                (range(KT), lambda k: (wh[:, k, col:col + P], wl[:, k, col:col + P])),
                                lambda k, c: xt(k, *ch[c]))

            def row_tile(slot, t, width, o):
                wh, wl = w_view(w_hi, slot, width), w_view(w_lo, slot, width)
                return products([o], (range(KT), lambda k: xt(k, t * P, P)), lambda k, c: (wh[:, k, :], wl[:, k, :]))

            def attention(l, g, nmaps, q, k, v, p, pt, dv):
                s = AT[l][g]
                items = ITEMS[l]

                def keys(qt):
                    return (0, TOK) if qt < LT else (SEQ, CTX)

                def scores(n):
                    qt, h = items[n]
                    k0, nk = keys(qt)
                    for m in range(nmaps):
                        if nmaps == 2:
                            b = 2 * m
                            if n >= 1:
                                pe.wait_ge(*s["probs"].at(2 * (n - 1) + m + 1))
                        else:
                            b = 2 * (n % 2)
                            if n >= 2:
                                pe.wait_ge(*s["probs"].at(n - 1))
                        for c in range(0, nk, 512):
                            w = min(512, nk - c)
                            ins = pe.matmul(bank(b, w, at=c), q(h, m)[:, qt * P:(qt + 1) * P], k(h, m)[:, k0 + c:k0 + c + w], start=True, stop=True)
                        ins.then_inc(s["scores"].sem, 1)

                scores(0)
                for n, (qt, h) in enumerate(items):
                    k0, nk = keys(qt)
                    if n + 1 < len(items):
                        scores(n + 1)
                    if nmaps == 2:
                        pe.wait_ge(*s["mixed"].at(n + 1))
                    else:
                        pe.wait_ge(*s["probs"].at(n + 1))
                    if n >= 1:
                        pe.wait_ge(*s["turned_copied"].at(n))
                    for c in range(nk // P):
                        ins = pe.transpose(bank(4, P, at=c * P), p[:, n % 2, 0, c * P:(c + 1) * P], ident[:, :])
                    ins.then_inc(s["turned"].sem, 1)
                    pe.wait_ge(*s["turned_copied"].at(n + 1))
                    if n >= 2:
                        pe.wait_ge(*s["mean_square" if nmaps == 2 else "y"].at(n - 1))
                    for c in range(nk // P):
                        ins = pe.matmul(bank(6 + n % 2, dv), pt[:, n % 2, c * P:(c + 1) * P], v[:, k0 // P + c, h * dv:(h + 1) * dv],
                                        start=c == 0, stop=c == nk // P - 1)
                    ins.then_inc(s["mixed_values"].sem, 1)

            for l in range(DEPTH):
                q_ctx = T_Q[l] == NT
                fence(pe, l, "inA")
                s = IN[l][0]

                def rotation(i):
                    pe.wait_ge(*s["raw"].at(i + 1))
                    if i >= 2:
                        pe.wait_ge(*s["done"].at(i - 1))
                    pe.matmul(bank(4 + i % 2), rot64[:, :], da_raw[:, i % 2, :], start=True, stop=True).then_inc(s["rot"].sem, 1)

                for i in range(8):
                    u = in_unit(l, i // 2)
                    if i % 2 == 0:
                        weights_ready(u)
                    if i >= 2:
                        pe.wait_ge(*s["raw"].at(i - 1))
                    feature_tile(u, (i % 2) * P, l, i >= HEADS, 2 * (i % 2)).then_inc(s["tile"].sem, 1)
                    if i >= 1:
                        rotation(i - 1)
                rotation(7)
                for u in range(2):
                    weights_ready(in_unit(l, 4 + u))
                    for t in range(NT):
                        n = u * NT + t
                        if n >= 2:
                            pe.wait_ge(*s["v_copied"].at(n - 1))
                        row_tile(in_unit(l, 4 + u), t, UW, bank(6 + t % 2, UW)).then_inc(s["v"].sem, 1)
                end()
                fence(pe, l, "atA")
                attention(l, 0, 2, lambda h, m: da_q[m * HD:(m + 1) * HD, h, :], lambda h, m: da_k[m * HD:(m + 1) * HD, h, :],
                          da_v, da_p, da_pt, DA_V)
                end()

                fence(pe, l, "inB")
                s, m = IN[l][1], ML[l]
                n = 0
                for u, tiles, w in ((6, T_Q[l], Q_RANK), (7, NT, KV_RANK + ROPE)):
                    weights_ready(in_unit(l, u))
                    for t in range(tiles):
                        if n >= 4:
                            pe.wait_ge(*m["rows_copied"].at(n - 3))
                        row_tile(in_unit(l, u), t, w, bank(n % 4, w)).then_inc(s["v"].sem, 1)
                        n += 1
                for t in range(NT):
                    pe.wait_ge(*m["normed"].at(t + 1))
                    if t >= 2:
                        pe.wait_ge(*m["evacuated"].at(t - 1))
                    b = 4 + t % 2
                    if t < T_Q[l]:
                        for k in range(2):
                            pe.transpose(bank(b, P, at=k * P), ml_rows[:, t, k * P:(k + 1) * P], ident[:, :])
                    pe.transpose(bank(b, P, at=2 * P), ml_rows[:, t, Q_RANK:Q_RANK + KV_RANK], ident[:, :])
                    pe.transpose(bank(b, P, MQ, at=3 * P), ml_rows[:, t, Q_RANK + KV_RANK - HD:Q_RANK + KV_RANK + ROPE], ident[:, :]).then_inc(m["turned"].sem, 1)
                pe.wait_ge(*m["weights"].at(32))
                pe.wait_ge(*m["evacuated"].at(NT))
                pe.wait_ge(*m["rows_copied"].at(T_Q[l] + NT))

                def rotation_q(h):
                    pe.wait_ge(*s["raw"].at(h + 1))
                    if h >= 2:
                        pe.wait_ge(*s["done"].at(h - 1))
                    pe.matmul(bank(4 + h % 2, parts=MQ), rot32[:, :], ml_raw[0:MQ, h % 2, :], start=True, stop=True).then_inc(s["rot"].sem, 1)

                for h in range(HEADS):
                    if h >= 2:
                        pe.wait_ge(*s["raw"].at(h - 1))
                    for k in range(2):
                        for c, (c0, w) in enumerate(chunks(l)):
                            ins = pe.matmul(bank(2 * (h % 2) + c, w, MQ), ml_wq[:, k, h * MQ:(h + 1) * MQ], ml_cq[:, k, c0:c0 + w], start=k == 0, stop=k == 1)
                    ins.then_inc(s["tile"].sem, 1)
                    if h >= 1:
                        rotation_q(h - 1)
                rotation_q(HEADS - 1)
                for h in range(HEADS):
                    if h < 2:
                        pe.wait_ge(*s["raw"].at(HEADS - 1 + h))
                    else:
                        pe.wait_ge(*m["up"].at(h - 1))
                    for c, (c0, w) in enumerate(chunks(l, True)):
                        ins = pe.matmul(bank(2 * (h % 2) + c, w, HD), ml_wkv[:, h * P:h * P + HD], ml_ckv[:, c0:c0 + w], start=True, stop=True)
                    ins.then_inc(s["tile"].sem, 1)
                pe.wait_ge(*s["done"].at(HEADS))
                pe.matmul(psum[HD:MQ, 4 * 512:5 * 512], rot32[HD:MQ, HD:MQ], ml_kr[HD:MQ, 0:SEQ], start=True, stop=True).then_inc(s["rot"].sem, 1)
                wv = ml_wkv[:, :].rearrange("p (h n) -> p h n", n=P)[:, :, HD:P]
                for t in range(NT):
                    if t >= 2:
                        pe.wait_ge(*m["v_copied"].at(t - 1))
                    pe.matmul(bank(6 + t % 2, 256), ml_ckv[:, t * P:(t + 1) * P], wv, start=True, stop=True).then_inc(m["v_ready"].sem, 1)
                end()
                fence(pe, l, "atB")
                attention(l, 1, 1, lambda h, m: ml_q[:, h, :], lambda h, m: ml_k[:, h, :], ml_v, ml_p, ml_pt, HD)
                end()

                fence(pe, l, "inC")
                s = IN[l][2]
                for i in range(4):
                    u = in_unit(l, 8 + i // 2)
                    if i % 2 == 0:
                        weights_ready(u)
                    if i >= 2:
                        pe.wait_ge(*s["done"].at(i - 1))
                    feature_tile(u, (i % 2) * P, l, i >= 2, 2 * (i % 2)).then_inc(s["tile"].sem, 1)
                weights_ready(in_unit(l, 10))
                for t in range(NT):
                    if t >= 2:
                        pe.wait_ge(*s["v_copied"].at(t - 1))
                    row_tile(in_unit(l, 10), t, UW, bank(6 + t % 2, UW)).then_inc(s["v"].sem, 1)
                end()
                fence(pe, l, "atC")
                attention(l, 2, 1, lambda h, m: na_q[(h % 2) * HD:(h % 2 + 1) * HD, h // 2, :],
                          lambda h, m: na_k[(h % 2) * HD:(h % 2 + 1) * HD, h // 2, :], na_v, na_p, na_pt, HD)
                end()

                fence(pe, l, "yT")
                for t in range(T_Q[l]):
                    turn_rows(YT[l], t, x_in, (YT[l]["loaded0"], YT[l]["loaded1"])[t % 2].at(16 * (t // 2 + 1)))
                end()

                fence(pe, l, "out")
                n = 0
                for u in range(N_OUT):
                    g = in_unit(l, N_IN + u)
                    weights_ready(g)
                    for t in range(T_Q[l]):
                        if n >= 4:
                            pe.wait_ge(*OP[l]["gated"].at(n - 3))
                        row_tile(g, t, UW, bank(4 + n % 4, UW)).then_inc(OP[l]["product"].sem, 1)
                        n += 1
                end()
                fence(pe, l, "ln0")
                for t in range(T_Q[l]):
                    turn_rows(LN[l][0], t, x_n, LN[l][0]["normed"].at(t + 1))
                end()

                fence(pe, l, "ffn")
                s = FF[l]
                u0 = in_unit(l, N_IN + N_OUT)
                with pe.Fori(0, GROUPS) as i:
                    for a in range(2):
                        pe.wait_ge(w_lo_ready, i * FU + (u0 + a + 1))
                        for j in (2 * a, 2 * a + 1):
                            pe.wait_ge(*s["bank1_free"].at(i * FG + j + 1))
                            feature_tile(u0 + a, (j % 2) * P, l, False, 2 * (j % 2)).then_inc(s["hidden"].sem, 1)
                    for b in range(2):
                        pe.wait_ge(w_lo_ready, i * FU + (u0 + 2 + b + 1))
                        wh, wl = w_view_ff2(w_hi, u0 + b), w_view_ff2(w_lo, u0 + b)
                        for t in range(T_Q[l]):
                            n = b * T_Q[l] + t
                            pe.wait_ge(*s["bank2_free"].at(i * (2 * T_Q[l]) + n + 1))
                            for j in range(FG):
                                if n == 0:
                                    pe.wait_ge(*s["hid_lo"].at(i * FG + j + 3))
                                tk = slice(t * P, (t + 1) * P)
                                ins = products([bank(4 + n % 4)], ([j], lambda k: (hid_hi[:, k, tk], hid_lo[:, k, tk])),
                                               lambda k, c: (wh[:, k, :], wl[:, k, :]), start=j == 0, stop=j == FG - 1)
                            ins.then_inc(s["product"].sem, 1)
                end()
                fence(pe, l, "ln1")
                if l + 1 < DEPTH:
                    for t in range(T_Q[l]):
                        turn_rows(LN[l][1], t, x_n, LN[l][1]["normed"].at(t + 1))
                end()


_NAMES = ["x", "c", "ctx", "c_ctx", "w_mod", "b_mod", "w_in", "da_lam_q1", "da_lam_k1", "da_lam_q2", "da_lam_k2",
          "da_subln_g", "mla_q_norm_g", "mla_w_uq", "mla_kv_norm_g", "mla_w_ukv", "na_rpb", "w_out",
          "ln1_g", "ln1_b", "w_ff1", "w_ff2", "ln2_g", "ln2_b"]


def kernel(**inputs):
    import concourse.bacc as _bacc
    from concourse.bass_utils import run_bass_kernel_spmd as _run

    nc = _bacc.Bacc("TRN2", target_bir_lowering=False, num_devices=1)
    arrays, aps = {}, {}
    given = {n: np.ascontiguousarray(inputs[n]) for n in _NAMES}
    given.update(shape_constants())
    for name, a in given.items():
        arrays[f"in_{name}"] = a
        aps[name] = nc.dram_tensor(f"in_{name}", a.shape, mybir.dt.from_np(a.dtype), kind="ExternalInput").ap()
    out = nc.dram_tensor("out_x", (1, SEQ, D), F32, kind="ExternalOutput").ap()
    build(nc, aps, out)
    r = _run(nc, [arrays], core_ids=[0])
    return r.results[0]["out_x"]
```

```python
from contextlib import ExitStack

import numpy as np

import concourse.bass as bass
from concourse import mybir

P = 128
F32 = mybir.dt.float32
F32R = mybir.dt.float32r
ALU = mybir.AluOpType
ACT = mybir.ActivationFunctionType
AX = mybir.AxisListType

D = 1024
DEPTH = 2
GRID_W = 64
SEQ = 512
CTX = 256
ROWS = SEQ // GRID_W
TOK = SEQ + CTX
LT = SEQ // P
NT = TOK // P
KT = D // P
HEADS = 4
HD = 64
DA_V = 2 * HD
ROPE = 32
MQ = HD + ROPE
Q_RANK, KV_RANK = D // 4, D // 8
NA_KH, NA_KW = 8, 16
D_FF = 4 * D
IN_WIDTH = 2720
COL_CQ = 1536
COL_CKV = COL_CQ + Q_RANK
COL_NQ = COL_CKV + KV_RANK + ROPE
ALPHA = (2.0 * DEPTH) ** 0.25
LN_EPS = 1e-6
RMS_EPS = 1e-6
SUBLN_EPS = 1e-5
LAM_INIT = [float(0.8 - 0.6 * np.exp(-0.3 * l)) for l in range(DEPTH)]
MASKED = -1.0e30

UW = 256
UC = KT * UW
IN_UNITS = [(c, min(UW, lim - c)) for lo, lim in ((0, COL_CQ), (COL_CQ, COL_CKV), (COL_CKV, COL_NQ),
                                                  (COL_NQ, IN_WIDTH)) for c in range(lo, lim, UW)]
N_IN = len(IN_UNITS)
N_OUT = D // UW
FG = 4
GF = FG * P
GROUPS = D_FF // GF
FU = 4
N_UNITS = N_IN + N_OUT + GROUPS * FU
WMOD_UNITS = 6 * D // UW
MR = 3
WM_FIRST = 2 * D // UW

V_BMOD, V_G1, V_B1, V_G2, V_B2, V_QN, V_KN, V_C, V_CC, V_ROWS = 0, 48, 56, 64, 72, 80, 82, 83, 91, 99
SHIFT1, SCALE1, GATE1, SHIFT2, SCALE2, GATE2 = (8 * i for i in range(6))
SKEW = 64 * 129


def shape_constants():
    def inv(n):
        return (np.float32(10000.0) ** (np.float32(-2.0) * np.arange(n // 2, dtype=np.float32) / np.float32(n))).astype(np.float32)
    tok = np.arange(SEQ)
    row, col = (tok // GRID_W).astype(np.float32), (tok % GRID_W).astype(np.float32)

    def tables(width, parts):
        n = width // 2
        cos = np.ones((parts, SEQ), np.float32)
        sin = np.zeros((parts, SEQ), np.float32)
        rot = np.zeros((parts, parts), np.float32)
        first = 0 if width == HD else HD
        for d in range(first, parts):
            e = (d - first) % width
            pos = row if e < n else col
            ang = (pos * inv(n)[e % n % (n // 2)]).astype(np.float32)
            cos[d] = np.cos(ang)
            sin[d] = np.sin(ang)
            if e % n < n // 2:
                rot[d + n // 2, d] = -1.0
            else:
                rot[d - n // 2, d] = 1.0
        return cos, sin, rot

    c64, s64, r64 = tables(HD, P)
    c32, s32, r32 = tables(ROPE, MQ)
    q = np.arange(P) % GRID_W
    start = np.clip(q - NA_KW // 2, 0, GRID_W - NA_KW)
    k = np.arange(GRID_W)[None, :]
    inside = (k >= start[:, None]) & (k < start[:, None] + NA_KW)
    mask = np.where(inside, np.float32(0), np.float32(MASKED)).astype(np.float32)
    return {"k_cos64": c64, "k_sin64": s64, "k_rot64": r64, "k_cos32": c32, "k_sin32": s32,
            "k_rot32": r32, "k_mask": mask, "k_ident": np.eye(P, dtype=np.float32)}


def build(nc, A, out):
    ctx = ExitStack()
    with ctx:
        def sb(name, shape, dt=F32):
            return ctx.enter_context(nc.sbuf_tensor(name, shape, dt))

        def sem(name):
            return ctx.enter_context(nc.semaphore(name))

        xt_hi = sb("xt_hi", [P, KT, TOK], F32R)
        xt_lo = sb("xt_lo", [P, KT, TOK], F32R)
        w_raw = sb("w_raw", [P, 2, UC])
        w_hi = sb("w_hi", [P, 2, UC], F32R)
        w_lo = sb("w_lo", [P, 2, UC], F32R)
        hid_hi = sb("hid_hi", [P, FG, TOK], F32R)
        hid_lo = sb("hid_lo", [P, FG, TOK], F32R)
        arena = sb("arena", [P, 20480])
        rot64, rot32 = sb("rot64", [P, P]), sb("rot32", [MQ, MQ])
        ident = sb("ident", [P, P])
        mod_rows = sb("mod_rows", [96, P])
        mask = sb("mask", [P, GRID_W])
        vec = [sb(f"vec{l}", [P, V_ROWS]) for l in range(DEPTH)]
        modv = [sb(f"modv{l}", [P, 48, 2]) for l in range(DEPTH)]
        mod_a = [[sb(f"mod_a{l}{w}", [P, KT, 2]) for w in range(2)] for l in range(DEPTH)]
        mod_b = [[sb(f"mod_b{l}{w}", [P, KT, 2]) for w in range(2)] for l in range(DEPTH)]
        silu = sb("silu", [P, 2, KT])
        silu_tmp = sb("silu_tmp", [P, 2, KT])
        neg_lam = [sb(f"neg_lam{l}", [P, 1]) for l in range(DEPTH)]
        lam_tmp = sb("lam_tmp", [P, 4])
        subln = [sb(f"subln{l}", [P, DA_V]) for l in range(DEPTH)]
        att_st = sb("att_st", [P, 6, 12])
        ln_st = sb("ln_st", [P, NT, 17])
        rms_st = sb("rms_st", [P, 2 * NT])
        rms_eps = sb("rms_eps", [P, 2 * NT])
        rms_inv = sb("rms_inv", [P, 2 * NT])
        neg_half = sb("neg_half", [P, 2 * NT])

        def ar(c, *dims, parts=P):
            n = int(np.prod(dims))
            v = arena[0:parts, c:c + n]
            if len(dims) == 2:
                v = v.rearrange("p (a b) -> p a b", b=dims[1])
            if len(dims) == 3:
                v = v.rearrange("p (a b c) -> p a b c", b=dims[1], c=dims[2])
            return v

        x_first, h32_first = ar(0, NT, D), ar(10240, 2, D)
        vrow, lamv, pad, lam_junk = ar(6144, DEPTH, P), ar(6400, 4 * DEPTH, HD), ar(6912, DEPTH, P), ar(7168, HD)
        wm_rings = [ar(12288, MR, KT, UW), ar(3584, MR, KT, UW)]
        mod_row = [[ar(c, D, parts=2) for c in cs] for cs in ((18432, 19456), (9728, 19456))]
        da_q, da_k, da_v = ar(0, HEADS, TOK), ar(3072, HEADS, TOK), ar(6144, NT, HEADS * DA_V)
        da_raw, da_t = ar(9216, 2, SEQ), ar(10240, 2, SEQ)
        cos64, sin64 = ar(11264, SEQ), ar(11776, SEQ)
        da_p, da_pt, da_y = ar(9216, 2, 2, TOK), ar(12288, 2, TOK), ar(13824, 2, 512)
        da_o, da_junk = ar(14848, 2, 128), ar(15104, 128)
        ml_q, ml_k, ml_v = ar(0, HEADS, TOK, parts=MQ), ar(3072, HEADS, TOK, parts=MQ), ar(6144, NT, 256)
        ml_rows = ar(15232, NT, Q_RANK + KV_RANK + ROPE)
        ml_cq, ml_ckv, ml_kr = ar(7680, 2, TOK), ar(9216, TOK), ar(9984, TOK)
        ml_wq, ml_wkv = ar(10752, 2, HEADS * MQ), ar(11520, 512)
        ml_raw, ml_t, ml_junk = ar(12032, 2, SEQ), ar(13056, 2, SEQ), ar(14080, Q_RANK)
        cos32, sin32 = ar(17728, SEQ, parts=MQ), ar(18240, SEQ, parts=MQ)
        ml_p, ml_pt, ml_y = ar(7680, 2, 1, TOK), ar(9216, 2, TOK), ar(10752, 2, 256)
        na_bias = ar(11264, HEADS, 14 * GRID_W)
        na_q, na_k, na_v = ar(14848, 2, TOK), ar(16384, 2, TOK), ar(17920, NT, 256)
        na_p, na_pt, na_y = ar(0, 2, 1, TOK), ar(1536, 2, TOK), ar(3072, 2, 256)
        acc, x_res = ar(0, NT, D), ar(6144, NT, D)
        y_in = h32 = ar(12288, 2, D)
        relu, squares = ar(12288, 2, TOK), ar(18432, 2, TOK)
        gain_row = ar(14336, 2, D)
        gate_row = ar(16384, 2, D)

        psum = ctx.enter_context(nc.psum_tensor("psum", [P, 8 * 512], F32))

        def bank(b, n=512, parts=P, at=0):
            return psum[0:parts, b * 512 + at:b * 512 + at + n]

        y_dram = nc.dram_tensor("y_scratch", [NT, P, D], F32).ap()
        x_dram = nc.dram_tensor("x_scratch", [NT, P, D], F32).ap()
        mod_dram = nc.dram_tensor("mod_scratch", [DEPTH, 2, 6 * D], F32).ap()
        skew_dram = nc.dram_tensor("skew_scratch", [DEPTH, HEADS * 15, SKEW], F32).ap()

        pe_phase, act_phase, dve_phase, pool_phase = (sem(n) for n in ("pe_phase", "act_phase", "dve_phase", "pool_phase"))
        raw_landed = [sem("raw_landed0"), sem("raw_landed1")]
        w_hi_ready, w_lo_ready = sem("w_hi_ready"), sem("w_lo_ready")
        const_landed, ident_landed, lamv_landed, pad_landed = (sem(n) for n in ("const_landed", "ident_landed", "lamv_landed", "pad_landed"))
        vrow_landed = [sem("vrow_landed0"), sem("vrow_landed1")]
        wm_landed = [sem(f"wm_landed{i}") for i in range(MR)]
        wm_used = sem("wm_used")
        pad_zeroed, skew_written = sem("pad_zeroed"), sem("skew_written")
        b_landed, row_added, mod_stored = [sem("b_landed0"), sem("b_landed1")], sem("row_added"), sem("mod_stored")
        vec_turned, silu_exp, silu_ready, vec_ready = sem("vec_turned"), sem("silu_exp"), sem("silu_ready"), sem("vec_ready")
        modv_ready, mod_rows_landed, mod_turned = sem("modv_ready"), sem("mod_rows_landed"), sem("mod_turned")
        lam_dot, lam_exp = sem("lam_dot"), sem("lam_exp")
        dve_step = sem("dve_step")
        act_step = sem("act_step")
        pool_step = sem("pool_step")

        T_Q = [NT if l < DEPTH - 1 else LT for l in range(DEPTH)]

        class Signal:
            def __init__(self, sem, base):
                self.sem, self.base = sem, base

            def at(self, n):
                return self.sem, self.base + n

        semaphores, counted = {}, {}

        def signals(family, **increments):
            of = {}
            for name, n in increments.items():
                key = f"{family}_{name}"
                if key not in semaphores:
                    semaphores[key], counted[key] = sem(key), 0
                of[name] = Signal(semaphores[key], counted[key])
                counted[key] += n
            return of

        def halves(T):
            return 16 * ((T + 1) // 2), 16 * (T // 2)

        def ln_signals(l, w, turned):
            T, final = T_Q[l], l == DEPTH - 1 and w == 1
            n = T if turned else 0
            res = T if l or w else 0
            return signals("ln", loaded=16 * T * (1 - w), gain_landed=64 if final else 32 if res else 0, res_gained=res, res_ready=res,
                           variance=T, rstd=T, stats=T, normed=T, turned=n, h_act=n, h_dve=n, hi=n, lo=n,
                           gate_landed=16 * (2 if T == NT else 1), stored=16 * T * w, out_gained=T * final, out_ready=T * final)

        X0 = signals("ln", turned=NT, h_act=NT, h_dve=NT, hi=NT, lo=NT)
        x_first_landed = sem("x_first_landed")
        ML_PARTS = {T: [("rows", 6, t) for t in range(T)] + [("rows", 7, t) for t in range(NT)] for T in set(T_Q)}
        NA_PARTS = {T: [("features", u, i, c, n) for u in (8, 9) for i in range(2) for c, n in ((0, SEQ), (SEQ, CTX))
                        if u == 9 or c == 0 or T == NT] + [("rows", 10, t) for t in range(NT)] for T in set(T_Q)}

        VU = D // UW
        def wmod_bank(n):
            return 7 if n >= WMOD_UNITS else 6 + n % 2

        MOD_COLUMNS = [(0, 0, 16), (0, 16, 48), (1, 0, 48)]

        def halves_beside(parts, items, n):
            h = 2 * len(parts)
            return range(n * h // items, (n + 1) * h // items)

        IN, ML, AT, YT, OP, LN, FF, BIAS = [], [], [], [], [], [], [], []
        for T in T_Q:
            a, b = halves(T)
            IN.append([signals("in", tile=8, raw=8, rot=8, done=8, v=2 * NT, v_copied=2 * NT, tables=32, part=0, part_copied=0),
                       signals("in", tile=2 * HEADS, raw=HEADS, rot=HEADS + 1, done=HEADS + 1, v=0, v_copied=0, tables=32, part=T + NT, part_copied=T + NT),
                       signals("in", part=len(NA_PARTS[T]), part_copied=len(NA_PARTS[T]))])
            ML.append(signals("ml", mean_squares=1, rms=1, normed=NT, turned=NT, evacuated=NT, up=HEADS, weights=32, v_ready=NT, v_copied=NT))
            n = HEADS * T
            AT.append([signals("at", scores=k * n, negmax=k * n, probs=k * n, mixed=(k - 1) * n, mean_square=(k - 1) * n, rms=(k - 1) * n, turned=n, turned_copied=n,
                               mixed_values=n, y=n, y_stored0=a, y_stored1=b) for k in (2, 1, 1)])
            BIAS.append(signals("bias", landed=16 * 2 * HEADS, ready=1))
            YT.append(signals("yt", loaded0=a, loaded1=b, turned=T, hi=T, lo=T))
            OP.append(signals("op", product=N_OUT * T, gated=N_OUT * T))
            LN.append([ln_signals(len(LN), 0, True), ln_signals(len(LN), 1, len(LN) + 1 < DEPTH)])
            FF.append(signals("ff", hidden=GROUPS * FG, bank1_free=2 + GROUPS * FG, hid_hi=GROUPS * FG, hid_lo=2 + GROUPS * FG, squared=GROUPS * FG,
                              product=GROUPS * 2 * T, bank2_free=4 + GROUPS * 2 * T))

        def chunks(l, all_tokens=False):
            return [(0, SEQ), (SEQ, CTX)] if all_tokens or T_Q[l] == NT else [(0, SEQ)]

        phases = {}
        for l in range(DEPTH):
            for name in (["setup"] if l == 0 else []) + ["inA", "atA", "inB", "atB", "atC", "yT", "out", "ffn"]:
                phases[(l, name)] = len(phases)

        def fence(eng, l, name):
            n = phases[(l, name)]
            if n:
                for s in (pe_phase, act_phase, dve_phase, pool_phase):
                    eng.wait_ge(s, n)

        def in_unit(l, u):
            return l * N_UNITS + u

        def w_view(t, u, cols=UW):
            return t[:, u % 2, 0:KT * cols].rearrange("p (k n) -> p k n", n=cols)

        def w_view_ff2(t, u):
            return t[:, u % 2, :].rearrange("p (k n) -> p k n", n=512)

        ITEMS = [[(qt, h) for qt in range(T_Q[l]) for h in range(HEADS)] for l in range(DEPTH)]

        block = ctx.enter_context(nc.Block())

        @block.sync
        def _(sp):
            def load(u, dst, src):
                if not isinstance(u, int) or u >= 2:
                    sp.wait_ge(w_lo_ready, u - 1)
                return sp.dma_start(dst, src)

            def projection(l, u):
                g = in_unit(l, u)
                if u < N_IN:
                    c, n = IN_UNITS[u]
                    src = A["w_in"][l, :, c:c + n]
                else:
                    c, n = (u - N_IN) * UW, UW
                    src = A["w_out"][l, :, c:c + n]
                load(g, w_view(w_raw, g, n), src.rearrange("(k p) n -> p k n", p=P)).then_inc(raw_landed[g % 2], 16)

            def b_row(v):
                l, m = v // 6, v % 6
                if v >= 2:
                    sp.wait_ge(mod_stored, 16 * (v - 1))
                sp.dma_start(mod_row[l][v % 2], A["b_mod"][l, m * D:(m + 1) * D].partition_broadcast(2)).then_inc(b_landed[v % 2], 16)

            def store_row(v):
                l, m = v // 6, v % 6
                sp.wait_ge(row_added, VU * (v + 1))
                if v:
                    sp.wait_ge(mod_stored, 16 * v)
                sp.dma_start(mod_dram[l][:, m * D:(m + 1) * D], mod_row[l][v % 2]).then_inc(mod_stored, 16)

            def wmod(n):
                l, m = n // WMOD_UNITS, n % WMOD_UNITS
                if n % VU == 0 and m >= 2 * VU:
                    b_row(n // VU)
                if n % VU == VU - 1 and m >= 2 * VU - 1 and n != WM_FIRST + VU - 1:
                    store_row(n // VU - 1)
                if n >= MR:
                    sp.wait_ge(wm_used, n - MR + 1)
                sp.dma_start(wm_rings[l][:, n % MR, :, :], A["w_mod"][l, :, m * UW:(m + 1) * UW].rearrange("(k p) n -> p k n", p=P))\
                    .then_inc(wm_landed[n % MR], 16)

            b_row(0)
            b_row(1)
            for n in range(MR):
                wmod(n)
            projection(0, 0)
            projection(0, 1)
            for n in range(MR, WM_FIRST):
                wmod(n)
            store_row(1)
            projection(0, 2)
            projection(0, 3)
            for n in range(WM_FIRST, WM_FIRST + MR):
                wmod(n)
            for i in range(8):
                wmod(WM_FIRST + MR + i)
                if i % 2:
                    projection(0, 4 + i // 2)
            for i in range(WM_FIRST + MR + 8, WMOD_UNITS):
                wmod(i)
            store_row(5)
            for l in range(DEPTH):
                for u in range(8 if l == 0 else 0, N_IN):
                    projection(l, u)
                projection(l, N_IN)
                projection(l, N_IN + 1)
                if l == 0:
                    fence(sp, 0, "atC")
                    b_row(6)
                    b_row(7)
                    for n in range(WMOD_UNITS, 2 * WMOD_UNITS):
                        wmod(n)
                    store_row(11)
                for u in range(N_IN + 2, N_IN + N_OUT):
                    projection(l, u)
                u0 = in_unit(l, N_IN + N_OUT)
                with sp.Fori(0, GROUPS) as i:
                    for k in range(FU):
                        s = (u0 + k) % 2
                        if k < 2:
                            src = A["w_ff1"][l, :, bass.ds(i * GF + k * UW, UW)].rearrange("(k p) n -> p k n", p=P)
                            dst = w_view(w_raw, s)
                        else:
                            src = A["w_ff2"][l, bass.ds(i * GF, GF), (k - 2) * 512:(k - 1) * 512].rearrange("(k p) n -> p k n", p=P)
                            dst = w_view_ff2(w_raw, s)
                        load(i * FU + (u0 + k), dst, src).then_inc(raw_landed[s], 16)

        @block.gpsimd
        def _(pool):
            def end():
                pool.drain().then_inc(pool_phase, 1)

            pool.memset(pad[:, :, :], 0.0).then_inc(pad_zeroed, 1)
            pool.memset(neg_half[:, :], -0.5).then_inc(pad_zeroed, 1)

            def vec_rows(eng, l):
                for r, src in ((V_C, A["c"][0]), (V_CC, A["c_ctx"]), (V_BMOD, A["b_mod"][l]), (V_G1, A["ln1_g"][l]), (V_B1, A["ln1_b"][l]),
                               (V_G2, A["ln2_g"][l]), (V_B2, A["ln2_b"][l]), (V_QN, A["mla_q_norm_g"][l]), (V_KN, A["mla_kv_norm_g"][l])):
                    n = src.shape[0] // P
                    eng.dma_start(vrow[r:r + n, l, :], src.rearrange("(a p) -> a p", p=P)).then_inc(vrow_landed[l], 16)

            vec_rows(pool, 1)
            for t, name in ((rot64, "k_rot64"), (rot32, "k_rot32"), (mask, "k_mask")):
                pool.dma_start(t[:, :], A[name]).then_inc(const_landed, 16)
            pool.wait_ge(pad_zeroed, 2)
            for l in range(DEPTH):
                for i, name in enumerate(("da_lam_q1", "da_lam_k1", "da_lam_q2", "da_lam_k2")):
                    pool.dma_start(lamv[:, 4 * l + i, :], A[name][l].partition_broadcast(P)).then_inc(lamv_landed, 16)
                pool.dma_start(subln[l][:, :], A["da_subln_g"][l].partition_broadcast(P)).then_inc(lamv_landed, 16)
                pool.dma_start(pad[0:HEADS * 15, l, 48:79], A["na_rpb"][l].rearrange("h y x -> (h y) x")).then_inc(pad_landed, 16)
            pool.wait_ge(pad_landed, 16 * DEPTH)
            for l in range(DEPTH):
                dst = skew_dram[l].rearrange("r (q x) -> r q x", x=129)[:, :, 0:P]
                src = pad[0:HEADS * 15, l, :].unsqueeze(1).broadcast_to([HEADS * 15, GRID_W, P])
                pool.dma_start(dst, src).then_inc(skew_written, 16)
            pool.wait_ge(skew_written, 16 * DEPTH)

            def load_mod_rows(i):
                l, first, last = MOD_COLUMNS[i]
                pool.wait_ge(mod_stored, 16 * (6 * l + last // KT))
                for strm in range(2):
                    pool.dma_start(mod_rows[strm * (last - first):(strm + 1) * (last - first), :],
                                   mod_dram[l, strm, first * P:last * P].rearrange("(n p) -> n p", p=P)).then_inc(mod_rows_landed, 16)

            load_mod_rows(0)
            end()

            def store_y(l, g, off, width, y):
                s = AT[l][g]
                for qt in range(T_Q[l]):
                    if g == 0:
                        for n in range(HEADS * qt, HEADS * (qt + 1)):
                            st = att_st[:, n % 6, :]
                            pool.wait_ge(*s["mean_square"].at(n + 1))
                            pool.tensor_tensor(st[:, 9:10], st[:, 8:9], neg_half[:, 0:1], ALU.pow).then_inc(s["rms"].sem, 1)
                    pool.wait_ge(*s["y"].at(HEADS * (qt + 1)))
                    pool.dma_start(y_dram[qt][:, off:off + width], y[:, qt % 2, :]).then_inc((s["y_stored0"], s["y_stored1"])[qt % 2].sem, 16)
                for i, q in enumerate((s["y_stored0"], s["y_stored1"])):
                    pool.wait_ge(*q.at(16 * len(range(i, T_Q[l], 2))))

            def gain_rows(s, l, w):
                pool.dma_start(gain_row[:, 0, :], A["ln1_g" if w == 0 else "ln2_g"][l].partition_broadcast(P)).then_inc(s["gain_landed"].sem, 16)
                pool.dma_start(gain_row[:, 1, :], A["ln1_b" if w == 0 else "ln2_b"][l].partition_broadcast(P)).then_inc(s["gain_landed"].sem, 16)

            def gate_rows(s, l, w):
                gate = GATE1 if w == 0 else GATE2
                for strm in range(2 if T_Q[l] == NT else 1):
                    pool.dma_start(gate_row[:, strm, :],
                                   mod_dram[l, strm, gate * P:gate * P + D].partition_broadcast(P)).then_inc(s["gate_landed"].sem, 16)

            def residual(s, t, src):
                pool.tensor_tensor(x_res[:, t, :], src[:, t, :], gain_row[:, 0, :], ALU.mult).then_inc(s["res_gained"].sem, 1)
                pool.wait_ge(*s["res_gained"].at(t + 1))
                pool.tensor_tensor(x_res[:, t, :], x_res[:, t, :], gain_row[:, 1, :], ALU.add).then_inc(s["res_ready"].sem, 1)

            def spreads(s, l):
                for t in range(T_Q[l]):
                    st = ln_st[:, t, :]
                    pool.wait_ge(*s["variance"].at(t + 1))
                    pool.tensor_tensor(st[:, 15:16], st[:, 14:15], neg_half[:, 0:1], ALU.pow).then_inc(s["rstd"].sem, 1)
                    pool.wait_ge(*s["rstd"].at(t + 1))
                    pool.tensor_tensor(st[:, 16:17], st[:, 12:13], st[:, 15:16], ALU.mult).then_inc(s["stats"].sem, 1)

            for l in range(DEPTH):
                fence(pool, l, "inA")
                pool.dma_start(cos64, A["k_cos64"]).then_inc(IN[l][0]["tables"].sem, 16)
                pool.dma_start(sin64, A["k_sin64"]).then_inc(IN[l][0]["tables"].sem, 16)
                end()
                fence(pool, l, "atA")
                store_y(l, 0, 0, 512, da_y)
                end()
                fence(pool, l, "inB")
                if l == 0:
                    load_mod_rows(1)
                pool.dma_start(ml_wq[:, :, :], A["mla_w_uq"][l].rearrange("(k p) n -> p k n", p=P)).then_inc(ML[l]["weights"].sem, 16)
                pool.dma_start(ml_wkv[:, :], A["mla_w_ukv"][l]).then_inc(ML[l]["weights"].sem, 16)
                pool.dma_start(cos32, A["k_cos32"]).then_inc(IN[l][1]["tables"].sem, 16)
                pool.dma_start(sin32, A["k_sin32"]).then_inc(IN[l][1]["tables"].sem, 16)
                pool.wait_ge(*ML[l]["mean_squares"].at(1))
                pool.tensor_tensor(rms_inv[:, :], rms_eps[:, :], neg_half[:, :], ALU.pow).then_inc(ML[l]["rms"].sem, 1)
                end()
                fence(pool, l, "atB")
                for rr in range(2):
                    for h in range(HEADS):
                        r = h * 15 + 1 - rr
                        src = skew_dram[l, r:r + 14, 63:63 + GRID_W * P].rearrange("j (q k) -> q j k", k=P)[:, :, 0:GRID_W]
                        dst = na_bias[rr * GRID_W:(rr + 1) * GRID_W, h, :].rearrange("p (j k) -> p j k", k=GRID_W)
                        pool.dma_start(dst, src).then_inc(BIAS[l]["landed"].sem, 16)
                pool.wait_ge(*BIAS[l]["landed"].at(16 * 2 * HEADS))
                b3 = na_bias[:, :, :].rearrange("p h (j k) -> p (h j) k", k=GRID_W)
                pool.tensor_tensor(b3, b3, mask[:, :].unsqueeze(1).broadcast_to([P, HEADS * 14, GRID_W]), ALU.add).then_inc(BIAS[l]["ready"].sem, 1)
                store_y(l, 1, 512, 256, ml_y)
                end()
                fence(pool, l, "atC")
                store_y(l, 2, 768, 256, na_y)
                end()
                fence(pool, l, "yT")
                s = LN[l][0]
                if l == 0:
                    load_mod_rows(2)
                for t in range(T_Q[l]):
                    if t >= 2:
                        pool.wait_ge(*YT[l]["turned"].at(t - 1))
                    pool.dma_start(y_in[:, t % 2, :], y_dram[t]).then_inc((YT[l]["loaded0"], YT[l]["loaded1"])[t % 2].sem, 16)
                gate_rows(s, l, 0)
                if l:
                    gain_rows(s, l - 1, 1)
                for t in range(T_Q[l]):
                    src = x_dram[t] if l else A["x"][0, t * P:(t + 1) * P, :] if t < LT else A["ctx"][0, (t - LT) * P:(t - LT + 1) * P, :]
                    pool.dma_start(x_res[:, t, :], src).then_inc(s["loaded"].sem, 16)
                end()
                fence(pool, l, "out")
                if l:
                    pool.wait_ge(*s["loaded"].at(16 * T_Q[l]))
                    pool.wait_ge(*s["gain_landed"].at(32))
                    for t in range(T_Q[l]):
                        residual(s, t, x_res)
                spreads(s, l)
                end()
                fence(pool, l, "ffn")
                s = LN[l][1]
                gain_rows(s, l, 0)
                gate_rows(s, l, 1)
                pool.wait_ge(*s["gain_landed"].at(32))
                for t in range(T_Q[l]):
                    residual(s, t, acc)
                if l == DEPTH - 1:
                    pool.wait_ge(*s["res_ready"].at(T_Q[l]))
                    pool.dma_start(gain_row[:, 0, :], A["ln2_g"][l].partition_broadcast(P)).then_inc(s["gain_landed"].sem, 16)
                    pool.dma_start(gain_row[:, 1, :], A["ln2_b"][l].partition_broadcast(P)).then_inc(s["gain_landed"].sem, 16)
                spreads(s, l)
                for t in range(T_Q[l]):
                    if l < DEPTH - 1:
                        pool.wait_ge(*s["normed"].at(t + 1))
                        pool.dma_start(x_dram[t], acc[:, t, :]).then_inc(s["stored"].sem, 16)
                    else:
                        pool.wait_ge(*s["out_gained"].at(t + 1))
                        pool.tensor_tensor(acc[:, t, :], acc[:, t, :], gain_row[:, 1, :], ALU.add).then_inc(s["out_ready"].sem, 1)
                        pool.wait_ge(*s["out_ready"].at(t + 1))
                        pool.dma_start(out[0, t * P:(t + 1) * P, :], acc[:, t, :]).then_inc(s["stored"].sem, 16)
                pool.wait_ge(*s["stored"].at(16 * T_Q[l]))
                end()

        @block.scalar
        def _(act):
            def end():
                act.drain().then_inc(act_phase, 1)

            def split(u):
                if isinstance(u, int) and u >= DEPTH * N_UNITS:
                    return
                split_at(u % 2, u // 2)

            def split_at(slot, turn):
                act.wait_ge(raw_landed[slot], (turn + 1) * 16)
                act.activation(w_hi[:, slot, :], w_raw[:, slot, :], ACT.Copy).then_inc(w_hi_ready, 1)

            def modulated(s, t, l, w, h):
                strm = 0 if t < LT else 1
                act.wait_ge(*s["turned"].at(t + 1))
                if t >= 2:
                    act.wait_ge(*s["lo"].at(t - 1))
                for k in range(4):
                    i = act.activation(h[:, t % 2, k * P:(k + 1) * P], bank(2 * (t % 2), P, at=k * P), ACT.Identity,
                                       bias=mod_b[l][w][:, k, strm:strm + 1], scale=mod_a[l][w][:, k, strm:strm + 1])
                i.then_inc(s["h_act"].sem, 1)
                act.wait_ge(*s["h_act"].at(t + 1))
                act.wait_ge(*s["h_dve"].at(t + 1))
                act.activation(xt_hi[:, :, t * P:(t + 1) * P], h[:, t % 2, :].rearrange("p (k n) -> p k n", n=P), ACT.Copy).then_inc(s["hi"].sem, 1)

            act.dma_start(ident[:, :], A["k_ident"]).then_inc(ident_landed, 16)
            for r, src in ((V_C, A["c"][0]), (V_CC, A["c_ctx"]), (V_BMOD, A["b_mod"][0]), (V_G1, A["ln1_g"][0]), (V_B1, A["ln1_b"][0]),
                           (V_G2, A["ln2_g"][0]), (V_B2, A["ln2_b"][0]), (V_QN, A["mla_q_norm_g"][0]), (V_KN, A["mla_kv_norm_g"][0])):
                act.dma_start(vrow[r:r + src.shape[0] // P, 0, :], src.rearrange("(a p) -> a p", p=P)).then_inc(vrow_landed[0], 16)
            for t in range(NT):
                src = A["x"][0, t * P:(t + 1) * P, :] if t < LT else A["ctx"][0, (t - LT) * P:(t - LT + 1) * P, :]
                act.dma_start(x_first[:, t, :], src).then_inc(x_first_landed, 16)
            act.wait_ge(vec_ready, 1)
            act.activation(silu_tmp[:, :, :], vec[0][:, V_C:V_ROWS].rearrange("p (s k) -> p s k", k=KT), ACT.Exp, scale=-1.0).then_inc(silu_exp, 1)
            split(0)
            split(1)
            act.wait_ge(modv_ready, 1)
            for t in range(NT):
                modulated(X0, t, 0, 0, h32_first)
            for l in range(DEPTH):
                act.wait_ge(lam_dot, l + 1)
                act.activation(lam_tmp[:, 2 * l:2 * l + 2], lam_tmp[:, 2 * l:2 * l + 2], ACT.Exp).then_inc(lam_exp, 1)
            end()

            def in_tile(s, i, psum_bank, parts, raw, dst, scale, ctx_too):
                act.wait_ge(*s["tile"].at(i + 1))
                if i >= 2:
                    act.wait_ge(*s["done"].at(i - 1))
                if ctx_too:
                    act.activation(dst[:, SEQ:TOK], bank(psum_bank + 1, CTX, parts), ACT.Copy, scale=scale)
                act.activation(raw[0:parts, i % 2, :], bank(psum_bank, SEQ, parts), ACT.Copy, scale=scale).then_inc(s["raw"].sem, 1)

            def beside(l, g, parts, n):
                s = IN[l][g] if parts else None
                for h in halves_beside(parts, len(ITEMS[l]), n):
                    if h % 2 == 0:
                        continue
                    kind, u, i = parts[h // 2][:3]
                    act.wait_ge(*s["part"].at(h // 2 + 1))
                    if kind == "features":
                        c, w = parts[h // 2][3:]
                        dst, sc = (na_q, HD ** -0.5) if u == 8 else (na_k, 1.0)
                        act.activation(dst[:, i, c:c + w], bank(7, w), ACT.Copy, scale=sc).then_inc(s["part_copied"].sem, 1)
                    else:
                        w = IN_UNITS[u][1]
                        dst = ml_rows[:, i, 0:w] if u == 6 else ml_rows[:, i, Q_RANK:Q_RANK + w] if u == 7 else na_v[:, i, :]
                        act.activation(dst, bank(7, w), ACT.Copy).then_inc(s["part_copied"].sem, 1)
                    if h // 2 + 1 == len(parts) or parts[h // 2 + 1][1] != u:
                        split(in_unit(l, u + 2))

            def attention(l, g, nmaps, p, pt, parts):
                s = AT[l][g]
                items = ITEMS[l]

                def exps(n):
                    qt, h = items[n]
                    st = att_st[:, n % 6, :]
                    nk = TOK if qt < LT else CTX
                    if n >= 2:
                        act.wait_ge(*s["turned"].at(n - 1))
                    for m in range(nmaps):
                        act.wait_ge(*s["negmax"].at(n * nmaps + m + 1))
                        b = 2 * m if nmaps == 2 else 2 * (n % 2)
                        if g == 2 and qt < LT:
                            act.activation(p[:, n % 2, 0, 0:SEQ], p[:, n % 2, 0, 0:SEQ], ACT.Exp, bias=st[:, 0:1], accum_out=st[:, 2:3])
                            act.activation(p[:, n % 2, 0, SEQ:TOK], bank(b + 1, CTX), ACT.Exp, bias=st[:, 0:1],
                                           accum_out=st[:, 3:4]).then_inc(s["probs"].sem, 1)
                        else:
                            act.activation(p[:, n % 2, m, 0:nk], bank(b, nk), ACT.Exp, bias=st[:, m:m + 1],
                                           accum_out=st[:, 2 + m:3 + m]).then_inc(s["probs"].sem, 1)

                def turned_copy(n):
                    nk = TOK if items[n][0] < LT else CTX
                    act.wait_ge(*s["turned"].at(n + 1))
                    if n >= 2:
                        act.wait_ge(*s["mixed_values"].at(n - 1))
                    act.activation(pt[:, n % 2, 0:nk], bank(4, nk), ACT.Copy).then_inc(s["turned_copied"].sem, 1)

                lead = 1 if nmaps == 2 else 2
                for n in range(lead):
                    exps(n)
                if lead == 2:
                    turned_copy(0)
                for n in range(len(items)):
                    if n + lead < len(items):
                        exps(n + lead)
                    if n + lead - 1 < len(items):
                        turned_copy(n + lead - 1)
                    beside(l, g + 1, parts, n)

            def norm(s, t):
                act.wait_ge(*s["stats"].at(t + 1))
                act.activation(acc[:, t, :], acc[:, t, :], ACT.Identity, bias=ln_st[:, t, 16:17], scale=ln_st[:, t, 15:16]).then_inc(s["normed"].sem, 1)

            for l in range(DEPTH):
                q_ctx = T_Q[l] == NT
                T = T_Q[l]
                fence(act, l, "inA")
                s = IN[l][0]
                for i in range(8):
                    dst = da_q[:, i, :] if i < HEADS else da_k[:, i - HEADS, :]
                    in_tile(s, i, 2 * (i % 2), P, da_raw, dst, HD ** -0.5 if i < HEADS else 1.0, i >= HEADS or q_ctx)
                    if i % 2:
                        split(in_unit(l, i // 2 + 2))
                for u in range(2):
                    for t in range(NT):
                        act.wait_ge(*s["v"].at(u * NT + t + 1))
                        act.activation(da_v[:, t, u * UW:(u + 1) * UW], bank(4 + t % 2, UW), ACT.Copy).then_inc(s["v_copied"].sem, 1)
                    split(in_unit(l, 4 + u + 2))
                end()
                fence(act, l, "atA")
                attention(l, 0, 2, da_p, da_pt, ML_PARTS[T])
                end()

                fence(act, l, "inB")
                s, m = IN[l][1], ML[l]
                for t in range(NT):
                    act.wait_ge(*m["turned"].at(t + 1))
                    b = 4 + t % 2
                    tk = slice(t * P, (t + 1) * P)
                    if t < T:
                        for k in range(2):
                            act.activation(ml_cq[:, k, tk], bank(b, P, at=k * P), ACT.Copy, scale=vec[l][:, V_QN + k:V_QN + k + 1])
                    act.activation(ml_kr[HD:MQ, tk], psum[HD:MQ, b * 512 + 3 * P:b * 512 + 4 * P], ACT.Copy)
                    act.activation(ml_ckv[:, tk], bank(b, P, at=2 * P), ACT.Copy, scale=vec[l][:, V_KN:V_KN + 1]).then_inc(m["evacuated"].sem, 1)
                for h in range(HEADS):
                    in_tile(s, h, 2 * (h % 2), MQ, ml_raw, ml_q[:, h, :], MQ ** -0.5, q_ctx)
                for h in range(HEADS):
                    act.wait_ge(*s["tile"].at(HEADS + h + 1))
                    b = 2 * (h % 2)
                    act.activation(ml_k[0:HD, h, :], psum[0:HD, b * 512:b * 512 + TOK], ACT.Copy).then_inc(m["up"].sem, 1)
                for t in range(NT):
                    act.wait_ge(*m["v_ready"].at(t + 1))
                    act.activation(ml_v[:, t, :], bank(6 + t % 2, 256), ACT.Copy).then_inc(m["v_copied"].sem, 1)
                act.wait_ge(*s["done"].at(HEADS + 1))
                for h in range(HEADS):
                    act.activation(ml_k[HD:MQ, h, SEQ:TOK], ml_kr[HD:MQ, SEQ:TOK], ACT.Copy)
                    act.activation(ml_k[HD:MQ, h, 0:SEQ], ml_t[HD:MQ, 0, :], ACT.Copy)
                end()
                fence(act, l, "atB")
                attention(l, 1, 1, ml_p, ml_pt, NA_PARTS[T])
                end()
                fence(act, l, "atC")
                attention(l, 2, 1, na_p, na_pt, [])
                end()

                fence(act, l, "yT")
                for t in range(T):
                    act.wait_ge(*YT[l]["turned"].at(t + 1))
                    act.activation(xt_hi[:, :, t * P:(t + 1) * P], bank(2 * (t % 2), D).rearrange("p (k n) -> p k n", n=P), ACT.Copy).then_inc(YT[l]["hi"].sem, 1)
                end()

                fence(act, l, "out")
                s = LN[l][0]
                for u in range(N_OUT - 1):
                    act.wait_ge(*OP[l]["product"].at((u + 1) * T))
                    split(in_unit(l, N_IN + u + 2))
                for t in range(T):
                    norm(s, t)
                    if t >= 2:
                        modulated(s, t - 2, l, 1, h32)
                act.wait_ge(*OP[l]["product"].at(N_OUT * T))
                split(in_unit(l, N_IN + N_OUT + 1))
                for t in range(T - 2, T):
                    modulated(s, t, l, 1, h32)
                end()

                fence(act, l, "ffn")
                s = FF[l]
                tokens = T * P
                u0 = in_unit(l, N_IN + N_OUT)
                act.drain().then_inc(s["bank1_free"].sem, 2)

                def hidden(i):
                    for a in range(2):
                        for j in (2 * a, 2 * a + 1):
                            act.wait_ge(*s["hidden"].at(i * FG + j + 1))
                            act.wait_ge(*s["hid_lo"].at(i * FG + j + 1))
                            act.activation(relu[:, j % 2, 0:tokens], bank(2 * (j % 2), tokens), ACT.Relu).then_inc(s["bank1_free"].sem, 1)
                            act.wait_ge(*s["bank1_free"].at(i * FG + j + 3))
                            act.activation(hid_hi[:, j, 0:tokens], relu[:, j % 2, 0:tokens], ACT.Square).then_inc(s["hid_hi"].sem, 1)
                        u = u0 + a + 2
                        split_at(u % 2, i * 2 + u // 2)

                def second(i, b):
                    act.wait_ge(*s["product"].at(i * (2 * T) + (b + 1) * T))
                    u = u0 + 2 + b + 2
                    split_at(u % 2, i * 2 + u // 2)

                with act.Fori(0, GROUPS - 1) as i:
                    hidden(i)
                    second(i, 0)
                    second(i, 1)
                hidden(GROUPS - 1)
                n = LN[l][1]
                if l + 1 < DEPTH:
                    second(GROUPS - 1, 0)
                    for t in range(T):
                        norm(n, t)
                        if t >= 2:
                            modulated(n, t - 2, l + 1, 0, h32)
                    second(GROUPS - 1, 1)
                    for t in range(T - 2, T):
                        modulated(n, t, l + 1, 0, h32)
                else:
                    for t in range(T):
                        norm(n, t)
                end()

        @block.vector
        def _(dve):
            def end():
                dve.drain().then_inc(dve_phase, 1)

            steps = [0]

            def link(ins):
                steps[0] += 1
                ins.then_inc(dve_step, 1)
                dve.wait_ge(dve_step, steps[0])

            def split(u):
                if isinstance(u, int) and u >= DEPTH * N_UNITS:
                    return
                split_at(u, u % 2)

            def split_at(u, slot):
                dve.wait_ge(w_hi_ready, u + 1)
                dve.tensor_tensor(w_lo[:, slot, :], w_raw[:, slot, :], w_hi[:, slot, :].bitcast(F32), ALU.subtract).then_inc(w_lo_ready, 1)

            def add_row(n):
                l, v = n // WMOD_UNITS, n // VU
                dve.wait_ge(wm_used, n + 1)
                if n % VU == 0:
                    dve.wait_ge(b_landed[v % 2], 16 * (v // 2 + 1))
                dst = mod_row[l][v % 2][:, n % VU * UW:(n % VU + 1) * UW]
                dve.tensor_tensor(dst, bank(wmod_bank(n), UW, 2), dst, ALU.add).then_inc(row_added, 1)

            def modulation(i, b):
                l, first, last = MOD_COLUMNS[i]
                dve.wait_ge(mod_turned, i + 1)
                link(dve.tensor_copy(modv[l][:, first:last, :], bank(b, 2 * (last - first)).rearrange("p (s n) -> p n s", s=2)))

            def factors(l, w):
                sh, sc = (SHIFT1, SCALE1) if w == 0 else (SHIFT2, SCALE2)
                a, b = mod_a[l][w], mod_b[l][w]
                link(dve.tensor_scalar(a[:, :, :], modv[l][:, sc:sc + KT, :], 1.0, None, ALU.add))
                if w == 0 and l == 0:
                    dve.tensor_copy(b[:, :, :], modv[l][:, sh:sh + KT, :]).then_inc(modv_ready, 1)
                    dve.wait_ge(modv_ready, 1)
                    return
                v, g0, b0 = (vec[l], V_G1, V_B1) if w == 1 else (vec[l - 1], V_G2, V_B2)
                link(dve.tensor_tensor(b[:, :, :], a[:, :, :], v[:, b0:b0 + KT].unsqueeze(2).broadcast_to([P, KT, 2]), ALU.mult))
                link(dve.tensor_tensor(b[:, :, :], b[:, :, :], modv[l][:, sh:sh + KT, :], ALU.add))
                link(dve.tensor_tensor(a[:, :, :], a[:, :, :], v[:, g0:g0 + KT].unsqueeze(2).broadcast_to([P, KT, 2]), ALU.mult))

            def modulated(s, t, l, w, h):
                strm = 0 if t < LT else 1
                dve.wait_ge(*s["turned"].at(t + 1))
                if t >= 2:
                    dve.wait_ge(*s["lo"].at(t - 1))
                for k in range(4, 8):
                    i = dve.tensor_scalar(h[:, t % 2, k * P:(k + 1) * P], bank(2 * (t % 2) + 1, P, at=(k - 4) * P),
                                          mod_a[l][w][:, k, strm:strm + 1], mod_b[l][w][:, k, strm:strm + 1], ALU.mult, ALU.add)
                i.then_inc(s["h_dve"].sem, 1)

            def low(s, t, h):
                dve.wait_ge(*s["hi"].at(t + 1))
                tk = slice(t * P, (t + 1) * P)
                dve.tensor_tensor(xt_lo[:, :, tk], h[:, t % 2, :].rearrange("p (k n) -> p k n", n=P),
                                  xt_hi[:, :, tk].bitcast(F32), ALU.subtract).then_inc(s["lo"].sem, 1)

            dve.memset(rms_st[:, :], 1.0)
            dve.wait_ge(vec_turned, 1)
            dve.tensor_copy(vec[0][:, :], bank(4, V_ROWS)).then_inc(vec_ready, 1)
            dve.wait_ge(silu_exp, 1)
            link(dve.tensor_scalar(silu_tmp[:, :, :], silu_tmp[:, :, :], 1.0, None, ALU.add))
            link(dve.reciprocal(silu_tmp[:, :, :], silu_tmp[:, :, :]))
            dve.tensor_tensor(silu[:, :, :], vec[0][:, V_C:V_ROWS].rearrange("p (s k) -> p s k", k=KT), silu_tmp[:, :, :], ALU.mult).then_inc(silu_ready, 1)
            for n in range(WM_FIRST):
                add_row(n)
                if n in (3, 5):
                    split(n // 2 - 1)
            modulation(0, 6)
            factors(0, 0)
            for t in range(NT):
                modulated(X0, t, 0, 0, h32_first)
                if t >= 1:
                    low(X0, t - 1, h32_first)
            low(X0, NT - 1, h32_first)
            dve.wait_ge(vec_turned, DEPTH)
            dve.tensor_copy(vec[1][:, :], bank(5, V_ROWS)).then_inc(vec_ready, 1)
            dve.wait_ge(lamv_landed, 16 * 5 * DEPTH)
            for l in range(DEPTH):
                link(dve.tensor_tensor_reduce(lam_junk, lamv[:, 4 * l, :], lamv[:, 4 * l + 1, :], 1.0, 0.0, ALU.mult, ALU.add, lam_tmp[:, 2 * l:2 * l + 1]))
                dve.tensor_tensor_reduce(lam_junk, lamv[:, 4 * l + 2, :], lamv[:, 4 * l + 3, :], 1.0, 0.0, ALU.mult, ALU.add, lam_tmp[:, 2 * l + 1:2 * l + 2]).then_inc(lam_dot, 1)
                dve.wait_ge(lam_dot, l + 1)
                dve.tensor_scalar(subln[l][:, :], subln[l][:, :], 1.0 - LAM_INIT[l], None, ALU.mult)
            for l in range(DEPTH):
                dve.wait_ge(lam_exp, l + 1)
                link(dve.tensor_tensor(neg_lam[l][:, :], lam_tmp[:, 2 * l + 1:2 * l + 2], lam_tmp[:, 2 * l:2 * l + 1], ALU.subtract))
                link(dve.tensor_scalar(neg_lam[l][:, :], neg_lam[l][:, :], LAM_INIT[l], None, ALU.subtract))
            end()

            def rotate(s, i, rot_bank, parts, lo, raw, tmp, dst, cos, sin):
                r = slice(lo, parts)
                dve.wait_ge(*s["raw"].at(i + 1))
                if i >= 1:
                    dve.wait_ge(*s["done"].at(i))
                dve.tensor_tensor(tmp[r, 0, :], raw[r, i % 2, :], cos[r, :], ALU.mult)
                dve.wait_ge(*s["rot"].at(i + 1))
                link(dve.tensor_tensor(tmp[r, 1, :], psum[r, rot_bank * 512:rot_bank * 512 + SEQ], sin[r, :], ALU.mult))
                dve.tensor_tensor(dst, tmp[r, 0, :], tmp[r, 1, :], ALU.add).then_inc(s["done"].sem, 1)

            def beside(l, parts, n):
                for h in halves_beside(parts, len(ITEMS[l]), n):
                    if h % 2 and (h // 2 + 1 == len(parts) or parts[h // 2 + 1][1] != parts[h // 2][1]):
                        split(in_unit(l, parts[h // 2][1] + 2))

            def attention(l, g, nmaps, p, y, dv, bias, parts):
                s = AT[l][g]
                items = ITEMS[l]

                def maxima(n):
                    qt, h = items[n]
                    nk = TOK if qt < LT else CTX
                    st = att_st[:, n % 6, :]
                    for m in range(nmaps):
                        dve.wait_ge(*s["scores"].at(n * nmaps + m + 1))
                        b = 2 * m if nmaps == 2 else 2 * (n % 2)
                        if bias is not None and qt < LT:
                            if n >= 2:
                                dve.wait_ge(*s["turned"].at(n - 1))
                            j = (6 - 2 * qt) * GRID_W
                            dve.tensor_tensor_reduce(p[:, n % 2, 0, 0:SEQ], bank(b, SEQ), bias[:, h, j:j + SEQ], 1.0, 3.0 * MASKED,
                                                     ALU.add, ALU.max, st[:, 8:9])
                            link(dve.tensor_reduce(st[:, 9:10], bank(b + 1, CTX), AX.X, ALU.max))
                            dve.tensor_scalar(st[:, 0:1], st[:, 8:9], st[:, 9:10], -1.0, ALU.max, ALU.mult).then_inc(s["negmax"].sem, 1)
                        else:
                            dve.tensor_reduce(st[:, m:m + 1], bank(b, nk), AX.X, ALU.max, negate=True).then_inc(s["negmax"].sem, 1)

                def mix(n):
                    qt, h = items[n]
                    nk = TOK if qt < LT else CTX
                    st = att_st[:, n % 6, :]
                    dve.wait_ge(*s["probs"].at(2 * n + 2))
                    link(dve.reciprocal(st[:, 4:5], st[:, 3:4]))
                    link(dve.tensor_scalar(st[:, 5:6], st[:, 2:3], st[:, 4:5], neg_lam[l][:, 0:1], ALU.mult, ALU.mult))
                    dve.scalar_tensor_tensor(out=p[:, n % 2, 0, 0:nk], in0=p[:, n % 2, 1, 0:nk], scalar=st[:, 5:6],
                                             in1=p[:, n % 2, 0, 0:nk], op0=ALU.mult, op1=ALU.add).then_inc(s["mixed"].sem, 1)

                def finish(n):
                    qt, h = items[n]
                    st = att_st[:, n % 6, :]
                    o = bank(6, dv)
                    dst = y[:, qt % 2, h * dv:(h + 1) * dv]
                    dve.wait_ge(*s["probs"].at((n + 1) * nmaps))
                    if bias is not None and qt < LT:
                        link(dve.tensor_tensor(st[:, 2:3], st[:, 2:3], st[:, 3:4], ALU.add))
                    link(dve.reciprocal(st[:, 6:7], st[:, 2:3]))
                    dve.wait_ge(*s["mixed_values"].at(n + 1))
                    if nmaps == 1:
                        if h == 0 and qt >= 2:
                            dve.wait_ge(*(s["y_stored0"], s["y_stored1"])[qt % 2].at(16 * (qt // 2)))
                        dve.tensor_scalar(dst, o, st[:, 6:7], None, ALU.mult).then_inc(s["y"].sem, 1)
                        return
                    oh = da_o[:, n % 2, :]
                    if n >= 2:
                        dve.wait_ge(*s["y"].at(n - 1))
                    link(dve.tensor_scalar(oh, o, st[:, 6:7], None, ALU.mult))
                    link(dve.tensor_tensor_reduce(da_junk, oh, oh, 1.0 / DA_V, 0.0, ALU.mult, ALU.add, st[:, 7:8]))
                    dve.tensor_scalar(st[:, 8:9], st[:, 7:8], SUBLN_EPS, None, ALU.add).then_inc(s["mean_square"].sem, 1)

                def sub_norm(n):
                    qt, h = items[n]
                    dve.wait_ge(*s["rms"].at(n + 1))
                    if h == 0 and qt >= 2:
                        dve.wait_ge(*(s["y_stored0"], s["y_stored1"])[qt % 2].at(16 * (qt // 2)))
                    dve.scalar_tensor_tensor(out=y[:, qt % 2, h * dv:(h + 1) * dv], in0=da_o[:, n % 2, :], scalar=att_st[:, n % 6, 9:10],
                                             in1=subln[l][:, :], op0=ALU.mult, op1=ALU.mult).then_inc(s["y"].sem, 1)

                if nmaps == 2:
                    maxima(0)
                    for n in range(len(items) + 1):
                        if n < len(items):
                            mix(n)
                        if n + 1 < len(items):
                            maxima(n + 1)
                        if n >= 2:
                            sub_norm(n - 2)
                        if n >= 1:
                            finish(n - 1)
                        if n < len(items):
                            beside(l, parts, n)
                    sub_norm(len(items) - 1)
                else:
                    for n in range(3):
                        maxima(n)
                    for n in range(len(items)):
                        if n + 3 < len(items):
                            maxima(n + 3)
                        finish(n)
                        beside(l, parts, n)
                        if g == 2 and l == 0:
                            add_row(WMOD_UNITS + n)

            def norm_rows(l, n_q):
                m = ML[l]
                parts = [(k, c, w, t) for t in range(NT) for k, c, w in ((0, 0, Q_RANK), (1, Q_RANK, KV_RANK)) if k or t < n_q]
                for k, c, w, t in parts:
                    r = ml_rows[:, t, c:c + w]
                    link(dve.tensor_tensor_reduce(ml_junk[:, 0:w], r, r, 1.0 / w, 0.0, ALU.mult, ALU.add, rms_st[:, k * NT + t:k * NT + t + 1]))
                dve.tensor_scalar(rms_eps[:, :], rms_st[:, :], RMS_EPS, None, ALU.add).then_inc(m["mean_squares"].sem, 1)
                dve.wait_ge(*m["rms"].at(1))
                for k, c, w, t in parts:
                    r = ml_rows[:, t, c:c + w]
                    ins = dve.tensor_scalar(r, r, rms_inv[:, k * NT + t:k * NT + t + 1], None, ALU.mult)
                    if k:
                        ins.then_inc(m["normed"].sem, 1)

            def half_stats(t, k):
                link(dve.bn_stats(ln_st[:, t, 6 * k:6 * k + 6], acc[:, t, k * 512:(k + 1) * 512]))

            def variance(s, t):
                st = ln_st[:, t, :]
                link(dve.bn_aggr(st[:, 12:14], st[:, 0:12]))
                dve.tensor_scalar(st[:, 12:13], st[:, 12:13], -1.0, None, ALU.mult)
                dve.tensor_scalar(st[:, 14:15], st[:, 13:14], LN_EPS, None, ALU.add).then_inc(s["variance"].sem, 1)

            for l in range(DEPTH):
                T = T_Q[l]
                fence(dve, l, "inA")
                s = IN[l][0]
                dve.wait_ge(*s["tables"].at(32))
                for i in range(8):
                    dst = da_q[:, i, 0:SEQ] if i < HEADS else da_k[:, i - HEADS, 0:SEQ]
                    rotate(s, i, 4 + i % 2, P, 0, da_raw, da_t, dst, cos64, sin64)
                    if l == 0:
                        add_row(WM_FIRST + i)
                    if i % 2:
                        split(in_unit(l, i // 2 + 2))
                for n in range(2 * NT):
                    if l == 0 and WM_FIRST + 8 + n < WMOD_UNITS:
                        add_row(WM_FIRST + 8 + n)
                    if n % NT == NT - 1:
                        split(in_unit(l, 4 + n // NT + 2))
                end()
                fence(dve, l, "atA")
                attention(l, 0, 2, da_p, da_y, DA_V, None, ML_PARTS[T])
                end()

                fence(dve, l, "inB")
                s, m = IN[l][1], ML[l]
                norm_rows(l, T)
                if l == 0:
                    modulation(1, 7)
                    factors(0, 1)
                dve.wait_ge(*s["tables"].at(32))
                for h in range(HEADS):
                    rotate(s, h, 4 + h % 2, MQ, 0, ml_raw, ml_t, ml_q[:, h, 0:SEQ], cos32, sin32)
                dve.wait_ge(*s["rot"].at(HEADS + 1))
                dve.wait_ge(*s["done"].at(HEADS))
                r = slice(HD, MQ)
                dve.tensor_tensor(ml_t[r, 0, :], ml_kr[r, 0:SEQ], cos32[r, :], ALU.mult)
                link(dve.tensor_tensor(ml_t[r, 1, :], psum[r, 4 * 512:5 * 512], sin32[r, :], ALU.mult))
                dve.tensor_tensor(ml_t[r, 0, :], ml_t[r, 0, :], ml_t[r, 1, :], ALU.add).then_inc(s["done"].sem, 1)
                end()
                fence(dve, l, "atB")
                attention(l, 1, 1, ml_p, ml_y, HD, None, NA_PARTS[T])
                end()

                fence(dve, l, "atC")
                dve.wait_ge(*BIAS[l]["ready"].at(1))
                attention(l, 2, 1, na_p, na_y, HD, na_bias, [])
                end()

                fence(dve, l, "yT")
                for t in range(T):
                    dve.wait_ge(*YT[l]["hi"].at(t + 1))
                    tk = slice(t * P, (t + 1) * P)
                    dve.tensor_tensor(xt_lo[:, :, tk], bank(2 * (t % 2), D).rearrange("p (k n) -> p k n", n=P),
                                      xt_hi[:, :, tk].bitcast(F32), ALU.subtract).then_inc(YT[l]["lo"].sem, 1)
                if l == 0:
                    modulation(2, 7)
                    factors(1, 0)
                    factors(1, 1)
                end()

                fence(dve, l, "out")
                s = LN[l][0]
                dve.wait_ge(*s["gate_landed"].at(16 * (2 if T == NT else 1)))
                if l == 0:
                    dve.wait_ge(*s["loaded"].at(16 * T))
                for u in range(N_OUT):
                    for t in range(T):
                        n = u * T + t
                        cols = slice(u * UW, (u + 1) * UW)
                        dve.wait_ge(*OP[l]["product"].at(n + 1))
                        dve.tensor_tensor(acc[:, t, cols], bank(4 + n % 4, UW), gate_row[:, 0 if t < LT else 1, cols], ALU.mult).then_inc(OP[l]["gated"].sem, 1)
                        if l:
                            dve.wait_ge(*s["res_ready"].at(t + 1))
                        dve.wait_ge(*OP[l]["gated"].at(n + 1))
                        ins = dve.scalar_tensor_tensor(out=acc[:, t, cols], in0=x_res[:, t, cols], scalar=ALPHA, in1=acc[:, t, cols], op0=ALU.mult, op1=ALU.add)
                        if u % 2:
                            link(ins)
                            half_stats(t, u // 2)
                        if u == N_OUT - 1:
                            variance(s, t)
                            if t >= 2:
                                modulated(s, t - 2, l, 1, h32)
                            if t >= 3:
                                low(s, t - 3, h32)
                    if u < N_OUT - 1:
                        split(in_unit(l, N_IN + u + 2))
                split(in_unit(l, N_IN + N_OUT + 1))
                low(s, T - 3, h32)
                for t in range(T - 2, T):
                    modulated(s, t, l, 1, h32)
                    low(s, t, h32)
                end()

                fence(dve, l, "ffn")
                s, n1 = FF[l], LN[l][1]
                tokens = T * P
                u0 = in_unit(l, N_IN + N_OUT)
                dve.drain().then_inc(s["hid_lo"].sem, 2)
                dve.drain().then_inc(s["bank2_free"].sem, 4)

                def hidden(i):
                    for a in range(2):
                        for j in (2 * a, 2 * a + 1):
                            dve.wait_ge(*s["bank1_free"].at(i * FG + j + 3))
                            r = relu[:, j % 2, 0:tokens]
                            dve.tensor_tensor(squares[:, j % 2, 0:tokens], r, r, ALU.mult).then_inc(s["squared"].sem, 1)
                            dve.wait_ge(*s["squared"].at(i * FG + j + 1))
                            dve.wait_ge(*s["hid_hi"].at(i * FG + j + 1))
                            dve.tensor_tensor(hid_lo[:, j, 0:tokens], squares[:, j % 2, 0:tokens], hid_hi[:, j, 0:tokens].bitcast(F32),
                                              ALU.subtract).then_inc(s["hid_lo"].sem, 1)
                        split_at(i * FU + (u0 + a + 2), (u0 + a) % 2)

                def added(i, b, t):
                    n = b * T + t
                    dve.wait_ge(*s["product"].at(i * (2 * T) + n + 1))
                    dst = acc[:, t, b * 512:(b + 1) * 512]
                    return dve.tensor_tensor(dst, dst, bank(4 + n % 4), ALU.add).then_inc(s["bank2_free"].sem, 1)

                def second_split(i, b):
                    split_at(i * FU + (u0 + 2 + b + 2), (u0 + b) % 2)

                hidden(0)
                for b in range(2):
                    for t in range(T):
                        n = b * T + t
                        dve.wait_ge(*s["product"].at(n + 1))
                        dve.wait_ge(*n1["res_ready"].at(t + 1))
                        dve.tensor_copy(acc[:, t, b * 512:(b + 1) * 512], bank(4 + n % 4)).then_inc(s["bank2_free"].sem, 1)
                    second_split(0, b)
                with dve.Fori(1, GROUPS - 1) as i:
                    dve.wait_ge(*s["bank2_free"].at(i * (2 * T) + 4))
                    hidden(i)
                    for b in range(2):
                        for t in range(T):
                            added(i, b, t)
                        second_split(i, b)
                i = GROUPS - 1
                dve.wait_ge(*s["bank2_free"].at(i * (2 * T) + 4))
                hidden(i)
                dve.wait_ge(*n1["gate_landed"].at(16 * (2 if T == NT else 1)))

                def out_gain(t):
                    dve.wait_ge(*n1["normed"].at(t + 1))
                    dve.tensor_tensor(acc[:, t, :], acc[:, t, :], gain_row[:, 0, :], ALU.mult).then_inc(n1["out_gained"].sem, 1)

                if l == DEPTH - 1:
                    dve.wait_ge(*n1["gain_landed"].at(64))
                for b in range(2):
                    cols = slice(b * 512, (b + 1) * 512)
                    for t in range(T):
                        added(i, b, t)
                        dve.wait_ge(*s["bank2_free"].at(i * (2 * T) + b * T + t + 5))
                        link(dve.tensor_tensor(acc[:, t, cols], acc[:, t, cols], gate_row[:, 0 if t < LT else 1, cols], ALU.mult))
                        link(dve.scalar_tensor_tensor(out=acc[:, t, cols], in0=x_res[:, t, cols], scalar=ALPHA, in1=acc[:, t, cols], op0=ALU.mult, op1=ALU.add))
                        half_stats(t, b)
                        if b == 1:
                            variance(n1, t)
                            if l == DEPTH - 1:
                                if t >= 1:
                                    out_gain(t - 1)
                                continue
                            if t >= 2:
                                modulated(n1, t - 2, l + 1, 0, h32)
                            if t >= 3:
                                low(n1, t - 3, h32)
                    if l + 1 < DEPTH:
                        second_split(i, b)
                if l + 1 < DEPTH:
                    low(n1, T - 3, h32)
                    for t in range(T - 2, T):
                        modulated(n1, t, l + 1, 0, h32)
                        low(n1, t, h32)
                else:
                    out_gain(T - 1)
                end()

        @block.tensor
        def _(pe):
            def end():
                pe.drain().then_inc(pe_phase, 1)

            def products(outs, lhs, rhs, start=True, stop=True):
                ks = lhs[0]
                for i, k in enumerate(ks):
                    l_hi, l_lo = lhs[1](k)
                    for n, (a, half) in enumerate(((l_hi, 0), (l_hi, 1), (l_lo, 0))):
                        for c, o in enumerate(outs):
                            ins = pe.matmul(o, a, rhs(k, c)[half], start=start and i == 0 and n == 0,
                                            stop=stop and i == len(ks) - 1 and n == 2)
                return ins

            def turn(s, t, rows):
                if t >= 2:
                    for name in ("h_act", "h_dve") if "h_act" in s else ("hi", "lo"):
                        pe.wait_ge(*s[name].at(t - 1))
                for k in range(KT):
                    ins = pe.transpose(bank(2 * (t % 2), P, at=k * P), rows[:, k * P:(k + 1) * P], ident[:, :])
                ins.then_inc(s["turned"].sem, 1)

            def wmod_unit(n):
                l, k = n // WMOD_UNITS, n % MR
                pe.wait_ge(wm_landed[k], 16 * (n // MR + 1))
                if n >= 2:
                    pe.wait_ge(row_added, n if n >= WMOD_UNITS else n - 1)
                for kt in range(KT):
                    ins = pe.matmul(bank(wmod_bank(n), UW, 2), silu[:, :, kt], wm_rings[l][:, k, kt, :], start=kt == 0, stop=kt == KT - 1)
                ins.then_inc(wm_used, 1)

            def turn_mod_rows(i, b):
                n = 2 * (MOD_COLUMNS[i][2] - MOD_COLUMNS[i][1])
                pe.wait_ge(mod_rows_landed, 32 * (i + 1))
                pe.transpose(bank(b, n), mod_rows[0:n, :], ident[0:n, 0:n]).then_inc(mod_turned, 1)

            pe.wait_ge(ident_landed, 16)
            pe.wait_ge(vrow_landed[0], 16 * 9)
            pe.transpose(bank(4, V_ROWS), vrow[0:V_ROWS, 0, :], ident[0:V_ROWS, 0:V_ROWS]).then_inc(vec_turned, 1)
            pe.wait_ge(silu_ready, 1)
            for n in range(WM_FIRST):
                wmod_unit(n)
            pe.wait_ge(x_first_landed, 16 * NT)
            for t in range(NT):
                turn(X0, t, x_first[:, t, :])
                if t == 1:
                    turn_mod_rows(0, 6)
            pe.wait_ge(vrow_landed[1], 16 * 9)
            pe.transpose(bank(5, V_ROWS), vrow[0:V_ROWS, 1, :], ident[0:V_ROWS, 0:V_ROWS]).then_inc(vec_turned, 1)
            pe.wait_ge(const_landed, 16 * 3)
            end()

            def xt(k, c0, n):
                return xt_hi[:, k, c0:c0 + n], xt_lo[:, k, c0:c0 + n]

            def weights_ready(u):
                pe.wait_ge(w_lo_ready, u + 1)

            def feature_tile(slot, col, l, all_tokens, banks):
                wh, wl = w_view(w_hi, slot), w_view(w_lo, slot)
                ch = chunks(l, all_tokens)
                return products([bank(banks + c, n) for c, (_, n) in enumerate(ch)],
                                (range(KT), lambda k: (wh[:, k, col:col + P], wl[:, k, col:col + P])),
                                lambda k, c: xt(k, *ch[c]))

            def row_tile(slot, t, width, o):
                wh, wl = w_view(w_hi, slot, width), w_view(w_lo, slot, width)
                return products([o], (range(KT), lambda k: xt(k, t * P, P)), lambda k, c: (wh[:, k, :], wl[:, k, :]))

            def beside(l, g, parts, n):
                s = IN[l][g] if parts else None
                for h in halves_beside(parts, len(ITEMS[l]), n):
                    kind, u, i = parts[h // 2][:3]
                    first = h % 2 == 0
                    if first:
                        weights_ready(in_unit(l, u))
                        if h >= 2:
                            pe.wait_ge(*s["part_copied"].at(h // 2))
                    ks = range(0, KT // 2) if first else range(KT // 2, KT)
                    width = IN_UNITS[u][1]
                    wh, wl = w_view(w_hi, in_unit(l, u), width), w_view(w_lo, in_unit(l, u), width)
                    if kind == "features":
                        c, w = parts[h // 2][3:]
                        ins = products([bank(7, w)], (ks, lambda k: (wh[:, k, i * P:(i + 1) * P], wl[:, k, i * P:(i + 1) * P])),
                                       lambda k, _: xt(k, c, w), start=first, stop=not first)
                    else:
                        ins = products([bank(7, width)], (ks, lambda k: xt(k, i * P, P)), lambda k, _: (wh[:, k, :], wl[:, k, :]),
                                       start=first, stop=not first)
                    if not first:
                        ins.then_inc(s["part"].sem, 1)

            def attention(l, g, nmaps, q, k, v, p, pt, dv, parts):
                s = AT[l][g]
                items = ITEMS[l]

                def keys(qt):
                    return (0, TOK) if qt < LT else (SEQ, CTX)

                def scores(n):
                    qt, h = items[n]
                    k0, nk = keys(qt)
                    for m in range(nmaps):
                        if nmaps == 2:
                            b = 2 * m
                            if n >= 1:
                                pe.wait_ge(*s["probs"].at(2 * (n - 1) + m + 1))
                        else:
                            b = 2 * (n % 2)
                            if n >= 2:
                                pe.wait_ge(*s["probs"].at(n - 1))
                        for c in range(0, nk, 512):
                            w = min(512, nk - c)
                            ins = pe.matmul(bank(b, w, at=c), q(h, m)[:, qt * P:(qt + 1) * P], k(h, m)[:, k0 + c:k0 + c + w], start=True, stop=True)
                        ins.then_inc(s["scores"].sem, 1)

                def turn_probs(n):
                    _, nk = keys(items[n][0])
                    pe.wait_ge(*s["mixed" if nmaps == 2 else "probs"].at(n + 1))
                    if n >= 1:
                        pe.wait_ge(*s["turned_copied"].at(n))
                    for c in range(nk // P):
                        ins = pe.transpose(bank(4, P, at=c * P), p[:, n % 2, 0, c * P:(c + 1) * P], ident[:, :])
                    ins.then_inc(s["turned"].sem, 1)

                def values(n):
                    qt, h = items[n]
                    k0, nk = keys(qt)
                    pe.wait_ge(*s["turned_copied"].at(n + 1))
                    if n >= 1:
                        pe.wait_ge(*s["mean_square" if nmaps == 2 else "y"].at(n))
                    for c in range(nk // P):
                        ins = pe.matmul(bank(6, dv), pt[:, n % 2, c * P:(c + 1) * P], v[:, k0 // P + c, h * dv:(h + 1) * dv],
                                        start=c == 0, stop=c == nk // P - 1)
                    ins.then_inc(s["mixed_values"].sem, 1)

                scores(0)
                if nmaps == 1:
                    scores(1)
                    turn_probs(0)
                    scores(2)
                for n in range(len(items)):
                    if nmaps == 2:
                        if n + 1 < len(items):
                            scores(n + 1)
                        turn_probs(n)
                    else:
                        if n + 1 < len(items):
                            turn_probs(n + 1)
                        if n + 3 < len(items):
                            scores(n + 3)
                    beside(l, g + 1, parts, n)
                    if g == 2 and l == 0:
                        wmod_unit(WMOD_UNITS + n)
                    if nmaps == 1:
                        values(n)
                    elif n >= 1:
                        values(n - 1)
                if nmaps == 2:
                    values(len(items) - 1)

            for l in range(DEPTH):
                T = T_Q[l]
                fence(pe, l, "inA")
                s = IN[l][0]

                def rotation(i):
                    pe.wait_ge(*s["raw"].at(i + 1))
                    if i >= 2:
                        pe.wait_ge(*s["done"].at(i - 1))
                    pe.matmul(bank(4 + i % 2), rot64[:, :], da_raw[:, i % 2, :], start=True, stop=True).then_inc(s["rot"].sem, 1)

                for i in range(8):
                    u = in_unit(l, i // 2)
                    if i % 2 == 0:
                        weights_ready(u)
                    if i >= 2:
                        pe.wait_ge(*s["raw"].at(i - 1))
                    feature_tile(u, (i % 2) * P, l, i >= HEADS, 2 * (i % 2)).then_inc(s["tile"].sem, 1)
                    if i >= 1:
                        rotation(i - 1)
                    if l == 0:
                        wmod_unit(WM_FIRST + i)
                rotation(7)
                for n in range(2 * NT):
                    u, t = n // NT, n % NT
                    if t == 0:
                        weights_ready(in_unit(l, 4 + u))
                    if n < 2:
                        pe.wait_ge(*s["done"].at(7 + n))
                    if n >= 2:
                        pe.wait_ge(*s["v_copied"].at(n - 1))
                    row_tile(in_unit(l, 4 + u), t, UW, bank(4 + t % 2, UW)).then_inc(s["v"].sem, 1)
                    if l == 0 and WM_FIRST + 8 + n < WMOD_UNITS:
                        wmod_unit(WM_FIRST + 8 + n)
                end()
                fence(pe, l, "atA")
                attention(l, 0, 2, lambda h, m: da_q[m * HD:(m + 1) * HD, h, :], lambda h, m: da_k[m * HD:(m + 1) * HD, h, :],
                          da_v, da_p, da_pt, DA_V, ML_PARTS[T])
                end()

                fence(pe, l, "inB")
                s, m = IN[l][1], ML[l]
                if l == 0:
                    turn_mod_rows(1, 7)
                for t in range(NT):
                    pe.wait_ge(*m["normed"].at(t + 1))
                    if t >= 2:
                        pe.wait_ge(*m["evacuated"].at(t - 1))
                    b = 4 + t % 2
                    if t < T:
                        for k in range(2):
                            pe.transpose(bank(b, P, at=k * P), ml_rows[:, t, k * P:(k + 1) * P], ident[:, :])
                    pe.transpose(bank(b, P, at=2 * P), ml_rows[:, t, Q_RANK:Q_RANK + KV_RANK], ident[:, :])
                    pe.transpose(bank(b, P, MQ, at=3 * P), ml_rows[:, t, Q_RANK + KV_RANK - HD:Q_RANK + KV_RANK + ROPE], ident[:, :]).then_inc(m["turned"].sem, 1)
                pe.wait_ge(*m["weights"].at(32))
                pe.wait_ge(*m["evacuated"].at(NT))

                def rotation_q(h):
                    pe.wait_ge(*s["raw"].at(h + 1))
                    if h >= 2:
                        pe.wait_ge(*s["done"].at(h - 1))
                    pe.matmul(bank(4 + h % 2, parts=MQ), rot32[:, :], ml_raw[0:MQ, h % 2, :], start=True, stop=True).then_inc(s["rot"].sem, 1)

                for h in range(HEADS):
                    if h >= 2:
                        pe.wait_ge(*s["raw"].at(h - 1))
                    for k in range(2):
                        for c, (c0, w) in enumerate(chunks(l)):
                            ins = pe.matmul(bank(2 * (h % 2) + c, w, MQ), ml_wq[:, k, h * MQ:(h + 1) * MQ], ml_cq[:, k, c0:c0 + w], start=k == 0, stop=k == 1)
                    ins.then_inc(s["tile"].sem, 1)
                    if h >= 1:
                        rotation_q(h - 1)
                rotation_q(HEADS - 1)
                for h in range(HEADS):
                    if h < 2:
                        pe.wait_ge(*s["raw"].at(HEADS - 1 + h))
                    else:
                        pe.wait_ge(*m["up"].at(h - 1))
                    for c, (c0, w) in enumerate(chunks(l, True)):
                        ins = pe.matmul(bank(2 * (h % 2) + c, w, HD), ml_wkv[:, h * P:h * P + HD], ml_ckv[:, c0:c0 + w], start=True, stop=True)
                    ins.then_inc(s["tile"].sem, 1)
                pe.wait_ge(*s["done"].at(HEADS))
                pe.matmul(psum[HD:MQ, 4 * 512:5 * 512], rot32[HD:MQ, HD:MQ], ml_kr[HD:MQ, 0:SEQ], start=True, stop=True).then_inc(s["rot"].sem, 1)
                wv = ml_wkv[:, :].rearrange("p (h n) -> p h n", n=P)[:, :, HD:P]
                for t in range(NT):
                    if t >= 2:
                        pe.wait_ge(*m["v_copied"].at(t - 1))
                    pe.matmul(bank(6 + t % 2, 256), ml_ckv[:, t * P:(t + 1) * P], wv, start=True, stop=True).then_inc(m["v_ready"].sem, 1)
                end()
                fence(pe, l, "atB")
                attention(l, 1, 1, lambda h, m: ml_q[:, h, :], lambda h, m: ml_k[:, h, :], ml_v, ml_p, ml_pt, HD, NA_PARTS[T])
                end()

                fence(pe, l, "atC")
                attention(l, 2, 1, lambda h, m: na_q[(h % 2) * HD:(h % 2 + 1) * HD, h // 2, :],
                          lambda h, m: na_k[(h % 2) * HD:(h % 2 + 1) * HD, h // 2, :], na_v, na_p, na_pt, HD, [])
                end()

                fence(pe, l, "yT")
                for t in range(T):
                    pe.wait_ge(*(YT[l]["loaded0"], YT[l]["loaded1"])[t % 2].at(16 * (t // 2 + 1)))
                    turn(YT[l], t, y_in[:, t % 2, :])
                if l == 0:
                    turn_mod_rows(2, 7)
                end()

                fence(pe, l, "out")
                s = LN[l][0]
                for u in range(N_OUT):
                    g = in_unit(l, N_IN + u)
                    weights_ready(g)
                    for t in range(T):
                        n = u * T + t
                        if n >= 4:
                            pe.wait_ge(*OP[l]["gated"].at(n - 3))
                        row_tile(g, t, UW, bank(4 + n % 4, UW)).then_inc(OP[l]["product"].sem, 1)
                        if u == N_OUT - 1 and t >= 2:
                            pe.wait_ge(*s["normed"].at(t - 1))
                            turn(s, t - 2, acc[:, t - 2, :])
                for t in range(T - 2, T):
                    pe.wait_ge(*s["normed"].at(t + 1))
                    turn(s, t, acc[:, t, :])
                end()

                fence(pe, l, "ffn")
                s, n1 = FF[l], LN[l][1]
                u0 = in_unit(l, N_IN + N_OUT)

                def group(i, turned):
                    for a in range(2):
                        pe.wait_ge(w_lo_ready, i * FU + (u0 + a + 1))
                        for j in (2 * a, 2 * a + 1):
                            pe.wait_ge(*s["bank1_free"].at(i * FG + j + 1))
                            feature_tile(u0 + a, (j % 2) * P, l, False, 2 * (j % 2)).then_inc(s["hidden"].sem, 1)
                    for b in range(2):
                        pe.wait_ge(w_lo_ready, i * FU + (u0 + 2 + b + 1))
                        wh, wl = w_view_ff2(w_hi, u0 + b), w_view_ff2(w_lo, u0 + b)
                        for t in range(T):
                            n = b * T + t
                            pe.wait_ge(*s["bank2_free"].at(i * (2 * T) + n + 1))
                            for j in range(FG):
                                if n == 0:
                                    pe.wait_ge(*s["hid_lo"].at(i * FG + j + 3))
                                tk = slice(t * P, (t + 1) * P)
                                ins = products([bank(4 + n % 4)], ([j], lambda k: (hid_hi[:, k, tk], hid_lo[:, k, tk])),
                                               lambda k, c: (wh[:, k, :], wl[:, k, :]), start=j == 0, stop=j == FG - 1)
                            ins.then_inc(s["product"].sem, 1)
                            if turned and b == 1 and t >= 2:
                                pe.wait_ge(*n1["normed"].at(t - 1))
                                turn(n1, t - 2, acc[:, t - 2, :])

                with pe.Fori(0, GROUPS - 1) as i:
                    group(i, False)
                group(GROUPS - 1, l + 1 < DEPTH)
                if l + 1 < DEPTH:
                    for t in range(T - 2, T):
                        pe.wait_ge(*n1["normed"].at(t + 1))
                        turn(n1, t, acc[:, t, :])
                end()


_NAMES = ["x", "c", "ctx", "c_ctx", "w_mod", "b_mod", "w_in", "da_lam_q1", "da_lam_k1", "da_lam_q2", "da_lam_k2",
          "da_subln_g", "mla_q_norm_g", "mla_w_uq", "mla_kv_norm_g", "mla_w_ukv", "na_rpb", "w_out",
          "ln1_g", "ln1_b", "w_ff1", "w_ff2", "ln2_g", "ln2_b"]


def kernel(**inputs):
    import concourse.bacc as _bacc
    from concourse.bass_utils import run_bass_kernel_spmd as _run

    nc = _bacc.Bacc("TRN2", target_bir_lowering=False, num_devices=1)
    arrays, aps = {}, {}
    given = {n: np.ascontiguousarray(inputs[n]) for n in _NAMES}
    given.update(shape_constants())
    for name, a in given.items():
        arrays[f"in_{name}"] = a
        aps[name] = nc.dram_tensor(f"in_{name}", a.shape, mybir.dt.from_np(a.dtype), kind="ExternalInput").ap()
    out = nc.dram_tensor("out_x", (1, SEQ, D), F32, kind="ExternalOutput").ap()
    build(nc, aps, out)
    r = _run(nc, [arrays], core_ids=[0])
    return r.results[0]["out_x"]
```

```python
from contextlib import ExitStack

import numpy as np

import concourse.bass as bass
from concourse import mybir

P = 128
F32 = mybir.dt.float32
F32R = mybir.dt.float32r
ALU = mybir.AluOpType
ACT = mybir.ActivationFunctionType
AX = mybir.AxisListType

D = 1024
DEPTH = 2
GRID_W = 64
SEQ = 512
CTX = 256
ROWS = SEQ // GRID_W
TOK = SEQ + CTX
LT = SEQ // P
NT = TOK // P
KT = D // P
HEADS = 4
HD = 64
DA_V = 2 * HD
ROPE = 32
MQ = HD + ROPE
Q_RANK, KV_RANK = D // 4, D // 8
NA_KH, NA_KW = 8, 16
D_FF = 4 * D
IN_WIDTH = 2720
COL_CQ = 1536
COL_CKV = COL_CQ + Q_RANK
COL_NQ = COL_CKV + KV_RANK + ROPE
ALPHA = (2.0 * DEPTH) ** 0.25
LN_EPS = 1e-6
RMS_EPS = 1e-6
SUBLN_EPS = 1e-5
LAM_INIT = [float(0.8 - 0.6 * np.exp(-0.3 * l)) for l in range(DEPTH)]
MASKED = -1.0e30

UW = 256
UC = KT * UW
IN_UNITS = [(c, min(UW, lim - c)) for lo, lim in ((0, COL_CQ), (COL_CQ, COL_CKV), (COL_CKV, COL_NQ),
                                                  (COL_NQ, IN_WIDTH)) for c in range(lo, lim, UW)]
N_IN = len(IN_UNITS)
N_OUT = D // UW
FG = 4
GF = FG * P
GROUPS = D_FF // GF
FU = 4
N_UNITS = N_IN + N_OUT + GROUPS * FU
WMOD_UNITS = 6 * D // UW
MR = 3
WM_FIRST = 2 * D // UW

V_BMOD, V_G1, V_B1, V_G2, V_B2, V_QN, V_KN, V_C, V_CC, V_ROWS = 0, 48, 56, 64, 72, 80, 82, 83, 91, 99
SHIFT1, SCALE1, GATE1, SHIFT2, SCALE2, GATE2 = (8 * i for i in range(6))
SKEW = 64 * 129


def shape_constants():
    def inv(n):
        return (np.float32(10000.0) ** (np.float32(-2.0) * np.arange(n // 2, dtype=np.float32) / np.float32(n))).astype(np.float32)
    tok = np.arange(SEQ)
    row, col = (tok // GRID_W).astype(np.float32), (tok % GRID_W).astype(np.float32)

    def tables(width, parts):
        n = width // 2
        cos = np.ones((parts, SEQ), np.float32)
        sin = np.zeros((parts, SEQ), np.float32)
        rot = np.zeros((parts, parts), np.float32)
        first = 0 if width == HD else HD
        for d in range(first, parts):
            e = (d - first) % width
            pos = row if e < n else col
            ang = (pos * inv(n)[e % n % (n // 2)]).astype(np.float32)
            cos[d] = np.cos(ang)
            sin[d] = np.sin(ang)
            if e % n < n // 2:
                rot[d + n // 2, d] = -1.0
            else:
                rot[d - n // 2, d] = 1.0
        return cos, sin, rot

    c64, s64, r64 = tables(HD, P)
    c32, s32, r32 = tables(ROPE, MQ)
    q = np.arange(P) % GRID_W
    start = np.clip(q - NA_KW // 2, 0, GRID_W - NA_KW)
    k = np.arange(GRID_W)[None, :]
    inside = (k >= start[:, None]) & (k < start[:, None] + NA_KW)
    mask = np.where(inside, np.float32(0), np.float32(MASKED)).astype(np.float32)
    comb = np.zeros((P, 2), np.float32)
    for j in range(4):
        comb[32 * j, 0] = comb[32 * j + 1, 1] = 1.0
    return {"k_comb": comb, "k_cos64": c64, "k_sin64": s64, "k_rot64": r64, "k_cos32": c32, "k_sin32": s32,
            "k_rot32": r32, "k_mask": mask, "k_ident": np.eye(P, dtype=np.float32)}


def build(nc, A, out):
    ctx = ExitStack()
    with ctx:
        def sb(name, shape, dt=F32):
            return ctx.enter_context(nc.sbuf_tensor(name, shape, dt))

        def sem(name):
            return ctx.enter_context(nc.semaphore(name))

        xt_hi = sb("xt_hi", [P, KT, TOK], F32R)
        xt_lo = sb("xt_lo", [P, KT, TOK], F32R)
        w_raw = sb("w_raw", [P, 2, UC])
        w_hi = sb("w_hi", [P, 2, UC], F32R)
        w_lo = sb("w_lo", [P, 2, UC], F32R)
        hid_hi = sb("hid_hi", [P, FG, TOK], F32R)
        hid_lo = sb("hid_lo", [P, FG, TOK], F32R)
        arena = sb("arena", [P, 20480])
        rot64, rot32 = sb("rot64", [P, P]), sb("rot32", [MQ, MQ])
        ident = sb("ident", [P, P])
        mod_rows = sb("mod_rows", [96, P])
        mask = sb("mask", [P, GRID_W])
        vec = [sb(f"vec{l}", [P, V_ROWS]) for l in range(DEPTH)]
        modv = [sb(f"modv{l}", [P, 48, 2]) for l in range(DEPTH)]
        mod_a = [[sb(f"mod_a{l}{w}", [P, KT, 2]) for w in range(2)] for l in range(DEPTH)]
        mod_b = [[sb(f"mod_b{l}{w}", [P, KT, 2]) for w in range(2)] for l in range(DEPTH)]
        silu = sb("silu", [P, KT, 32])
        comb = sb("comb", [P, 2])
        silu_tmp = sb("silu_tmp", [P, 2, KT])
        neg_lam = [sb(f"neg_lam{l}", [P, 1]) for l in range(DEPTH)]
        lam_tmp = sb("lam_tmp", [P, 4])
        subln = [sb(f"subln{l}", [P, DA_V]) for l in range(DEPTH)]
        att_st = sb("att_st", [P, 6, 12])
        ln_st = sb("ln_st", [P, NT, 17])
        rms_st = sb("rms_st", [P, 2 * NT])
        rms_eps = sb("rms_eps", [P, 2 * NT])
        rms_inv = sb("rms_inv", [P, 2 * NT])
        neg_half = sb("neg_half", [P, 2 * NT])

        def ar(c, *dims, parts=P):
            n = int(np.prod(dims))
            v = arena[0:parts, c:c + n]
            if len(dims) == 2:
                v = v.rearrange("p (a b) -> p a b", b=dims[1])
            if len(dims) == 3:
                v = v.rearrange("p (a b c) -> p a b c", b=dims[1], c=dims[2])
            return v

        x_first, h32_first = ar(0, NT, D), ar(10240, 2, D)
        vrow, lamv, pad, lam_junk = ar(6144, DEPTH, P), ar(6400, 4 * DEPTH, HD), ar(6912, DEPTH, P), ar(7168, HD)
        wm_rings = [ar(12288, MR, KT, UW), ar(3584, MR, KT, UW)]
        mod_row = [[arena[32 * v:32 * v + 2, c:c + D] for v in range(2)] for c in (18432, 9728)]
        wm_parts = [[ar(19456, UW), ar(19712, UW)], [ar(3328, UW)]]
        da_q, da_k, da_v = ar(0, HEADS, TOK), ar(3072, HEADS, TOK), ar(6144, NT, HEADS * DA_V)
        da_raw, da_t = ar(9216, 2, SEQ), ar(10240, 2, SEQ)
        cos64, sin64 = ar(11264, SEQ), ar(11776, SEQ)
        da_p, da_pt, da_y = ar(9216, 2, 2, TOK), [ar(c, TOK) for c in (12288, 13056)], ar(13824, 2, 512)
        da_o, da_junk = ar(14848, 2, 128), ar(15104, 128)
        ml_q, ml_k, ml_v = ar(0, HEADS, TOK, parts=MQ), ar(3072, HEADS, TOK, parts=MQ), ar(6144, NT, 256)
        ml_rows = ar(15232, NT, Q_RANK + KV_RANK + ROPE)
        ml_cq, ml_ckv, ml_kr = ar(7680, 2, TOK), ar(9216, TOK), ar(9984, TOK)
        ml_wq, ml_wkv = ar(10752, 2, HEADS * MQ), ar(11520, 512)
        ml_raw, ml_t, ml_junk = ar(12032, 2, SEQ), ar(13056, 2, SEQ), ar(17728, Q_RANK)
        cos32, sin32 = ar(17728, SEQ, parts=MQ), ar(18240, SEQ, parts=MQ)
        ml_p, ml_pt, ml_diag = ar(7680, 2, 1, TOK), [ar(c, TOK) for c in (9216, 9984, 19456)], ar(10752, 2, P)
        na_bias = ar(11264, HEADS, 14 * GRID_W)
        na_q, na_k, na_v = ar(14848, 2, TOK), ar(16384, 2, TOK), ar(17920, NT, 256)
        na_p, na_pt, na_diag = ar(0, 2, 1, TOK), [ar(c, TOK) for c in (1536, 2304, 19456)], ar(3072, 2, P)
        y_in = ar(10752, 512)
        acc, x_res = ar(0, NT, D), ar(6144, NT, D)
        h32 = ar(12288, 2, D)
        relu, squares = ar(12288, 2, TOK), ar(18432, 2, TOK)
        gain_row = ar(14336, 2, D)
        gate_row = ar(16384, 2, D)

        psum = ctx.enter_context(nc.psum_tensor("psum", [P, 8 * 512], F32))

        def bank(b, n=512, parts=P, at=0):
            return psum[0:parts, b * 512 + at:b * 512 + at + n]

        y_dram = nc.dram_tensor("y_scratch", [NT, P, HEADS * DA_V], F32).ap()
        x_dram = nc.dram_tensor("x_scratch", [NT, P, D], F32).ap()
        mod_dram = nc.dram_tensor("mod_scratch", [DEPTH, 2, 6 * D], F32).ap()
        skew_dram = nc.dram_tensor("skew_scratch", [DEPTH, HEADS * 15, SKEW], F32).ap()

        pe_phase, act_phase, dve_phase, pool_phase = (sem(n) for n in ("pe_phase", "act_phase", "dve_phase", "pool_phase"))
        raw_landed = [sem("raw_landed0"), sem("raw_landed1")]
        w_hi_ready, w_lo_ready = sem("w_hi_ready"), sem("w_lo_ready")
        const_landed, ident_landed, lamv_landed, pad_landed = (sem(n) for n in ("const_landed", "ident_landed", "lamv_landed", "pad_landed"))
        vrow_landed = [sem("vrow_landed0"), sem("vrow_landed1")]
        wm_landed = [sem(f"wm_landed{i}") for i in range(MR)]
        wm_used, parts_copied, wm_summed = sem("wm_used"), sem("parts_copied"), sem("wm_summed")
        out_stored = sem("out_stored")
        first_turned = sem("first_turned")
        pad_zeroed, skew_written = sem("pad_zeroed"), sem("skew_written")
        b_landed, row_added, mod_stored = [sem("b_landed0"), sem("b_landed1")], sem("row_added"), sem("mod_stored")
        vec_turned, silu_exp, silu_ready, vec_ready = sem("vec_turned"), sem("silu_exp"), sem("silu_ready"), sem("vec_ready")
        modv_ready, mod_rows_landed, mod_turned = sem("modv_ready"), sem("mod_rows_landed"), sem("mod_turned")
        lam_dot, lam_exp = sem("lam_dot"), sem("lam_exp")
        dve_step = sem("dve_step")
        act_step = sem("act_step")
        pool_step = sem("pool_step")

        T_Q = [NT if l < DEPTH - 1 else LT for l in range(DEPTH)]

        class Signal:
            def __init__(self, sem, base):
                self.sem, self.base = sem, base

            def at(self, n):
                return self.sem, self.base + n

        semaphores, counted = {}, {}

        def signals(family, **increments):
            of = {}
            for name, n in increments.items():
                key = f"{family}_{name}"
                if key not in semaphores:
                    semaphores[key], counted[key] = sem(key), 0
                of[name] = Signal(semaphores[key], counted[key])
                counted[key] += n
            return of

        def halves(T):
            return 16 * ((T + 1) // 2), 16 * (T // 2)

        def ln_signals(l, w, turned):
            T, final = T_Q[l], l == DEPTH - 1 and w == 1
            n = T if turned else 0
            res = T if l or w else 0
            return signals("ln", **{f"loaded{t}": 16 * (1 - w) for t in range(T)}, gain_landed=64 if final else 32 if res else 0, res_gained=res, res_ready=res,
                           variance=T, rstd=T, stats=T, normed=T, turned=n, h_act=n, h_dve=n, hi=n, lo=n,
                           gate_landed=16 * (2 if T == NT else 1), stored=16 * T * w * (not final), out_gained=T * final, out_ready=T * final)

        X0 = signals("ln", turned=NT, h_act=NT, h_dve=NT, hi=NT, lo=NT)
        x_first_landed = sem("x_first_landed")
        ML_PARTS = {T: [("rows", 6, t) for t in range(T)] + [("rows", 7, t) for t in range(NT)] for T in set(T_Q)}
        NA_PARTS = {T: [("features", u, i, c, n) for u in (8, 9) for i in range(2) for c, n in ((0, SEQ), (SEQ, CTX))
                        if u == 9 or c == 0 or T == NT] + [("rows", 10, t) for t in range(NT)] for T in set(T_Q)}

        VU = D // UW
        def wmod_bank(n):
            return 7 if n >= WMOD_UNITS else 6 + n % 2

        MOD_COLUMNS = [(0, 16, 48), (1, 0, 48)]

        def halves_beside(parts, items, n):
            h = 2 * len(parts)
            return range(n * h // items, (n + 1) * h // items)

        IN, ML, AT, YT, OP, LN, FF, BIAS = [], [], [], [], [], [], [], []
        for T in T_Q:
            a, b = halves(T)
            IN.append([signals("in", tile=8, raw=8, rot=8, done=8, v=2 * NT, v_copied=2 * NT, tables=32, part=0, part_copied=0),
                       signals("in", tile=2 * HEADS, raw=HEADS, rot=HEADS + 1, done=HEADS + 1, v=0, v_copied=0, tables=32, part=T + NT, part_copied=T + NT),
                       signals("in", part=len(NA_PARTS[T]), part_copied=len(NA_PARTS[T]))])
            ML.append(signals("ml", mean_squares=1, rms=1, normed=NT, turned=NT, evacuated=NT, up=HEADS, weights=32, v_ready=NT, v_copied=NT))
            n = HEADS * T
            AT.append([signals("at", scores=k * n, negmax=k * n, probs=k * n, mixed=(k - 1) * n, mean_square=(k - 1) * n, rms=(k - 1) * n, scaled=(2 - k) * n,
                               turned=n, turned_copied=n, mixed_values=n * k // 2, y_hi=(2 - k) * n // 2, y=n * k // 2, y_stored0=(k - 1) * a, y_stored1=(k - 1) * b) for k in (2, 1, 1)])
            BIAS.append(signals("bias", landed=16 * 2 * HEADS, ready=1))
            YT.append(signals("yt", loaded=16 * T, turned=T, hi=T, lo=T))
            OP.append(signals("op", product=N_OUT * T, gated=N_OUT * T))
            LN.append([ln_signals(len(LN), 0, True), ln_signals(len(LN), 1, len(LN) + 1 < DEPTH)])
            FF.append(signals("ff", hidden=GROUPS * FG, bank1_free=2 + GROUPS * FG, hid_hi=GROUPS * FG, hid_lo=2 + GROUPS * FG, squared=GROUPS * FG,
                              product=GROUPS * 2 * T, bank2_free=4 + GROUPS * 2 * T))

        def chunks(l, all_tokens=False):
            return [(0, SEQ), (SEQ, CTX)] if all_tokens or T_Q[l] == NT else [(0, SEQ)]

        phases = {}
        for l in range(DEPTH):
            for name in (["setup"] if l == 0 else []) + ["inA", "atA", "inB", "atB", "atC", "out", "ffn"]:
                phases[(l, name)] = len(phases)

        def fence(eng, l, name):
            n = phases[(l, name)]
            if n:
                for s in (pe_phase, act_phase, dve_phase, pool_phase):
                    eng.wait_ge(s, n)

        def in_unit(l, u):
            return l * N_UNITS + u

        def w_view(t, u, cols=UW):
            return t[:, u % 2, 0:KT * cols].rearrange("p (k n) -> p k n", n=cols)

        def w_view_ff2(t, u):
            return t[:, u % 2, :].rearrange("p (k n) -> p k n", n=512)

        ITEMS = [[(qt, h) for qt in range(T_Q[l]) for h in range(HEADS)] for l in range(DEPTH)]

        def units_ended(parts, items, n):
            return [parts[h // 2][1] for h in halves_beside(parts, items, n)
                    if h % 2 and h // 2 + 1 < len(parts) and parts[h // 2 + 1][1] != parts[h // 2][1]] if n >= 0 else []

        def vec_rows(eng, l):
            for r, src in ((V_C, A["c"][0]), (V_CC, A["c_ctx"]), (V_BMOD, A["b_mod"][l]), (V_G1, A["ln1_g"][l]), (V_B1, A["ln1_b"][l]),
                           (V_G2, A["ln2_g"][l]), (V_B2, A["ln2_b"][l]), (V_QN, A["mla_q_norm_g"][l]), (V_KN, A["mla_kv_norm_g"][l])):
                eng.dma_start(vrow[r:r + src.shape[0] // P, l, :], src.rearrange("(a p) -> a p", p=P)).then_inc(vrow_landed[l], 16)

        block = ctx.enter_context(nc.Block())

        @block.sync
        def _(sp):
            def load(u, dst, src):
                if not isinstance(u, int) or u >= 2:
                    sp.wait_ge(w_lo_ready, u - 1)
                return sp.dma_start(dst, src)

            def projection(l, u):
                g = in_unit(l, u)
                if u < N_IN:
                    c, n = IN_UNITS[u]
                    src = A["w_in"][l, :, c:c + n]
                else:
                    c, n = (u - N_IN) * UW, UW
                    src = A["w_out"][l, :, c:c + n]
                load(g, w_view(w_raw, g, n), src.rearrange("(k p) n -> p k n", p=P)).then_inc(raw_landed[g % 2], 16)

            def b_row(v):
                l, m = v // 6, v % 6
                if v >= 2:
                    sp.wait_ge(mod_stored, 16 * (v - 1))
                if v in (2, 3):
                    sp.wait_ge(first_turned, 2)
                sp.dma_start(mod_row[l][v % 2], A["b_mod"][l, m * D:(m + 1) * D].partition_broadcast(2)).then_inc(b_landed[v % 2], 16)

            def store_row(v):
                l, m = v // 6, v % 6
                sp.wait_ge(row_added, VU * (v + 1))
                if v:
                    sp.wait_ge(mod_stored, 16 * v)
                sp.dma_start(mod_dram[l][:, m * D:(m + 1) * D], mod_row[l][v % 2]).then_inc(mod_stored, 16)

            def wmod(n):
                l, m = n // WMOD_UNITS, n % WMOD_UNITS
                if n % VU == 0 and m >= 2 * VU:
                    b_row(n // VU)
                if n % VU == VU - 1 and m >= 2 * VU - 1 and n != WM_FIRST + VU - 1:
                    store_row(n // VU - 1)
                if n >= MR:
                    sp.wait_ge(wm_used, n - MR + 1)
                sp.dma_start(wm_rings[l][:, n % MR, :, :], A["w_mod"][l, :, m * UW:(m + 1) * UW].rearrange("(k p) n -> p k n", p=P))\
                    .then_inc(wm_landed[n % MR], 16)

            sp.dma_start(ident[:, :], A["k_ident"]).then_inc(ident_landed, 16)
            sp.dma_start(comb[:, :], A["k_comb"]).then_inc(ident_landed, 16)
            vec_rows(sp, 0)
            b_row(0)
            for n in range(MR):
                wmod(n)
            b_row(1)
            projection(0, 0)
            for n in range(MR, WM_FIRST):
                wmod(n)
            projection(0, 1)
            store_row(1)
            projection(0, 2)
            projection(0, 3)
            for n in range(WM_FIRST, WM_FIRST + MR):
                wmod(n)
            for i in range(8):
                wmod(WM_FIRST + MR + i)
                if i % 2:
                    projection(0, 4 + i // 2)
            for i in range(WM_FIRST + MR + 8, WMOD_UNITS):
                wmod(i)
            store_row(5)
            for l in range(DEPTH):
                for u in range(8 if l == 0 else 0, N_IN):
                    projection(l, u)
                projection(l, N_IN)
                projection(l, N_IN + 1)
                if l == 0:
                    fence(sp, 0, "atC")
                    b_row(6)
                    b_row(7)
                    for n in range(WMOD_UNITS, 2 * WMOD_UNITS):
                        wmod(n)
                    store_row(11)
                for u in range(N_IN + 2, N_IN + N_OUT):
                    projection(l, u)
                u0 = in_unit(l, N_IN + N_OUT)
                with sp.Fori(0, GROUPS) as i:
                    for k in range(FU):
                        s = (u0 + k) % 2
                        if k < 2:
                            src = A["w_ff1"][l, :, bass.ds(i * GF + k * UW, UW)].rearrange("(k p) n -> p k n", p=P)
                            dst = w_view(w_raw, s)
                        else:
                            src = A["w_ff2"][l, bass.ds(i * GF, GF), (k - 2) * 512:(k - 1) * 512].rearrange("(k p) n -> p k n", p=P)
                            dst = w_view_ff2(w_raw, s)
                        load(i * FU + (u0 + k), dst, src).then_inc(raw_landed[s], 16)
            s = LN[DEPTH - 1][1]
            for t in range(T_Q[DEPTH - 1]):
                sp.wait_ge(*s["out_ready"].at(t + 1))
                sp.dma_start(out[0, t * P:(t + 1) * P, :], acc[:, t, :]).then_inc(out_stored, 16)
            sp.wait_ge(out_stored, 16 * T_Q[DEPTH - 1])

        @block.gpsimd
        def _(pool):
            def end():
                pool.drain().then_inc(pool_phase, 1)

            pool.memset(pad[:, :, :], 0.0).then_inc(pad_zeroed, 1)
            pool.memset(neg_half[:, :], -0.5).then_inc(pad_zeroed, 1)
            pool.memset(silu[:, :, :], 0.0).then_inc(pad_zeroed, 1)

            vec_rows(pool, 1)
            for t, name in ((rot64, "k_rot64"), (rot32, "k_rot32"), (mask, "k_mask")):
                pool.dma_start(t[:, :], A[name]).then_inc(const_landed, 16)
            pool.wait_ge(pad_zeroed, 3)
            for l in range(DEPTH):
                for i, name in enumerate(("da_lam_q1", "da_lam_k1", "da_lam_q2", "da_lam_k2")):
                    pool.dma_start(lamv[:, 4 * l + i, :], A[name][l].partition_broadcast(P)).then_inc(lamv_landed, 16)
                pool.dma_start(subln[l][:, :], A["da_subln_g"][l].partition_broadcast(P)).then_inc(lamv_landed, 16)
                pool.dma_start(pad[0:HEADS * 15, l, 48:79], A["na_rpb"][l].rearrange("h y x -> (h y) x")).then_inc(pad_landed, 16)
            def skew_tables():
                pool.wait_ge(pad_landed, 16 * DEPTH)
                for l in range(DEPTH):
                    dst = skew_dram[l].rearrange("r (q x) -> r q x", x=129)[:, :, 0:P]
                    src = pad[0:HEADS * 15, l, :].unsqueeze(1).broadcast_to([HEADS * 15, GRID_W, P])
                    pool.dma_start(dst, src).then_inc(skew_written, 16)
                pool.wait_ge(skew_written, 16 * DEPTH)

            def load_mod_rows(i):
                l, first, last = MOD_COLUMNS[i]
                pool.wait_ge(mod_stored, 16 * (6 * l + last // KT))
                for strm in range(2):
                    pool.dma_start(mod_rows[strm * (last - first):(strm + 1) * (last - first), :],
                                   mod_dram[l, strm, first * P:last * P].rearrange("(n p) -> n p", p=P)).then_inc(mod_rows_landed, 16)

            pool.wait_ge(pad_landed, 16 * DEPTH)
            end()

            def store_y(l):
                s = AT[l][0]
                for qt in range(T_Q[l]):
                    for n in range(HEADS * qt, HEADS * (qt + 1)):
                        st = att_st[:, n % 6, :]
                        pool.wait_ge(*s["mean_square"].at(n + 1))
                        pool.tensor_tensor(st[:, 9:10], st[:, 8:9], neg_half[:, 0:1], ALU.pow).then_inc(s["rms"].sem, 1)
                    pool.wait_ge(*s["y"].at(HEADS * (qt + 1)))
                    pool.dma_start(y_dram[qt], da_y[:, qt % 2, :]).then_inc((s["y_stored0"], s["y_stored1"])[qt % 2].sem, 16)
                pool.wait_ge(*ML[l]["mean_squares"].at(1))
                pool.tensor_tensor(rms_inv[:, :], rms_eps[:, :], neg_half[:, :], ALU.pow).then_inc(ML[l]["rms"].sem, 1)
                for i, q in enumerate((s["y_stored0"], s["y_stored1"])):
                    pool.wait_ge(*q.at(16 * len(range(i, T_Q[l], 2))))

            def gain_rows(s, l, w):
                pool.dma_start(gain_row[:, 0, :], A["ln1_g" if w == 0 else "ln2_g"][l].partition_broadcast(P)).then_inc(s["gain_landed"].sem, 16)
                pool.dma_start(gain_row[:, 1, :], A["ln1_b" if w == 0 else "ln2_b"][l].partition_broadcast(P)).then_inc(s["gain_landed"].sem, 16)

            def gate_rows(s, l, w):
                gate = GATE1 if w == 0 else GATE2
                for strm in range(2 if T_Q[l] == NT else 1):
                    pool.dma_start(gate_row[:, strm, :],
                                   mod_dram[l, strm, gate * P:gate * P + D].partition_broadcast(P)).then_inc(s["gate_landed"].sem, 16)

            def residual(s, t, src):
                pool.tensor_tensor(x_res[:, t, :], src[:, t, :], gain_row[:, 0, :], ALU.mult).then_inc(s["res_gained"].sem, 1)
                biased(s, t)

            def biased(s, t):
                pool.wait_ge(*s["res_gained"].at(t + 1))
                pool.tensor_tensor(x_res[:, t, :], x_res[:, t, :], gain_row[:, 1, :], ALU.add).then_inc(s["res_ready"].sem, 1)

            def spread(s, t):
                st = ln_st[:, t, :]
                pool.wait_ge(*s["variance"].at(t + 1))
                pool.tensor_tensor(st[:, 15:16], st[:, 14:15], neg_half[:, 0:1], ALU.pow).then_inc(s["rstd"].sem, 1)
                pool.wait_ge(*s["rstd"].at(t + 1))
                pool.tensor_tensor(st[:, 16:17], st[:, 12:13], st[:, 15:16], ALU.mult).then_inc(s["stats"].sem, 1)

            for l in range(DEPTH):
                fence(pool, l, "inA")
                pool.dma_start(cos64, A["k_cos64"]).then_inc(IN[l][0]["tables"].sem, 16)
                pool.dma_start(sin64, A["k_sin64"]).then_inc(IN[l][0]["tables"].sem, 16)
                if l == 0:
                    skew_tables()
                end()
                fence(pool, l, "atA")
                store_y(l)
                end()
                fence(pool, l, "inB")
                if l == 0:
                    load_mod_rows(0)
                pool.dma_start(ml_wq[:, :, :], A["mla_w_uq"][l].rearrange("(k p) n -> p k n", p=P)).then_inc(ML[l]["weights"].sem, 16)
                pool.dma_start(ml_wkv[:, :], A["mla_w_ukv"][l]).then_inc(ML[l]["weights"].sem, 16)
                pool.dma_start(cos32, A["k_cos32"]).then_inc(IN[l][1]["tables"].sem, 16)
                pool.dma_start(sin32, A["k_sin32"]).then_inc(IN[l][1]["tables"].sem, 16)
                end()
                fence(pool, l, "atB")
                for rr in range(2):
                    for h in range(HEADS):
                        r = h * 15 + 1 - rr
                        src = skew_dram[l, r:r + 14, 63:63 + GRID_W * P].rearrange("j (q k) -> q j k", k=P)[:, :, 0:GRID_W]
                        dst = na_bias[rr * GRID_W:(rr + 1) * GRID_W, h, :].rearrange("p (j k) -> p j k", k=GRID_W)
                        pool.dma_start(dst, src).then_inc(BIAS[l]["landed"].sem, 16)
                pool.wait_ge(*BIAS[l]["landed"].at(16 * 2 * HEADS))
                b3 = na_bias[:, :, :].rearrange("p h (j k) -> p (h j) k", k=GRID_W)
                pool.tensor_tensor(b3, b3, mask[:, :].unsqueeze(1).broadcast_to([P, HEADS * 14, GRID_W]), ALU.add).then_inc(BIAS[l]["ready"].sem, 1)
                end()
                fence(pool, l, "atC")
                for t in range(T_Q[l]):
                    if t:
                        pool.wait_ge(*YT[l]["turned"].at(t))
                    pool.dma_start(y_in, y_dram[t]).then_inc(YT[l]["loaded"].sem, 16)
                if l == 0:
                    pool.wait_ge(mod_stored, 16 * 6 * DEPTH)
                end()
                fence(pool, l, "out")
                s = LN[l][0]
                gate_rows(s, l, 0)
                if l:
                    gain_rows(s, l - 1, 1)
                for t in range(T_Q[l]):
                    src = x_dram[t] if l else A["x"][0, t * P:(t + 1) * P, :] if t < LT else A["ctx"][0, (t - LT) * P:(t - LT + 1) * P, :]
                    pool.dma_start(x_res[:, t, :], src).then_inc(s[f"loaded{t}"].sem, 16)
                if l == 0:
                    load_mod_rows(1)
                else:
                    for t in range(T_Q[l]):
                        biased(s, t)
                for t in range(T_Q[l]):
                    spread(s, t)
                end()
                fence(pool, l, "ffn")
                s = LN[l][1]
                gain_rows(s, l, 0)
                gate_rows(s, l, 1)
                pool.wait_ge(*s["gain_landed"].at(32))
                for t in range(T_Q[l]):
                    residual(s, t, acc)
                if l == DEPTH - 1:
                    pool.wait_ge(*s["res_ready"].at(T_Q[l]))
                    pool.dma_start(gain_row[:, 0, :], A["ln2_g"][l].partition_broadcast(P)).then_inc(s["gain_landed"].sem, 16)
                    pool.dma_start(gain_row[:, 1, :], A["ln2_b"][l].partition_broadcast(P)).then_inc(s["gain_landed"].sem, 16)

                def out_bias(t):
                    pool.wait_ge(*s["out_gained"].at(t + 1))
                    pool.tensor_tensor(acc[:, t, :], acc[:, t, :], gain_row[:, 1, :], ALU.add).then_inc(s["out_ready"].sem, 1)

                for t in range(T_Q[l]):
                    spread(s, t)
                    if l == DEPTH - 1 and t >= 1:
                        out_bias(t - 1)
                if l == DEPTH - 1:
                    out_bias(T_Q[l] - 1)
                    end()
                    continue
                for t in range(T_Q[l]):
                    pool.wait_ge(*s["normed"].at(t + 1))
                    pool.dma_start(x_dram[t], acc[:, t, :]).then_inc(s["stored"].sem, 16)
                pool.wait_ge(*s["stored"].at(16 * T_Q[l]))
                end()

        @block.scalar
        def _(act):
            def end():
                act.drain().then_inc(act_phase, 1)

            def split(u):
                if isinstance(u, int) and u >= DEPTH * N_UNITS:
                    return
                split_at(u % 2, u // 2)

            def split_at(slot, turn):
                act.wait_ge(raw_landed[slot], (turn + 1) * 16)
                act.activation(w_hi[:, slot, :], w_raw[:, slot, :], ACT.Copy).then_inc(w_hi_ready, 1)

            def copy_parts(n):
                buffers = wm_parts[n // WMOD_UNITS]
                act.wait_ge(wm_used, n + 1)
                if n >= len(buffers):
                    act.wait_ge(wm_summed, n + 1 - len(buffers))
                act.activation(buffers[n % len(buffers)], bank(wmod_bank(n), UW), ACT.Copy).then_inc(parts_copied, 1)

            def modulated(s, t, l, w, h):
                strm = 0 if t < LT else 1
                act.wait_ge(*s["turned"].at(t + 1))
                if t >= 2:
                    act.wait_ge(*s["lo"].at(t - 1))
                for k in range(4):
                    i = act.activation(h[:, t % 2, k * P:(k + 1) * P], bank(2 * (t % 2), P, at=k * P), ACT.Identity,
                                       bias=mod_b[l][w][:, k, strm:strm + 1], scale=mod_a[l][w][:, k, strm:strm + 1])
                i.then_inc(s["h_act"].sem, 1)
                act.wait_ge(*s["h_act"].at(t + 1))
                act.wait_ge(*s["h_dve"].at(t + 1))
                act.activation(xt_hi[:, :, t * P:(t + 1) * P], h[:, t % 2, :].rearrange("p (k n) -> p k n", n=P), ACT.Copy).then_inc(s["hi"].sem, 1)

            act.wait_ge(vrow_landed[0], 16 * 9)
            for t in range(NT):
                src = A["x"][0, t * P:(t + 1) * P, :] if t < LT else A["ctx"][0, (t - LT) * P:(t - LT + 1) * P, :]
                act.dma_start(x_first[:, t, :], src).then_inc(x_first_landed, 16)
            act.wait_ge(vec_ready, 1)
            act.activation(silu_tmp[:, :, :], vec[0][:, V_C:V_ROWS].rearrange("p (s k) -> p s k", k=KT), ACT.Exp, scale=-1.0).then_inc(silu_exp, 1)
            for n in range(WM_FIRST):
                copy_parts(n)
                if n in (3, 5):
                    split(n // 2 - 1)
            for l in range(DEPTH):
                act.wait_ge(lam_dot, l + 1)
                act.activation(lam_tmp[:, 2 * l:2 * l + 2], lam_tmp[:, 2 * l:2 * l + 2], ACT.Exp).then_inc(lam_exp, 1)
            act.wait_ge(modv_ready, 1)
            for t in range(NT):
                modulated(X0, t, 0, 0, h32_first)
            end()

            def in_tile(s, i, psum_bank, parts, raw, dst, scale, ctx_too):
                act.wait_ge(*s["tile"].at(i + 1))
                if i >= 2:
                    act.wait_ge(*s["done"].at(i - 1))
                if ctx_too:
                    act.activation(dst[:, SEQ:TOK], bank(psum_bank + 1, CTX, parts), ACT.Copy, scale=scale)
                act.activation(raw[0:parts, i % 2, :], bank(psum_bank, SEQ, parts), ACT.Copy, scale=scale).then_inc(s["raw"].sem, 1)

            def beside(l, g, parts, n):
                s = IN[l][g] if parts else None
                for h in halves_beside(parts, len(ITEMS[l]), n):
                    if h % 2 == 0:
                        continue
                    kind, u, i = parts[h // 2][:3]
                    act.wait_ge(*s["part"].at(h // 2 + 1))
                    if kind == "features":
                        c, w = parts[h // 2][3:]
                        dst, sc = (na_q, HD ** -0.5) if u == 8 else (na_k, 1.0)
                        act.activation(dst[:, i, c:c + w], bank(7, w), ACT.Copy, scale=sc).then_inc(s["part_copied"].sem, 1)
                    else:
                        w = IN_UNITS[u][1]
                        dst = ml_rows[:, i, 0:w] if u == 6 else ml_rows[:, i, Q_RANK:Q_RANK + w] if u == 7 else na_v[:, i, :]
                        act.activation(dst, bank(7, w), ACT.Copy).then_inc(s["part_copied"].sem, 1)
                if parts:
                    for u in units_ended(parts, len(ITEMS[l]), n):
                        split(in_unit(l, u + 2))

            def attention(l, g, nmaps, p, pt, parts, y_hi=None):
                s = AT[l][g]
                items = ITEMS[l]

                def exps(n):
                    qt, h = items[n]
                    st = att_st[:, n % 6, :]
                    nk = TOK if qt < LT else CTX
                    if n >= 2:
                        act.wait_ge(*s["turned"].at(n - 1))
                    for m in range(nmaps):
                        act.wait_ge(*s["negmax"].at(n * nmaps + m + 1))
                        b = 2 * m if nmaps == 2 else 2 * (n % 2)
                        if g == 2 and qt < LT:
                            act.activation(p[:, n % 2, 0, 0:SEQ], p[:, n % 2, 0, 0:SEQ], ACT.Exp, bias=st[:, 0:1], accum_out=st[:, 2:3])
                            act.activation(p[:, n % 2, 0, SEQ:TOK], bank(b + 1, CTX), ACT.Exp, bias=st[:, 0:1],
                                           accum_out=st[:, 3:4]).then_inc(s["probs"].sem, 1)
                        else:
                            act.activation(p[:, n % 2, m, 0:nk], bank(b, nk), ACT.Exp, bias=st[:, m:m + 1],
                                           accum_out=st[:, 2 + m:3 + m]).then_inc(s["probs"].sem, 1)

                def turned_copy(n):
                    nk = TOK if items[n][0] < LT else CTX
                    act.wait_ge(*s["turned"].at(n + 1))
                    if n >= len(pt):
                        act.wait_ge(*s["mixed_values"].at(n - 1 if nmaps == 2 else (n - 3) // 2 + 1))
                    act.activation(pt[n % len(pt)][:, 0:nk], bank(4, nk), ACT.Copy).then_inc(s["turned_copied"].sem, 1)

                def values_high(n):
                    qt, h = items[n]
                    act.wait_ge(*s["mixed_values"].at(n // 2 + 1))
                    act.activation(y_hi[:, h // 2, qt * P:(qt + 1) * P], bank(6, P), ACT.Copy).then_inc(s["y_hi"].sem, 1)

                lead = 1 if nmaps == 2 else 2
                for n in range(lead):
                    exps(n)
                if lead == 2:
                    turned_copy(0)
                for n in range(len(items)):
                    if n + lead < len(items):
                        exps(n + lead)
                    if g == 2 and n % HEADS == 1:
                        t = n // HEADS
                        act.wait_ge(*YT[l]["turned"].at(t + 1))
                        act.activation(xt_hi[:, 0:4, t * P:(t + 1) * P], bank(7).rearrange("p (k n) -> p k n", n=P), ACT.Copy).then_inc(YT[l]["hi"].sem, 1)
                    if n + lead - 1 < len(items):
                        turned_copy(n + lead - 1)
                    beside(l, g + 1, parts, n)
                    if g == 2 and n == 1:
                        split(in_unit(l, 12))
                    if g == 2 and l == 0:
                        copy_parts(WMOD_UNITS + n)
                    if nmaps == 1 and n % 2:
                        values_high(n)

            def norm(s, t):
                act.wait_ge(*s["stats"].at(t + 1))
                act.activation(acc[:, t, :], acc[:, t, :], ACT.Identity, bias=ln_st[:, t, 16:17], scale=ln_st[:, t, 15:16]).then_inc(s["normed"].sem, 1)

            for l in range(DEPTH):
                q_ctx = T_Q[l] == NT
                T = T_Q[l]
                fence(act, l, "inA")
                s = IN[l][0]
                if l:
                    split(in_unit(l, 1))
                for i in range(8):
                    dst = da_q[:, i, :] if i < HEADS else da_k[:, i - HEADS, :]
                    in_tile(s, i, 2 * (i % 2), P, da_raw, dst, HD ** -0.5 if i < HEADS else 1.0, i >= HEADS or q_ctx)
                    if l == 0:
                        copy_parts(WM_FIRST + i)
                    if i % 2:
                        split(in_unit(l, i // 2 + 2))
                if l == 0:
                    act.wait_ge(skew_written, 16 * DEPTH)
                for u in range(2):
                    for t in range(NT):
                        act.wait_ge(*s["v"].at(u * NT + t + 1))
                        act.activation(da_v[:, t, u * UW:(u + 1) * UW], bank(4 + t % 2, UW), ACT.Copy).then_inc(s["v_copied"].sem, 1)
                        if l == 0 and WM_FIRST + 8 + u * NT + t < WMOD_UNITS:
                            copy_parts(WM_FIRST + 8 + u * NT + t)
                    split(in_unit(l, 4 + u + 2))
                end()
                fence(act, l, "atA")
                attention(l, 0, 2, da_p, da_pt, ML_PARTS[T])
                end()

                fence(act, l, "inB")
                s, m = IN[l][1], ML[l]
                split(in_unit(l, 9))
                for t in range(NT):
                    act.wait_ge(*m["turned"].at(t + 1))
                    b = 4 + t % 2
                    tk = slice(t * P, (t + 1) * P)
                    if t < T:
                        for k in range(2):
                            act.activation(ml_cq[:, k, tk], bank(b, P, at=k * P), ACT.Copy, scale=vec[l][:, V_QN + k:V_QN + k + 1])
                    act.activation(ml_kr[HD:MQ, tk], psum[HD:MQ, b * 512 + 3 * P:b * 512 + 4 * P], ACT.Copy)
                    act.activation(ml_ckv[:, tk], bank(b, P, at=2 * P), ACT.Copy, scale=vec[l][:, V_KN:V_KN + 1]).then_inc(m["evacuated"].sem, 1)
                for h in range(HEADS):
                    in_tile(s, h, 2 * (h % 2), MQ, ml_raw, ml_q[:, h, :], MQ ** -0.5, q_ctx)
                for h in range(HEADS):
                    act.wait_ge(*s["tile"].at(HEADS + h + 1))
                    b = 2 * (h % 2)
                    act.activation(ml_k[0:HD, h, :], psum[0:HD, b * 512:b * 512 + TOK], ACT.Copy).then_inc(m["up"].sem, 1)
                for t in range(NT):
                    act.wait_ge(*m["v_ready"].at(t + 1))
                    act.activation(ml_v[:, t, :], bank(6 + t % 2, 256), ACT.Copy).then_inc(m["v_copied"].sem, 1)
                act.wait_ge(*s["done"].at(HEADS + 1))
                for h in range(HEADS):
                    act.activation(ml_k[HD:MQ, h, SEQ:TOK], ml_kr[HD:MQ, SEQ:TOK], ACT.Copy)
                    act.activation(ml_k[HD:MQ, h, 0:SEQ], ml_t[HD:MQ, 0, :], ACT.Copy)
                end()
                fence(act, l, "atB")
                attention(l, 1, 1, ml_p, ml_pt, NA_PARTS[T], hid_hi)
                end()
                fence(act, l, "atC")
                attention(l, 2, 1, na_p, na_pt, [], xt_hi[:, 6:8, :])
                end()

                fence(act, l, "out")
                s = LN[l][0]
                for u in range(N_OUT - 1):
                    act.wait_ge(*OP[l]["product"].at((u + 1) * T))
                    split(in_unit(l, N_IN + u + 2))
                for t in range(T):
                    norm(s, t)
                    if t >= 2:
                        modulated(s, t - 2, l, 1, h32)
                for t in range(T - 2, T):
                    modulated(s, t, l, 1, h32)
                end()

                fence(act, l, "ffn")
                s = FF[l]
                tokens = T * P
                u0 = in_unit(l, N_IN + N_OUT)
                act.drain().then_inc(s["bank1_free"].sem, 2)
                split(in_unit(l, N_IN + N_OUT + 1))

                def hidden(i):
                    for a in range(2):
                        for j in (2 * a, 2 * a + 1):
                            act.wait_ge(*s["hidden"].at(i * FG + j + 1))
                            act.wait_ge(*s["hid_lo"].at(i * FG + j + 1))
                            act.activation(relu[:, j % 2, 0:tokens], bank(2 * (j % 2), tokens), ACT.Relu).then_inc(s["bank1_free"].sem, 1)
                            act.wait_ge(*s["bank1_free"].at(i * FG + j + 3))
                            act.activation(hid_hi[:, j, 0:tokens], relu[:, j % 2, 0:tokens], ACT.Square).then_inc(s["hid_hi"].sem, 1)
                        u = u0 + a + 2
                        split_at(u % 2, i * 2 + u // 2)

                def second(i, b):
                    act.wait_ge(*s["product"].at(i * (2 * T) + (b + 1) * T))
                    u = u0 + 2 + b + 2
                    split_at(u % 2, i * 2 + u // 2)

                with act.Fori(0, GROUPS - 1) as i:
                    hidden(i)
                    second(i, 0)
                    second(i, 1)
                hidden(GROUPS - 1)
                n = LN[l][1]
                if l + 1 < DEPTH:
                    second(GROUPS - 1, 0)
                    for t in range(T):
                        norm(n, t)
                        if t >= 2:
                            modulated(n, t - 2, l + 1, 0, h32)
                    for t in range(T - 2, T):
                        modulated(n, t, l + 1, 0, h32)
                else:
                    for t in range(T):
                        norm(n, t)
                end()

        @block.vector
        def _(dve):
            def end():
                dve.drain().then_inc(dve_phase, 1)

            steps = [0]

            def link(ins):
                steps[0] += 1
                ins.then_inc(dve_step, 1)
                dve.wait_ge(dve_step, steps[0])

            def split(u):
                if isinstance(u, int) and u >= DEPTH * N_UNITS:
                    return
                split_at(u, u % 2)

            def split_at(u, slot):
                dve.wait_ge(w_hi_ready, u + 1)
                dve.tensor_tensor(w_lo[:, slot, :], w_raw[:, slot, :], w_hi[:, slot, :].bitcast(F32), ALU.subtract).then_inc(w_lo_ready, 1)

            def add_row(n):
                l, v = n // WMOD_UNITS, n // VU
                dve.wait_ge(wm_summed, n + 1)
                if n % VU == 0:
                    dve.wait_ge(b_landed[v % 2], 16 * (v // 2 + 1))
                dst = mod_row[l][v % 2][:, n % VU * UW:(n % VU + 1) * UW]
                r = 32 * (v % 2)
                dve.tensor_tensor(dst, psum[r:r + 2, wmod_bank(n) * 512 + UW:wmod_bank(n) * 512 + 2 * UW], dst, ALU.add).then_inc(row_added, 1)

            def modulation(i, b):
                l, first, last = MOD_COLUMNS[i]
                dve.wait_ge(mod_turned, i + 1)
                link(dve.tensor_copy(modv[l][:, first:last, :], bank(b, 2 * (last - first)).rearrange("p (s n) -> p n s", s=2)))

            def factors(l, w):
                sh, sc = (SHIFT1, SCALE1) if w == 0 else (SHIFT2, SCALE2)
                a, b = mod_a[l][w], mod_b[l][w]
                link(dve.tensor_scalar(a[:, :, :], modv[l][:, sc:sc + KT, :], 1.0, None, ALU.add))
                if w == 0 and l == 0:
                    dve.tensor_copy(b[:, :, :], modv[l][:, sh:sh + KT, :]).then_inc(modv_ready, 1)
                    dve.wait_ge(modv_ready, 1)
                    return
                v, g0, b0 = (vec[l], V_G1, V_B1) if w == 1 else (vec[l - 1], V_G2, V_B2)
                link(dve.tensor_tensor(b[:, :, :], a[:, :, :], v[:, b0:b0 + KT].unsqueeze(2).broadcast_to([P, KT, 2]), ALU.mult))
                link(dve.tensor_tensor(b[:, :, :], b[:, :, :], modv[l][:, sh:sh + KT, :], ALU.add))
                link(dve.tensor_tensor(a[:, :, :], a[:, :, :], v[:, g0:g0 + KT].unsqueeze(2).broadcast_to([P, KT, 2]), ALU.mult))

            def modulated(s, t, l, w, h):
                strm = 0 if t < LT else 1
                dve.wait_ge(*s["turned"].at(t + 1))
                if t >= 2:
                    dve.wait_ge(*s["lo"].at(t - 1))
                for k in range(4, 8):
                    i = dve.tensor_scalar(h[:, t % 2, k * P:(k + 1) * P], bank(2 * (t % 2) + 1, P, at=(k - 4) * P),
                                          mod_a[l][w][:, k, strm:strm + 1], mod_b[l][w][:, k, strm:strm + 1], ALU.mult, ALU.add)
                i.then_inc(s["h_dve"].sem, 1)

            def low(s, t, h):
                dve.wait_ge(*s["hi"].at(t + 1))
                tk = slice(t * P, (t + 1) * P)
                dve.tensor_tensor(xt_lo[:, :, tk], h[:, t % 2, :].rearrange("p (k n) -> p k n", n=P),
                                  xt_hi[:, :, tk].bitcast(F32), ALU.subtract).then_inc(s["lo"].sem, 1)

            dve.memset(rms_st[:, :], 1.0)
            dve.wait_ge(vec_turned, 1)
            dve.tensor_copy(vec[0][:, :], bank(4, V_ROWS)).then_inc(vec_ready, 1)
            dve.wait_ge(silu_exp, 1)
            link(dve.tensor_scalar(silu_tmp[:, :, :], silu_tmp[:, :, :], 1.0, None, ALU.add))
            link(dve.reciprocal(silu_tmp[:, :, :], silu_tmp[:, :, :]))
            dve.wait_ge(pad_zeroed, 3)
            dve.tensor_tensor(silu[:, :, 0:2].rearrange("p k s -> p s k"), vec[0][:, V_C:V_ROWS].rearrange("p (s k) -> p s k", k=KT), silu_tmp[:, :, :],
                              ALU.mult).then_inc(silu_ready, 1)
            for n in range(WM_FIRST):
                add_row(n)
                if n in (4, 6):
                    split(n // 2 - 2)
            dve.wait_ge(lamv_landed, 16 * 5 * DEPTH)
            for l in range(DEPTH):
                link(dve.tensor_tensor_reduce(lam_junk, lamv[:, 4 * l, :], lamv[:, 4 * l + 1, :], 1.0, 0.0, ALU.mult, ALU.add, lam_tmp[:, 2 * l:2 * l + 1]))
                dve.tensor_tensor_reduce(lam_junk, lamv[:, 4 * l + 2, :], lamv[:, 4 * l + 3, :], 1.0, 0.0, ALU.mult, ALU.add, lam_tmp[:, 2 * l + 1:2 * l + 2]).then_inc(lam_dot, 1)
                dve.wait_ge(lam_dot, l + 1)
                dve.tensor_scalar(subln[l][:, :], subln[l][:, :], 1.0 - LAM_INIT[l], None, ALU.mult)
            for l in range(DEPTH):
                dve.wait_ge(lam_exp, l + 1)
                link(dve.tensor_tensor(neg_lam[l][:, :], lam_tmp[:, 2 * l + 1:2 * l + 2], lam_tmp[:, 2 * l:2 * l + 1], ALU.subtract))
                link(dve.tensor_scalar(neg_lam[l][:, :], neg_lam[l][:, :], LAM_INIT[l], None, ALU.subtract))
            dve.wait_ge(first_turned, 2)
            for v in range(2):
                link(dve.tensor_copy(modv[0][:, v * KT:(v + 1) * KT, :], bank(4 + v, 2 * KT).rearrange("p (n s) -> p n s", s=2)))
            factors(0, 0)
            for t in range(NT):
                modulated(X0, t, 0, 0, h32_first)
                if t >= 1:
                    low(X0, t - 1, h32_first)
            low(X0, NT - 1, h32_first)
            dve.wait_ge(vec_turned, DEPTH)
            dve.tensor_copy(vec[1][:, :], bank(7, V_ROWS)).then_inc(vec_ready, 1)
            end()

            def rotate(s, i, rot_bank, parts, lo, raw, tmp, dst, cos, sin):
                r = slice(lo, parts)
                dve.wait_ge(*s["raw"].at(i + 1))
                if i >= 1:
                    dve.wait_ge(*s["done"].at(i))
                dve.tensor_tensor(tmp[r, 0, :], raw[r, i % 2, :], cos[r, :], ALU.mult)
                dve.wait_ge(*s["rot"].at(i + 1))
                link(dve.tensor_tensor(tmp[r, 1, :], psum[r, rot_bank * 512:rot_bank * 512 + SEQ], sin[r, :], ALU.mult))
                dve.tensor_tensor(dst, tmp[r, 0, :], tmp[r, 1, :], ALU.add).then_inc(s["done"].sem, 1)

            def mean_squares(l, n):
                parts = ML_PARTS[T_Q[l]]
                for h in halves_beside(parts, len(ITEMS[l]), n):
                    if h % 2:
                        _, u, t = parts[h // 2]
                        k, c, w = (0, 0, Q_RANK) if u == 6 else (1, Q_RANK, KV_RANK)
                        dve.wait_ge(*IN[l][1]["part_copied"].at(h // 2 + 1))
                        r = ml_rows[:, t, c:c + w]
                        link(dve.tensor_tensor_reduce(ml_junk[:, 0:w], r, r, 1.0 / w, 0.0, ALU.mult, ALU.add, rms_st[:, k * NT + t:k * NT + t + 1]))

            def split_quarter(u, c):
                if c == 0:
                    dve.wait_ge(w_hi_ready, u + 1)
                cols = slice(c * UC // 4, (c + 1) * UC // 4)
                ins = dve.tensor_tensor(w_lo[:, u % 2, cols], w_raw[:, u % 2, cols], w_hi[:, u % 2, cols].bitcast(F32), ALU.subtract)
                if c == 3:
                    ins.then_inc(w_lo_ready, 1)

            def beside(l, g, parts, n):
                for c in range(4):
                    for u in units_ended(parts, len(ITEMS[l]), n - 1 - c):
                        split_quarter(in_unit(l, u + 2), c)
                if g == 2 and 2 <= n < 6:
                    split_quarter(in_unit(l, 12), n - 2)

            def attention(l, g, nmaps, p, y, bias, parts, diag=None, y_hi=None, y_lo=None):
                s = AT[l][g]
                items = ITEMS[l]

                def maxima(n):
                    qt, h = items[n]
                    nk = TOK if qt < LT else CTX
                    st = att_st[:, n % 6, :]
                    for m in range(nmaps):
                        dve.wait_ge(*s["scores"].at(n * nmaps + m + 1))
                        b = 2 * m if nmaps == 2 else 2 * (n % 2)
                        if bias is not None and qt < LT:
                            if n >= 2:
                                dve.wait_ge(*s["turned"].at(n - 1))
                            j = (6 - 2 * qt) * GRID_W
                            dve.tensor_tensor_reduce(p[:, n % 2, 0, 0:SEQ], bank(b, SEQ), bias[:, h, j:j + SEQ], 1.0, 3.0 * MASKED,
                                                     ALU.add, ALU.max, st[:, 8:9])
                            link(dve.tensor_reduce(st[:, 9:10], bank(b + 1, CTX), AX.X, ALU.max))
                            dve.tensor_scalar(st[:, 0:1], st[:, 8:9], st[:, 9:10], -1.0, ALU.max, ALU.mult).then_inc(s["negmax"].sem, 1)
                        else:
                            dve.tensor_reduce(st[:, m:m + 1], bank(b, nk), AX.X, ALU.max, negate=True).then_inc(s["negmax"].sem, 1)

                def mix(n):
                    qt, h = items[n]
                    nk = TOK if qt < LT else CTX
                    st = att_st[:, n % 6, :]
                    dve.wait_ge(*s["probs"].at(2 * n + 2))
                    link(dve.reciprocal(st[:, 4:5], st[:, 3:4]))
                    link(dve.tensor_scalar(st[:, 5:6], st[:, 2:3], st[:, 4:5], neg_lam[l][:, 0:1], ALU.mult, ALU.mult))
                    dve.scalar_tensor_tensor(out=p[:, n % 2, 0, 0:nk], in0=p[:, n % 2, 1, 0:nk], scalar=st[:, 5:6],
                                             in1=p[:, n % 2, 0, 0:nk], op0=ALU.mult, op1=ALU.add).then_inc(s["mixed"].sem, 1)

                def scale(n):
                    qt, h = items[n]
                    st = att_st[:, n % 6, :]
                    dve.wait_ge(*s["probs"].at(n + 1))
                    if n >= 2:
                        dve.wait_ge(*s["turned"].at(n - 1))
                    if bias is not None and qt < LT:
                        link(dve.tensor_tensor(st[:, 2:3], st[:, 2:3], st[:, 3:4], ALU.add))
                    link(dve.reciprocal(st[:, 6:7], st[:, 2:3]))
                    dve.tensor_scalar(diag[:, n % 2, :], ident[:, :], st[:, 6:7], None, ALU.mult).then_inc(s["scaled"].sem, 1)

                def values_low(n):
                    qt, h = items[n]
                    dve.wait_ge(*s["y_hi"].at(n // 2 + 1))
                    cols = slice(qt * P, (qt + 1) * P)
                    dve.tensor_tensor(y_lo[:, h // 2, cols], bank(6, P), y_hi[:, h // 2, cols].bitcast(F32), ALU.subtract).then_inc(s["y"].sem, 1)

                def finish(n):
                    st = att_st[:, n % 6, :]
                    dve.wait_ge(*s["probs"].at(2 * n + 2))
                    link(dve.reciprocal(st[:, 6:7], st[:, 2:3]))
                    dve.wait_ge(*s["mixed_values"].at(n + 1))
                    oh = da_o[:, n % 2, :]
                    if n >= 2:
                        dve.wait_ge(*s["y"].at(n - 1))
                    link(dve.tensor_scalar(oh, bank(6, DA_V), st[:, 6:7], None, ALU.mult))
                    link(dve.tensor_tensor_reduce(da_junk, oh, oh, 1.0 / DA_V, 0.0, ALU.mult, ALU.add, st[:, 7:8]))
                    dve.tensor_scalar(st[:, 8:9], st[:, 7:8], SUBLN_EPS, None, ALU.add).then_inc(s["mean_square"].sem, 1)

                def sub_norm(n):
                    qt, h = items[n]
                    dve.wait_ge(*s["rms"].at(n + 1))
                    if h == 0 and qt >= 2:
                        dve.wait_ge(*(s["y_stored0"], s["y_stored1"])[qt % 2].at(16 * (qt // 2)))
                    dve.scalar_tensor_tensor(out=y[:, qt % 2, h * DA_V:(h + 1) * DA_V], in0=da_o[:, n % 2, :], scalar=att_st[:, n % 6, 9:10],
                                             in1=subln[l][:, :], op0=ALU.mult, op1=ALU.mult).then_inc(s["y"].sem, 1)

                if nmaps == 2:
                    maxima(0)
                    for n in range(len(items) + 1):
                        if n < len(items):
                            mix(n)
                        if n >= 1:
                            mean_squares(l, n - 1)
                        if n + 1 < len(items):
                            maxima(n + 1)
                        if n >= 2:
                            sub_norm(n - 2)
                        if n >= 1:
                            finish(n - 1)
                        if n < len(items):
                            beside(l, g, parts, n)
                    sub_norm(len(items) - 1)
                else:
                    for n in range(3):
                        maxima(n)
                        if n < 2:
                            scale(n)
                    for n in range(len(items)):
                        if g == 2 and l == 0 and n:
                            add_row(WMOD_UNITS + n - 1)
                        if n + 2 < len(items):
                            scale(n + 2)
                        if g == 2 and n % HEADS == 1:
                            t = n // HEADS
                            dve.wait_ge(*YT[l]["hi"].at(t + 1))
                            tk = slice(t * P, (t + 1) * P)
                            dve.tensor_tensor(xt_lo[:, 0:4, tk], bank(7).rearrange("p (k n) -> p k n", n=P), xt_hi[:, 0:4, tk].bitcast(F32),
                                              ALU.subtract).then_inc(YT[l]["lo"].sem, 1)
                        if n + 3 < len(items):
                            maxima(n + 3)
                        if n % 2:
                            values_low(n)
                        beside(l, g, parts, n)
                    if g == 2 and l == 0:
                        add_row(2 * WMOD_UNITS - 1)

            def norm_rows(l, n_q):
                m = ML[l]
                parts = [(k, c, w, t) for t in range(NT) for k, c, w in ((0, 0, Q_RANK), (1, Q_RANK, KV_RANK)) if k or t < n_q]
                dve.wait_ge(*m["rms"].at(1))
                for k, c, w, t in parts:
                    r = ml_rows[:, t, c:c + w]
                    ins = dve.tensor_scalar(r, r, rms_inv[:, k * NT + t:k * NT + t + 1], None, ALU.mult)
                    if k:
                        ins.then_inc(m["normed"].sem, 1)

            def last_tiles(s, T, l, w):
                for t in range(T - 2, T):
                    modulated(s, t, l, w, h32)
                    low(s, t - 1, h32)
                low(s, T - 1, h32)

            def half_stats(t, k):
                link(dve.bn_stats(ln_st[:, t, 6 * k:6 * k + 6], acc[:, t, k * 512:(k + 1) * 512]))

            def variance(s, t):
                st = ln_st[:, t, :]
                link(dve.bn_aggr(st[:, 12:14], st[:, 0:12]))
                dve.tensor_scalar(st[:, 12:13], st[:, 12:13], -1.0, None, ALU.mult)
                dve.tensor_scalar(st[:, 14:15], st[:, 13:14], LN_EPS, None, ALU.add).then_inc(s["variance"].sem, 1)

            for l in range(DEPTH):
                T = T_Q[l]
                fence(dve, l, "inA")
                s = IN[l][0]
                if l:
                    split(in_unit(l, 1))
                dve.wait_ge(*s["tables"].at(32))
                for i in range(8):
                    dst = da_q[:, i, 0:SEQ] if i < HEADS else da_k[:, i - HEADS, 0:SEQ]
                    rotate(s, i, 4 + i % 2, P, 0, da_raw, da_t, dst, cos64, sin64)
                    if l == 0:
                        add_row(WM_FIRST + i)
                    if i % 2:
                        split(in_unit(l, i // 2 + 2))
                for n in range(2 * NT):
                    if l == 0 and WM_FIRST + 8 + n < WMOD_UNITS:
                        add_row(WM_FIRST + 8 + n)
                    if n % NT == NT - 1:
                        split(in_unit(l, 4 + n // NT + 2))
                end()
                fence(dve, l, "atA")
                attention(l, 0, 2, da_p, da_y, None, ML_PARTS[T])
                dve.tensor_scalar(rms_eps[:, :], rms_st[:, :], RMS_EPS, None, ALU.add).then_inc(ML[l]["mean_squares"].sem, 1)
                end()

                fence(dve, l, "inB")
                s, m = IN[l][1], ML[l]
                norm_rows(l, T)
                split(in_unit(l, 9))
                if l == 0:
                    modulation(0, 7)
                    factors(0, 1)
                dve.wait_ge(*s["tables"].at(32))
                for h in range(HEADS):
                    rotate(s, h, 4 + h % 2, MQ, 0, ml_raw, ml_t, ml_q[:, h, 0:SEQ], cos32, sin32)
                dve.wait_ge(*s["rot"].at(HEADS + 1))
                dve.wait_ge(*s["done"].at(HEADS))
                r = slice(HD, MQ)
                dve.tensor_tensor(ml_t[r, 0, :], ml_kr[r, 0:SEQ], cos32[r, :], ALU.mult)
                link(dve.tensor_tensor(ml_t[r, 1, :], psum[r, 4 * 512:5 * 512], sin32[r, :], ALU.mult))
                dve.tensor_tensor(ml_t[r, 0, :], ml_t[r, 0, :], ml_t[r, 1, :], ALU.add).then_inc(s["done"].sem, 1)
                end()
                fence(dve, l, "atB")
                attention(l, 1, 1, ml_p, None, None, NA_PARTS[T], ml_diag, hid_hi, hid_lo)
                end()

                fence(dve, l, "atC")
                dve.wait_ge(*BIAS[l]["ready"].at(1))
                attention(l, 2, 1, na_p, None, na_bias, [], na_diag, xt_hi[:, 6:8, :], xt_lo[:, 6:8, :])
                end()

                fence(dve, l, "out")
                s = LN[l][0]
                dve.wait_ge(*s["gate_landed"].at(16 * (2 if T == NT else 1)))
                if l:
                    dve.wait_ge(*s["gain_landed"].at(32))
                    for t in range(T):
                        dve.wait_ge(*s[f"loaded{t}"].at(16))
                        dve.tensor_tensor(x_res[:, t, :], x_res[:, t, :], gain_row[:, 0, :], ALU.mult).then_inc(s["res_gained"].sem, 1)
                for u in range(N_OUT):
                    for t in range(T):
                        n = u * T + t
                        cols = slice(u * UW, (u + 1) * UW)
                        dve.wait_ge(*OP[l]["product"].at(n + 1))
                        dve.tensor_tensor(acc[:, t, cols], bank(4 + n % 4, UW), gate_row[:, 0 if t < LT else 1, cols], ALU.mult).then_inc(OP[l]["gated"].sem, 1)
                        if u == 0:
                            dve.wait_ge(*(s["res_ready"].at(t + 1) if l else s[f"loaded{t}"].at(16)))
                        dve.wait_ge(*OP[l]["gated"].at(n + 1))
                        ins = dve.scalar_tensor_tensor(out=acc[:, t, cols], in0=x_res[:, t, cols], scalar=ALPHA, in1=acc[:, t, cols], op0=ALU.mult, op1=ALU.add)
                        if u % 2:
                            link(ins)
                            half_stats(t, u // 2)
                        if u == N_OUT - 1:
                            variance(s, t)
                            if t >= 2:
                                modulated(s, t - 2, l, 1, h32)
                            if t >= 3:
                                low(s, t - 3, h32)
                    if u < N_OUT - 1:
                        split(in_unit(l, N_IN + u + 2))
                last_tiles(s, T, l, 1)
                end()

                fence(dve, l, "ffn")
                s, n1 = FF[l], LN[l][1]
                tokens = T * P
                u0 = in_unit(l, N_IN + N_OUT)
                dve.drain().then_inc(s["hid_lo"].sem, 2)
                split(in_unit(l, N_IN + N_OUT + 1))
                if l == 0:
                    modulation(1, 7)
                    factors(1, 0)
                    factors(1, 1)
                dve.drain().then_inc(s["bank2_free"].sem, 4)

                def hidden(i):
                    for a in range(2):
                        for j in (2 * a, 2 * a + 1):
                            dve.wait_ge(*s["bank1_free"].at(i * FG + j + 3))
                            r = relu[:, j % 2, 0:tokens]
                            dve.tensor_tensor(squares[:, j % 2, 0:tokens], r, r, ALU.mult).then_inc(s["squared"].sem, 1)
                            dve.wait_ge(*s["squared"].at(i * FG + j + 1))
                            dve.wait_ge(*s["hid_hi"].at(i * FG + j + 1))
                            dve.tensor_tensor(hid_lo[:, j, 0:tokens], squares[:, j % 2, 0:tokens], hid_hi[:, j, 0:tokens].bitcast(F32),
                                              ALU.subtract).then_inc(s["hid_lo"].sem, 1)
                        split_at(i * FU + (u0 + a + 2), (u0 + a) % 2)

                def added(i, b, t):
                    n = b * T + t
                    dve.wait_ge(*s["product"].at(i * (2 * T) + n + 1))
                    dst = acc[:, t, b * 512:(b + 1) * 512]
                    return dve.tensor_tensor(dst, dst, bank(4 + n % 4), ALU.add).then_inc(s["bank2_free"].sem, 1)

                def second_split(i, b):
                    split_at(i * FU + (u0 + 2 + b + 2), (u0 + b) % 2)

                hidden(0)
                for b in range(2):
                    for t in range(T):
                        n = b * T + t
                        dve.wait_ge(*s["product"].at(n + 1))
                        dve.wait_ge(*n1["res_ready"].at(t + 1))
                        dve.tensor_copy(acc[:, t, b * 512:(b + 1) * 512], bank(4 + n % 4)).then_inc(s["bank2_free"].sem, 1)
                    second_split(0, b)
                with dve.Fori(1, GROUPS - 1) as i:
                    dve.wait_ge(*s["bank2_free"].at(i * (2 * T) + 4))
                    hidden(i)
                    for b in range(2):
                        for t in range(T):
                            added(i, b, t)
                        second_split(i, b)
                i = GROUPS - 1
                dve.wait_ge(*s["bank2_free"].at(i * (2 * T) + 4))
                hidden(i)
                dve.wait_ge(*n1["gate_landed"].at(16 * (2 if T == NT else 1)))

                def out_gain(t):
                    dve.wait_ge(*n1["normed"].at(t + 1))
                    dve.tensor_tensor(acc[:, t, :], acc[:, t, :], gain_row[:, 0, :], ALU.mult).then_inc(n1["out_gained"].sem, 1)

                if l == DEPTH - 1:
                    dve.wait_ge(*n1["gain_landed"].at(64))
                for b in range(2):
                    cols = slice(b * 512, (b + 1) * 512)
                    for t in range(T):
                        added(i, b, t)
                        dve.wait_ge(*s["bank2_free"].at(i * (2 * T) + b * T + t + 5))
                        link(dve.tensor_tensor(acc[:, t, cols], acc[:, t, cols], gate_row[:, 0 if t < LT else 1, cols], ALU.mult))
                        link(dve.scalar_tensor_tensor(out=acc[:, t, cols], in0=x_res[:, t, cols], scalar=ALPHA, in1=acc[:, t, cols], op0=ALU.mult, op1=ALU.add))
                        half_stats(t, b)
                        if b == 1:
                            variance(n1, t)
                            if l == DEPTH - 1:
                                if t >= 1:
                                    out_gain(t - 1)
                                continue
                            if t >= 2:
                                modulated(n1, t - 2, l + 1, 0, h32)
                            if t >= 3:
                                low(n1, t - 3, h32)
                    if l + 1 < DEPTH and b == 0:
                        second_split(i, b)
                if l + 1 < DEPTH:
                    last_tiles(n1, T, l + 1, 0)
                else:
                    out_gain(T - 1)
                end()

        @block.tensor
        def _(pe):
            def end():
                pe.drain().then_inc(pe_phase, 1)

            def products(outs, lhs, rhs, start=True, stop=True):
                ks = lhs[0]
                for i, k in enumerate(ks):
                    l_hi, l_lo = lhs[1](k)
                    for n, (a, half) in enumerate(((l_hi, 0), (l_hi, 1), (l_lo, 0))):
                        for c, o in enumerate(outs):
                            ins = pe.matmul(o, a, rhs(k, c)[half], start=start and i == 0 and n == 0,
                                            stop=stop and i == len(ks) - 1 and n == 2)
                return ins

            def turn(s, t, rows):
                if t >= 2:
                    pe.wait_ge(*s["h_act"].at(t - 1))
                    pe.wait_ge(*s["h_dve"].at(t - 1))
                for k in range(KT):
                    ins = pe.transpose(bank(2 * (t % 2), P, at=k * P), rows[:, k * P:(k + 1) * P], ident[:, :])
                ins.then_inc(s["turned"].sem, 1)

            def wmod_unit(n):
                l, k = n // WMOD_UNITS, n % MR
                pe.wait_ge(wm_landed[k], 16 * (n // MR + 1))
                if n >= 2:
                    pe.wait_ge(row_added, n if n >= WMOD_UNITS else n - 1)
                b = wmod_bank(n) * 512
                for kt in range(KT):
                    j = 32 * (kt % 4)
                    ins = pe.matmul(psum[j:j + 32, b:b + UW], silu[:, kt, :], wm_rings[l][:, k, kt, :], start=kt < 4, stop=kt >= 4)
                ins.then_inc(wm_used, 1)

            def sum_parts(n):
                buffers = wm_parts[n // WMOD_UNITS]
                pe.wait_ge(parts_copied, n + 1)
                r, b = 32 * (n // VU % 2), wmod_bank(n) * 512 + UW
                pe.matmul(psum[r:r + 2, b:b + UW], comb[:, :], buffers[n % len(buffers)], start=True, stop=True).then_inc(wm_summed, 1)

            def turn_mod_rows(i, b):
                n = 2 * (MOD_COLUMNS[i][2] - MOD_COLUMNS[i][1])
                pe.wait_ge(mod_rows_landed, 32 * (i + 1))
                pe.transpose(bank(b, n), mod_rows[0:n, :], ident[0:n, 0:n]).then_inc(mod_turned, 1)

            pe.wait_ge(ident_landed, 32)
            pe.wait_ge(vrow_landed[0], 16 * 9)
            pe.transpose(bank(4, V_ROWS), vrow[0:V_ROWS, 0, :], ident[0:V_ROWS, 0:V_ROWS]).then_inc(vec_turned, 1)
            pe.wait_ge(silu_ready, 1)
            for n in range(WM_FIRST):
                wmod_unit(n)
                if n:
                    sum_parts(n - 1)
            sum_parts(WM_FIRST - 1)
            pe.wait_ge(x_first_landed, 16 * NT)
            for t in range(2):
                turn(X0, t, x_first[:, t, :])
            for v in range(2):
                pe.wait_ge(row_added, VU * (v + 1))
                for k in range(KT):
                    ins = pe.transpose(bank(4 + v, 2, at=2 * k), mod_row[0][v][:, k * P:(k + 1) * P], ident[32 * v:32 * v + 2, 32 * v:32 * v + 2])
                ins.then_inc(first_turned, 1)
            for t in range(2, NT):
                turn(X0, t, x_first[:, t, :])
            pe.wait_ge(vrow_landed[1], 16 * 9)
            pe.transpose(bank(7, V_ROWS), vrow[0:V_ROWS, 1, :], ident[0:V_ROWS, 0:V_ROWS]).then_inc(vec_turned, 1)
            pe.wait_ge(const_landed, 16 * 3)
            end()

            def xt(k, c0, n):
                return xt_hi[:, k, c0:c0 + n], xt_lo[:, k, c0:c0 + n]

            def weights_ready(u):
                pe.wait_ge(w_lo_ready, u + 1)

            def feature_tile(slot, col, l, all_tokens, banks):
                wh, wl = w_view(w_hi, slot), w_view(w_lo, slot)
                ch = chunks(l, all_tokens)
                return products([bank(banks + c, n) for c, (_, n) in enumerate(ch)],
                                (range(KT), lambda k: (wh[:, k, col:col + P], wl[:, k, col:col + P])),
                                lambda k, c: xt(k, *ch[c]))

            def row_tile(slot, t, width, o, left=xt):
                wh, wl = w_view(w_hi, slot, width), w_view(w_lo, slot, width)
                return products([o], (range(KT), lambda k: left(k, t * P, P)), lambda k, c: (wh[:, k, :], wl[:, k, :]))

            def mixed_heads(k, c0, n):
                return (hid_hi[:, k - 4, c0:c0 + n], hid_lo[:, k - 4, c0:c0 + n]) if k in (4, 5) else xt(k, c0, n)

            def beside(l, g, parts, n):
                s = IN[l][g] if parts else None
                for h in halves_beside(parts, len(ITEMS[l]), n):
                    kind, u, i = parts[h // 2][:3]
                    first = h % 2 == 0
                    if first:
                        weights_ready(in_unit(l, u))
                        if h >= 2:
                            pe.wait_ge(*s["part_copied"].at(h // 2))
                    ks = range(0, KT // 2) if first else range(KT // 2, KT)
                    width = IN_UNITS[u][1]
                    wh, wl = w_view(w_hi, in_unit(l, u), width), w_view(w_lo, in_unit(l, u), width)
                    if kind == "features":
                        c, w = parts[h // 2][3:]
                        ins = products([bank(7, w)], (ks, lambda k: (wh[:, k, i * P:(i + 1) * P], wl[:, k, i * P:(i + 1) * P])),
                                       lambda k, _: xt(k, c, w), start=first, stop=not first)
                    else:
                        ins = products([bank(7, width)], (ks, lambda k: xt(k, i * P, P)), lambda k, _: (wh[:, k, :], wl[:, k, :]),
                                       start=first, stop=not first)
                    if not first:
                        ins.then_inc(s["part"].sem, 1)

            def attention(l, g, nmaps, q, k, v, p, pt, parts, diag=None):
                s = AT[l][g]
                items = ITEMS[l]

                def keys(qt):
                    return (0, TOK) if qt < LT else (SEQ, CTX)

                def scores(n):
                    qt, h = items[n]
                    k0, nk = keys(qt)
                    if nmaps == 2:
                        if n >= 1:
                            pe.wait_ge(*s["probs"].at(2 * n))
                        for c in range(0, nk, 512):
                            w = min(512, nk - c)
                            for m in range(2):
                                ins = pe.matmul(bank(2 * m, w, at=c), q(h, m)[:, qt * P:(qt + 1) * P], k(h, m)[:, k0 + c:k0 + c + w], start=True, stop=True)
                                if c + w == nk:
                                    ins.then_inc(s["scores"].sem, 1)
                        return
                    b = 2 * (n % 2)
                    if n >= 2:
                        pe.wait_ge(*s["probs"].at(n - 1))
                    for c in range(0, nk, 512):
                        w = min(512, nk - c)
                        ins = pe.matmul(bank(b, w, at=c), q(h, 0)[:, qt * P:(qt + 1) * P], k(h, 0)[:, k0 + c:k0 + c + w], start=True, stop=True)
                    ins.then_inc(s["scores"].sem, 1)

                def turn_probs(n):
                    _, nk = keys(items[n][0])
                    pe.wait_ge(*s["mixed" if nmaps == 2 else "scaled"].at(n + 1))
                    if n >= 1:
                        pe.wait_ge(*s["turned_copied"].at(n))
                    for c in range(nk // P):
                        part = p[:, n % 2, 0, c * P:(c + 1) * P]
                        if nmaps == 2:
                            ins = pe.transpose(bank(4, P, at=c * P), part, ident[:, :])
                        else:
                            ins = pe.matmul(bank(4, P, at=c * P), part, diag[:, n % 2, :], start=True, stop=True)
                    ins.then_inc(s["turned"].sem, 1)

                def values(n):
                    qt, h = items[n]
                    k0, nk = keys(qt)
                    pe.wait_ge(*s["turned_copied"].at(n + 1))
                    if nmaps == 2:
                        if n >= 1:
                            pe.wait_ge(*s["mean_square"].at(n))
                        for c in range(nk // P):
                            ins = pe.matmul(bank(6, DA_V), pt[n % 2][:, c * P:(c + 1) * P], v[:, k0 // P + c, h * DA_V:(h + 1) * DA_V],
                                            start=c == 0, stop=c == nk // P - 1)
                    else:
                        if n >= 2:
                            pe.wait_ge(*s["y"].at(n // 2))
                        for c in range(nk // P):
                            for e in (n - 1, n):
                                r, hh = e % 2 * HD, items[e][1]
                                ins = pe.matmul(psum[r:r + HD, 6 * 512:6 * 512 + P], v[:, k0 // P + c, hh * HD:(hh + 1) * HD],
                                                pt[e % 3][:, c * P:(c + 1) * P], start=c == 0, stop=c == nk // P - 1)
                    ins.then_inc(s["mixed_values"].sem, 1)

                scores(0)
                if nmaps == 1:
                    scores(1)
                    turn_probs(0)
                    scores(2)
                for n in range(len(items)):
                    if g == 2 and l == 0 and n:
                        sum_parts(WMOD_UNITS + n - 1)
                    if g == 2 and n % HEADS == 1:
                        t = n // HEADS
                        pe.wait_ge(*YT[l]["loaded"].at(16 * (t + 1)))
                        if l == 0:
                            pe.wait_ge(row_added, WMOD_UNITS + n)
                        elif t:
                            pe.wait_ge(*YT[l]["lo"].at(t))
                        for c in range(4):
                            ins = pe.transpose(bank(7, P, at=c * P), y_in[:, c * P:(c + 1) * P], ident[:, :])
                        ins.then_inc(YT[l]["turned"].sem, 1)
                    if nmaps == 2:
                        if n + 1 < len(items):
                            scores(n + 1)
                        turn_probs(n)
                    else:
                        if n + 1 < len(items):
                            turn_probs(n + 1)
                        if n + 3 < len(items):
                            scores(n + 3)
                    beside(l, g + 1, parts, n)
                    if g == 2 and l == 0:
                        if n % HEADS == 1:
                            pe.wait_ge(*YT[l]["lo"].at(n // HEADS + 1))
                        wmod_unit(WMOD_UNITS + n)
                    if nmaps == 1:
                        if n % 2:
                            values(n)
                    elif n >= 1:
                        values(n - 1)
                if nmaps == 2:
                    values(len(items) - 1)
                if g == 2 and l == 0:
                    sum_parts(2 * WMOD_UNITS - 1)

            for l in range(DEPTH):
                T = T_Q[l]
                fence(pe, l, "inA")
                s = IN[l][0]

                def rotation(i):
                    pe.wait_ge(*s["raw"].at(i + 1))
                    if i >= 2:
                        pe.wait_ge(*s["done"].at(i - 1))
                    pe.matmul(bank(4 + i % 2), rot64[:, :], da_raw[:, i % 2, :], start=True, stop=True).then_inc(s["rot"].sem, 1)

                for i in range(8):
                    u = in_unit(l, i // 2)
                    if i % 2 == 0:
                        weights_ready(u)
                    if i >= 2:
                        pe.wait_ge(*s["raw"].at(i - 1))
                    feature_tile(u, (i % 2) * P, l, i >= HEADS, 2 * (i % 2)).then_inc(s["tile"].sem, 1)
                    if i >= 1:
                        rotation(i - 1)
                    if l == 0:
                        wmod_unit(WM_FIRST + i)
                        if i:
                            sum_parts(WM_FIRST + i - 1)
                rotation(7)
                for n in range(2 * NT):
                    u, t = n // NT, n % NT
                    if t == 0:
                        weights_ready(in_unit(l, 4 + u))
                    if n < 2:
                        pe.wait_ge(*s["done"].at(7 + n))
                    if n >= 2:
                        pe.wait_ge(*s["v_copied"].at(n - 1))
                    row_tile(in_unit(l, 4 + u), t, UW, bank(4 + t % 2, UW)).then_inc(s["v"].sem, 1)
                    if l == 0 and WM_FIRST + 8 + n < WMOD_UNITS:
                        wmod_unit(WM_FIRST + 8 + n)
                    if l == 0 and WM_FIRST + 8 + n <= WMOD_UNITS:
                        sum_parts(WM_FIRST + 7 + n)
                end()
                fence(pe, l, "atA")
                attention(l, 0, 2, lambda h, m: da_q[m * HD:(m + 1) * HD, h, :], lambda h, m: da_k[m * HD:(m + 1) * HD, h, :],
                          da_v, da_p, da_pt, ML_PARTS[T])
                end()

                fence(pe, l, "inB")
                s, m = IN[l][1], ML[l]
                if l == 0:
                    turn_mod_rows(0, 7)
                for t in range(NT):
                    pe.wait_ge(*m["normed"].at(t + 1))
                    if t >= 2:
                        pe.wait_ge(*m["evacuated"].at(t - 1))
                    b = 4 + t % 2
                    if t < T:
                        for k in range(2):
                            pe.transpose(bank(b, P, at=k * P), ml_rows[:, t, k * P:(k + 1) * P], ident[:, :])
                    pe.transpose(bank(b, P, at=2 * P), ml_rows[:, t, Q_RANK:Q_RANK + KV_RANK], ident[:, :])
                    pe.transpose(bank(b, P, MQ, at=3 * P), ml_rows[:, t, Q_RANK + KV_RANK - HD:Q_RANK + KV_RANK + ROPE], ident[:, :]).then_inc(m["turned"].sem, 1)
                pe.wait_ge(*m["weights"].at(32))
                pe.wait_ge(*m["evacuated"].at(NT))

                def rotation_q(h):
                    pe.wait_ge(*s["raw"].at(h + 1))
                    if h >= 2:
                        pe.wait_ge(*s["done"].at(h - 1))
                    pe.matmul(bank(4 + h % 2, parts=MQ), rot32[:, :], ml_raw[0:MQ, h % 2, :], start=True, stop=True).then_inc(s["rot"].sem, 1)

                for h in range(HEADS):
                    if h >= 2:
                        pe.wait_ge(*s["raw"].at(h - 1))
                    for k in range(2):
                        for c, (c0, w) in enumerate(chunks(l)):
                            ins = pe.matmul(bank(2 * (h % 2) + c, w, MQ), ml_wq[:, k, h * MQ:(h + 1) * MQ], ml_cq[:, k, c0:c0 + w], start=k == 0, stop=k == 1)
                    ins.then_inc(s["tile"].sem, 1)
                    if h >= 1:
                        rotation_q(h - 1)
                rotation_q(HEADS - 1)
                for h in range(HEADS):
                    if h < 2:
                        pe.wait_ge(*s["raw"].at(HEADS - 1 + h))
                    else:
                        pe.wait_ge(*m["up"].at(h - 1))
                    for c, (c0, w) in enumerate(chunks(l, True)):
                        ins = pe.matmul(bank(2 * (h % 2) + c, w, HD), ml_wkv[:, h * P:h * P + HD], ml_ckv[:, c0:c0 + w], start=True, stop=True)
                    ins.then_inc(s["tile"].sem, 1)
                pe.wait_ge(*s["done"].at(HEADS))
                pe.matmul(psum[HD:MQ, 4 * 512:5 * 512], rot32[HD:MQ, HD:MQ], ml_kr[HD:MQ, 0:SEQ], start=True, stop=True).then_inc(s["rot"].sem, 1)
                wv = ml_wkv[:, :].rearrange("p (h n) -> p h n", n=P)[:, :, HD:P]
                for t in range(NT):
                    if t >= 2:
                        pe.wait_ge(*m["v_copied"].at(t - 1))
                    pe.matmul(bank(6 + t % 2, 256), ml_ckv[:, t * P:(t + 1) * P], wv, start=True, stop=True).then_inc(m["v_ready"].sem, 1)
                end()
                fence(pe, l, "atB")
                attention(l, 1, 1, lambda h, m: ml_q[:, h, :], lambda h, m: ml_k[:, h, :], ml_v, ml_p, ml_pt, NA_PARTS[T], ml_diag)
                end()

                fence(pe, l, "atC")
                attention(l, 2, 1, lambda h, m: na_q[(h % 2) * HD:(h % 2 + 1) * HD, h // 2, :],
                          lambda h, m: na_k[(h % 2) * HD:(h % 2 + 1) * HD, h // 2, :], na_v, na_p, na_pt, [], na_diag)
                end()

                fence(pe, l, "out")
                s = LN[l][0]
                for u in range(N_OUT):
                    g = in_unit(l, N_IN + u)
                    weights_ready(g)
                    for t in range(T):
                        n = u * T + t
                        if n >= 4:
                            pe.wait_ge(*OP[l]["gated"].at(n - 3))
                        row_tile(g, t, UW, bank(4 + n % 4, UW), mixed_heads).then_inc(OP[l]["product"].sem, 1)
                        if u == N_OUT - 1 and t >= 2:
                            pe.wait_ge(*s["normed"].at(t - 1))
                            turn(s, t - 2, acc[:, t - 2, :])
                for t in range(T - 2, T):
                    pe.wait_ge(*s["normed"].at(t + 1))
                    turn(s, t, acc[:, t, :])
                if l == 0:
                    pe.wait_ge(*OP[l]["gated"].at(N_OUT * T))
                    turn_mod_rows(1, 7)
                end()

                fence(pe, l, "ffn")
                s, n1 = FF[l], LN[l][1]
                u0 = in_unit(l, N_IN + N_OUT)

                def group(i, turned):
                    for a in range(2):
                        pe.wait_ge(w_lo_ready, i * FU + (u0 + a + 1))
                        for j in (2 * a, 2 * a + 1):
                            pe.wait_ge(*s["bank1_free"].at(i * FG + j + 1))
                            feature_tile(u0 + a, (j % 2) * P, l, False, 2 * (j % 2)).then_inc(s["hidden"].sem, 1)
                    for b in range(2):
                        pe.wait_ge(w_lo_ready, i * FU + (u0 + 2 + b + 1))
                        wh, wl = w_view_ff2(w_hi, u0 + b), w_view_ff2(w_lo, u0 + b)

                        def part(t, js):
                            n = b * T + t
                            if js[0] == 0:
                                pe.wait_ge(*s["bank2_free"].at(i * (2 * T) + n + 1))
                            for j in js:
                                if n == 0:
                                    pe.wait_ge(*s["hid_lo"].at(i * FG + j + 3))
                                tk = slice(t * P, (t + 1) * P)
                                ins = products([bank(4 + n % 4)], ([j], lambda k: (hid_hi[:, k, tk], hid_lo[:, k, tk])),
                                               lambda k, c: (wh[:, k, :], wl[:, k, :]), start=j == 0, stop=j == FG - 1)
                            if js[-1] == FG - 1:
                                ins.then_inc(s["product"].sem, 1)

                        first = 0
                        if b == 0:
                            first = 2
                            for t in range(2):
                                part(t, range(FG - 1))
                            for t in range(2):
                                part(t, range(FG - 1, FG))
                        for t in range(first, T):
                            part(t, range(FG))
                            if turned and b == 1 and t >= 2:
                                pe.wait_ge(*n1["normed"].at(t - 1))
                                turn(n1, t - 2, acc[:, t - 2, :])

                with pe.Fori(0, GROUPS - 1) as i:
                    group(i, False)
                group(GROUPS - 1, l + 1 < DEPTH)
                if l + 1 < DEPTH:
                    for t in range(T - 2, T):
                        pe.wait_ge(*n1["normed"].at(t + 1))
                        turn(n1, t, acc[:, t, :])
                end()


_NAMES = ["x", "c", "ctx", "c_ctx", "w_mod", "b_mod", "w_in", "da_lam_q1", "da_lam_k1", "da_lam_q2", "da_lam_k2",
          "da_subln_g", "mla_q_norm_g", "mla_w_uq", "mla_kv_norm_g", "mla_w_ukv", "na_rpb", "w_out",
          "ln1_g", "ln1_b", "w_ff1", "w_ff2", "ln2_g", "ln2_b"]


def kernel(**inputs):
    import concourse.bacc as _bacc
    from concourse.bass_utils import run_bass_kernel_spmd as _run

    nc = _bacc.Bacc("TRN2", target_bir_lowering=False, num_devices=1)
    arrays, aps = {}, {}
    given = {n: np.ascontiguousarray(inputs[n]) for n in _NAMES}
    given.update(shape_constants())
    for name, a in given.items():
        arrays[f"in_{name}"] = a
        aps[name] = nc.dram_tensor(f"in_{name}", a.shape, mybir.dt.from_np(a.dtype), kind="ExternalInput").ap()
    out = nc.dram_tensor("out_x", (1, SEQ, D), F32, kind="ExternalOutput").ap()
    build(nc, aps, out)
    r = _run(nc, [arrays], core_ids=[0])
    return r.results[0]["out_x"]
```
